# Optimizing a Trainium2 kernel written in Bass

```python
import math
import jax, jax.numpy as jnp
from jax import lax
import numpy as np

D_MODEL = 1024
BATCH = 1
SEQ = 256
DEPTH = 2

N_A_LAYERS = DEPTH // 2
N_B_LAYERS = DEPTH - N_A_LAYERS
D_FF = 2816
A_HEADS = 8
A_KEY_DIM = 128
A_VAL_DIM = D_MODEL // A_HEADS
A_FORGET_DIM = A_HEADS * A_KEY_DIM
A_VAL_WIDTH = A_HEADS * A_VAL_DIM
A_IN_WIDTH = 2 * A_FORGET_DIM + 2 * A_VAL_WIDTH
A_CHUNK = 64
B_WINDOWS = (128, 512, 2048)
B_DILATIONS = (1, 4, 16)
B_GROUPS = 3
B_HEADS = 16
B_HEAD_DIM = D_MODEL // B_HEADS
B_QKV_WIDTH = B_GROUPS * B_HEADS * B_HEAD_DIM
B_BLOCK = 128
NUM_BUCKETS = 32
MAX_DISTANCE = 2048
EPS = 1e-6


def _rms(x, gain):
    xf = x.astype(jnp.float32)
    y = xf * lax.rsqrt(jnp.mean(xf * xf, axis=-1, keepdims=True) + EPS)
    return (y * gain.astype(jnp.float32)).astype(x.dtype)

def _swiglu(h, w_in, w_out):
    gate, up = jnp.split(h @ w_in, 2, axis=-1)
    return (jax.nn.silu(gate) * up) @ w_out

def _lower_bounds(lb_logits):
    p = jax.nn.softmax(lb_logits.astype(jnp.float32), axis=0)
    return jnp.cumsum(p, axis=0)[:-1]

def _hgrn2(h, w_in, lb, out_gain, w_out):
    bsz, seq, _ = h.shape
    n_chunks = seq // A_CHUNK
    f32 = jnp.float32
    q, f, i, g = jnp.split(h @ w_in, [A_FORGET_DIM, 2 * A_FORGET_DIM, 2 * A_FORGET_DIM + A_VAL_WIDTH], axis=-1)
    log_f = jnp.logaddexp(jnp.log(lb), jnp.log1p(-lb) + jax.nn.log_sigmoid(f.astype(f32)))
    k = -jnp.expm1(log_f)
    q = jax.nn.silu(q.astype(f32))
    v = i.astype(f32)

    def to_chunks(t, dh):
        return t.reshape(bsz, n_chunks, A_CHUNK, A_HEADS, dh).transpose(1, 0, 3, 2, 4)

    qc, kc, gc = (to_chunks(t, A_KEY_DIM) for t in (q, k, log_f))
    vc = to_chunks(v, A_VAL_DIM)
    causal = jnp.tril(jnp.ones((A_CHUNK, A_CHUNK), dtype=bool))

    def step(state, inp):
        qb, kb, vb, gb = inp
        cum = jnp.cumsum(gb, axis=2)
        rel = cum[:, :, :, None, :] - cum[:, :, None, :, :]
        decay = jnp.exp(jnp.where(causal[:, :, None], rel, -jnp.inf))
        scores = jnp.einsum('bhtd,bhtsd,bhsd->bhts', qb, decay, kb)
        out = (jnp.einsum('bhts,bhse->bhte', scores, vb)
               + jnp.einsum('bhtd,bhde->bhte', qb * jnp.exp(cum), state))
        last = cum[:, :, -1, :]
        state = (jnp.exp(last)[..., None] * state
                 + jnp.einsum('bhsd,bhse->bhde', kb * jnp.exp(last[:, :, None, :] - cum), vb))
        return state, out

    state0 = jnp.zeros((bsz, A_HEADS, A_KEY_DIM, A_VAL_DIM), f32)
    _, o = lax.scan(step, state0, (qc, kc, vc, gc))
    o = o.transpose(1, 0, 3, 2, 4).reshape(bsz, seq, A_HEADS, A_VAL_DIM)
    o = _rms(o, out_gain) * jax.nn.silu(g.astype(f32)).reshape(bsz, seq, A_HEADS, A_VAL_DIM)
    return o.reshape(bsz, seq, A_VAL_WIDTH).astype(h.dtype) @ w_out

def _t5_bucket(dist):
    dist = np.asarray(dist, np.int32)
    max_exact = NUM_BUCKETS // 2
    large = max_exact + (np.log(np.maximum(dist, 1) / max_exact)
                         / math.log(MAX_DISTANCE / max_exact) * (NUM_BUCKETS - max_exact)).astype(np.int32)
    large = np.minimum(large, NUM_BUCKETS - 1)
    return np.where(dist < max_exact, dist, large).astype(np.int32)

def _band_static(window, dilation):
    nq = B_BLOCK // dilation
    wd = window // dilation
    nj = wd + nq
    m = np.arange(nj)[None, :] - np.arange(nq)[:, None]
    band = (m >= 0) & (m <= wd)
    bucket = _t5_bucket((wd - np.clip(m, 0, wd)) * dilation)
    return band, bucket

def _shared_kv(x, kv_norm, w_kv, k_gain):
    bsz, seq, _ = x.shape
    kv = (_rms(x, kv_norm) @ w_kv).reshape(bsz, seq, 2, B_GROUPS, B_HEADS, B_HEAD_DIM)
    k = _rms(kv[:, :, 0], k_gain[:, None, :])
    v = kv[:, :, 1]
    k_pads = [jnp.pad(k[:, :, g], ((0, 0), (w, 0), (0, 0), (0, 0))) for g, w in enumerate(B_WINDOWS)]
    v_pads = [jnp.pad(v[:, :, g], ((0, 0), (w, 0), (0, 0), (0, 0))) for g, w in enumerate(B_WINDOWS)]
    return k_pads, v_pads

def _dilated_attention(h, w_q, q_gain, w_o, k_pads, v_pads, rel_bias):
    bsz, seq, _ = h.shape
    n_blocks = seq // B_BLOCK
    f32 = jnp.float32
    q = (h @ w_q).reshape(bsz, seq, B_GROUPS, B_HEADS, B_HEAD_DIM)
    q = _rms(q, q_gain[:, None, :]) * (B_HEAD_DIM ** -0.5)
    q_groups = [q[:, :, g] for g in range(B_GROUPS)]
    statics = [_band_static(w, d) for w, d in zip(B_WINDOWS, B_DILATIONS)]
    biases = [rel_bias[bucket][..., g * B_HEADS:(g + 1) * B_HEADS].transpose(2, 0, 1).astype(f32)
              for g, (_, bucket) in enumerate(statics)]

    def block(b):
        start = b * B_BLOCK
        outs, lses = [], []
        for g, (window, dil) in enumerate(zip(B_WINDOWS, B_DILATIONS)):
            band = statics[g][0]
            nq = B_BLOCK // dil
            nj = window // dil + nq
            qb = lax.dynamic_slice_in_dim(q_groups[g], start, B_BLOCK, axis=1).reshape(bsz, nq, dil, B_HEADS, B_HEAD_DIM)
            kb = lax.dynamic_slice_in_dim(k_pads[g], start, window + B_BLOCK, axis=1).reshape(bsz, nj, dil, B_HEADS, B_HEAD_DIM)
            vb = lax.dynamic_slice_in_dim(v_pads[g], start, window + B_BLOCK, axis=1).reshape(bsz, nj, dil, B_HEADS, B_HEAD_DIM)
            s = jnp.einsum('birhd,bjrhd->bhrij', qb, kb).astype(f32) + biases[g][None, :, None]
            pos = start - window + jnp.arange(nj)[:, None] * dil + jnp.arange(dil)[None, :]
            valid = band[None, :, :] & (pos.T >= 0)[:, None, :]
            s = jnp.where(valid[None, None], s, -jnp.inf)
            lse = jax.nn.logsumexp(s, axis=-1)
            p = jnp.exp(s - lse[..., None]).astype(vb.dtype)
            o = jnp.einsum('bhrij,bjrhd->birhd', p, vb).reshape(bsz, B_BLOCK, B_HEADS, B_HEAD_DIM)
            outs.append(o.astype(f32))
            lses.append(lse.transpose(0, 3, 2, 1).reshape(bsz, B_BLOCK, B_HEADS))
        wts = jax.nn.softmax(jnp.stack(lses), axis=0)
        o = jnp.einsum('gbqh,gbqhd->bqhd', wts, jnp.stack(outs))
        return o.reshape(bsz, B_BLOCK, B_HEADS * B_HEAD_DIM).astype(h.dtype)

    o = lax.map(block, jnp.arange(n_blocks))
    o = o.transpose(1, 0, 2, 3).reshape(bsz, seq, B_HEADS * B_HEAD_DIM)
    return o @ w_o

def first_inputs(seed: int = 0) -> dict:
    key = jax.random.key(seed)
    ks = jax.random.split(key, 16)

    def dense(k, shape, fan_in):
        return jax.random.normal(k, shape, jnp.float32) * fan_in ** -0.5

    def gain(k, shape):
        return 1.0 + 0.1 * jax.random.normal(k, shape, jnp.float32)

    return {
        'x': jax.random.normal(ks[0], (BATCH, SEQ, D_MODEL), jnp.float32),
        'norm_gain': gain(ks[1], (DEPTH, 3, D_MODEL)),
        'ffn_w_in': dense(ks[2], (DEPTH, 2, D_MODEL, 2 * D_FF), D_MODEL),
        'ffn_w_out': dense(ks[3], (DEPTH, 2, D_FF, D_MODEL), D_FF),
        'a_w_in': dense(ks[4], (N_A_LAYERS, D_MODEL, A_IN_WIDTH), D_MODEL),
        'a_lb_logits': 0.5 * jax.random.normal(ks[5], (N_A_LAYERS + 1, A_FORGET_DIM), jnp.float32),
        'a_out_gain': gain(ks[6], (N_A_LAYERS, A_VAL_DIM)),
        'a_w_out': dense(ks[7], (N_A_LAYERS, A_VAL_WIDTH, D_MODEL), A_VAL_WIDTH),
        'kv_norm': gain(ks[8], (D_MODEL,)),
        'w_kv': dense(ks[9], (D_MODEL, 2 * B_QKV_WIDTH), D_MODEL),
        'k_gain': gain(ks[10], (B_GROUPS, B_HEAD_DIM)),
        'b_w_q': dense(ks[11], (N_B_LAYERS, D_MODEL, B_QKV_WIDTH), D_MODEL),
        'b_q_gain': gain(ks[12], (N_B_LAYERS, B_GROUPS, B_HEAD_DIM)),
        'b_w_o': dense(ks[13], (N_B_LAYERS, B_HEADS * B_HEAD_DIM, D_MODEL), B_HEADS * B_HEAD_DIM),
        'rel_bias': 0.5 * jax.random.normal(ks[14], (NUM_BUCKETS, B_GROUPS * B_HEADS), jnp.float32),
    }

def first_block(x, norm_gain, ffn_w_in, ffn_w_out, a_w_in, a_lb_logits, a_out_gain, a_w_out,
              kv_norm, w_kv, k_gain, b_w_q, b_q_gain, b_w_o, rel_bias):
    lower_bounds = _lower_bounds(a_lb_logits)
    k_pads, v_pads = None, None
    for layer in range(DEPTH):
        if layer == N_A_LAYERS:
            k_pads, v_pads = _shared_kv(x, kv_norm, w_kv, k_gain)
        x = x + 0.5 * _swiglu(_rms(x, norm_gain[layer, 0]), ffn_w_in[layer, 0], ffn_w_out[layer, 0])
        h = _rms(x, norm_gain[layer, 1])
        if layer < N_A_LAYERS:
            x = x + _hgrn2(h, a_w_in[layer], lower_bounds[layer], a_out_gain[layer], a_w_out[layer])
        else:
            j = layer - N_A_LAYERS
            x = x + _dilated_attention(h, b_w_q[j], b_q_gain[j], b_w_o[j], k_pads, v_pads, rel_bias)
        x = x + 0.5 * _swiglu(_rms(x, norm_gain[layer, 2]), ffn_w_in[layer, 1], ffn_w_out[layer, 1])
    return x


N_A_LAYERS_2 = DEPTH // 2
N_B_LAYERS_2 = DEPTH - N_A_LAYERS_2
HEAD_DIM = 64
SB_HEADS = D_MODEL // HEAD_DIM
SWA_Q_HEADS = D_MODEL // HEAD_DIM
SWA_KV_HEADS = 4
SWA_GROUP = SWA_Q_HEADS // SWA_KV_HEADS
WINDOW = 128
Q_BLOCK = 128
ROPE_THETA = 10000.0
RMS_EPS = 1e-6
FFN_RES_SCALE = 0.5


def rms_norm(x, g):
    xf = x.astype(jnp.float32)
    y = xf * lax.rsqrt(jnp.mean(xf * xf, axis=-1, keepdims=True) + RMS_EPS)
    return (y * g.astype(jnp.float32)).astype(x.dtype)

def swiglu(x, w_in, w_out):
    gate, up = jnp.split(x @ w_in, 2, axis=-1)
    return (jax.nn.silu(gate) * up) @ w_out

def rotary(x, pos):
    half = HEAD_DIM // 2
    inv_freq = ROPE_THETA ** (-jnp.arange(half, dtype=jnp.float32) / half)
    ang = pos.astype(jnp.float32)[:, None] * inv_freq[None, :]
    cos = jnp.cos(ang)[None, :, None, :]
    sin = jnp.sin(ang)[None, :, None, :]
    xf = x.astype(jnp.float32)
    x1, x2 = xf[..., :half], xf[..., half:]
    return jnp.concatenate([x1 * cos - x2 * sin, x2 * cos + x1 * sin], axis=-1).astype(x.dtype)

def stick_breaking_attention(q, k, v):
    B, S, H, Dh = q.shape
    nb = S // Q_BLOCK
    scale = Dh ** -0.5
    key_pos = jnp.arange(S)
    qb = q.reshape(B, nb, Q_BLOCK, H, Dh).transpose(1, 0, 2, 3, 4)

    def block(args):
        qi, i = args
        z = jnp.einsum('bqhd,bshd->bhqs', qi, k).astype(jnp.float32) * scale
        q_pos = i * Q_BLOCK + jnp.arange(Q_BLOCK)
        strict = key_pos[None, :] < q_pos[:, None]
        log_beta = jax.nn.log_sigmoid(z)
        log_1m_beta = jnp.where(strict, log_beta - z, 0.0)
        suffix = lax.cumsum(log_1m_beta, axis=3, reverse=True) - log_1m_beta
        w = jnp.where(strict, jnp.exp(log_beta + suffix), 0.0)
        return jnp.einsum('bhqs,bshd->bqhd', w.astype(v.dtype), v)

    out = lax.map(block, (qb, jnp.arange(nb)))
    return out.transpose(1, 0, 2, 3, 4).reshape(B, S, H, Dh)

def sliding_window_sink_attention(q, k, v, sinks):
    B, S, Hq, Dh = q.shape
    nb = S // WINDOW
    qb = q.reshape(B, nb, WINDOW, SWA_KV_HEADS, SWA_GROUP, Dh)

    def band(t):
        tb = t.reshape(B, nb, WINDOW, SWA_KV_HEADS, Dh)
        prev = jnp.pad(tb[:, :-1], ((0, 0), (1, 0), (0, 0), (0, 0), (0, 0)))
        return jnp.concatenate([prev, tb], axis=2)

    kb, vb = band(k), band(v)
    s = jnp.einsum('bnqhgd,bnkhd->bnhgqk', qb, kb).astype(jnp.float32) * (Dh ** -0.5)
    qi = jnp.arange(WINDOW)[:, None]
    ki = jnp.arange(2 * WINDOW)[None, :]
    diff = qi + WINDOW - ki
    in_window = (diff >= 0) & (diff < WINDOW)
    blk = jnp.arange(nb)[:, None, None]
    valid = in_window[None] & ((blk > 0) | (ki[None] >= WINDOW))
    s = jnp.where(valid[None, :, None, None], s, -jnp.inf)
    sink = jnp.broadcast_to(
        sinks.astype(jnp.float32).reshape(SWA_KV_HEADS, SWA_GROUP)[None, None, :, :, None, None],
        s.shape[:-1] + (1,))
    p = jax.nn.softmax(jnp.concatenate([s, sink], axis=-1), axis=-1)[..., :-1]
    out = jnp.einsum('bnhgqk,bnkhd->bnqhgd', p.astype(v.dtype), vb)
    return out.reshape(B, S, Hq, Dh)

def second_inputs(seed: int = 0) -> dict:
    key = jax.random.key(seed)
    ks = jax.random.split(key, 20)
    f32 = jnp.float32

    def w(k, shape, fan_in):
        return jax.random.normal(k, shape, f32) * (fan_in ** -0.5)

    def gain(k, shape):
        return 1.0 + 0.02 * jax.random.normal(k, shape, f32)

    return {
        "x": jax.random.normal(ks[0], (BATCH, SEQ, D_MODEL), f32),
        "ffn1_norm": gain(ks[1], (DEPTH, D_MODEL)),
        "ffn1_w_in": w(ks[2], (DEPTH, D_MODEL, 2 * D_FF), D_MODEL),
        "ffn1_w_out": w(ks[3], (DEPTH, D_FF, D_MODEL), D_FF),
        "mix_norm": gain(ks[4], (DEPTH, D_MODEL)),
        "ffn2_norm": gain(ks[5], (DEPTH, D_MODEL)),
        "ffn2_w_in": w(ks[6], (DEPTH, D_MODEL, 2 * D_FF), D_MODEL),
        "ffn2_w_out": w(ks[7], (DEPTH, D_FF, D_MODEL), D_FF),
        "sb_w_qkv": w(ks[8], (N_A_LAYERS_2, D_MODEL, 3 * SB_HEADS * HEAD_DIM), D_MODEL),
        "sb_w_o": w(ks[9], (N_A_LAYERS_2, SB_HEADS * HEAD_DIM, D_MODEL), SB_HEADS * HEAD_DIM),
        "kv_norm": gain(ks[10], (D_MODEL,)),
        "kv_w": w(ks[11], (D_MODEL, 2 * SWA_KV_HEADS * HEAD_DIM), D_MODEL),
        "swa_w_q": w(ks[12], (N_B_LAYERS_2, D_MODEL, SWA_Q_HEADS * HEAD_DIM), D_MODEL),
        "swa_sinks": 0.5 * jax.random.normal(ks[13], (N_B_LAYERS_2, SWA_Q_HEADS), f32),
        "swa_w_o": w(ks[14], (N_B_LAYERS_2, SWA_Q_HEADS * HEAD_DIM, D_MODEL), SWA_Q_HEADS * HEAD_DIM),
        "final_norm": gain(ks[15], (D_MODEL,)),
    }

def second_block(x, ffn1_norm, ffn1_w_in, ffn1_w_out, mix_norm, ffn2_norm, ffn2_w_in, ffn2_w_out,
              sb_w_qkv, sb_w_o, kv_norm, kv_w, swa_w_q, swa_sinks, swa_w_o, final_norm):
    B, S, D = x.shape
    pos = jnp.arange(S)
    h = x
    k_shared = None
    v_shared = None
    for layer in range(DEPTH):
        h = h + FFN_RES_SCALE * swiglu(rms_norm(h, ffn1_norm[layer]), ffn1_w_in[layer], ffn1_w_out[layer])
        hn = rms_norm(h, mix_norm[layer])
        if layer < N_A_LAYERS_2:
            qkv = (hn @ sb_w_qkv[layer]).reshape(B, S, 3, SB_HEADS, HEAD_DIM)
            o = stick_breaking_attention(qkv[:, :, 0], qkv[:, :, 1], qkv[:, :, 2])
            h = h + o.reshape(B, S, SB_HEADS * HEAD_DIM) @ sb_w_o[layer]
        else:
            j = layer - N_A_LAYERS_2
            q = rotary((hn @ swa_w_q[j]).reshape(B, S, SWA_Q_HEADS, HEAD_DIM), pos)
            o = sliding_window_sink_attention(q, k_shared, v_shared, swa_sinks[j])
            h = h + o.reshape(B, S, SWA_Q_HEADS * HEAD_DIM) @ swa_w_o[j]
        h = h + FFN_RES_SCALE * swiglu(rms_norm(h, ffn2_norm[layer]), ffn2_w_in[layer], ffn2_w_out[layer])
        if layer == N_A_LAYERS_2 - 1:
            kv = (rms_norm(h, kv_norm) @ kv_w).reshape(B, S, 2, SWA_KV_HEADS, HEAD_DIM)
            k_shared = rotary(kv[:, :, 0], pos)
            v_shared = kv[:, :, 1]
    return rms_norm(h, final_norm)


def setup_inputs(seed=0):
    out = dict(first_inputs(seed))
    for name, value in second_inputs(seed + 1).items():
        if name != "x":
            out[name + "_2"] = value
    return out


def reference(
    x, norm_gain, ffn_w_in, ffn_w_out, a_w_in, a_lb_logits, a_out_gain, a_w_out, kv_norm, w_kv,
    k_gain, b_w_q, b_q_gain, b_w_o, rel_bias, ffn1_norm_2, ffn1_w_in_2, ffn1_w_out_2,
    mix_norm_2, ffn2_norm_2, ffn2_w_in_2, ffn2_w_out_2, sb_w_qkv_2, sb_w_o_2, kv_norm_2, kv_w_2,
    swa_w_q_2, swa_sinks_2, swa_w_o_2, final_norm_2,
):
    x = first_block(
        x, norm_gain, ffn_w_in, ffn_w_out, a_w_in, a_lb_logits, a_out_gain, a_w_out, kv_norm,
        w_kv, k_gain, b_w_q, b_q_gain, b_w_o, rel_bias,
    )
    return second_block(
        x, ffn1_norm_2, ffn1_w_in_2, ffn1_w_out_2, mix_norm_2, ffn2_norm_2, ffn2_w_in_2,
        ffn2_w_out_2, sb_w_qkv_2, sb_w_o_2, kv_norm_2, kv_w_2, swa_w_q_2, swa_sinks_2,
        swa_w_o_2, final_norm_2,
    )


_drawn_inputs = setup_inputs


def setup_inputs(seed=0):
    import zlib

    import numpy as np

    out = dict(_drawn_inputs(seed))
    spreads = {}
    factors = {'k_gain': 3.381,
     'b_q_gain': 3.607,
     'ffn1_norm_2': 6.31,
     'mix_norm_2': 4.928,
     'ffn2_norm_2': 7.312,
     'kv_norm_2': 8.0,
     'swa_sinks_2': 166.074,
     'final_norm_2': 23.987}
    for name, (base, spread) in spreads.items():
        noise = np.random.default_rng([zlib.crc32(name.encode()), seed]).standard_normal(out[name].shape)
        drawn = base * np.exp(spread * noise) if base else spread * noise
        out[name] = __import__('jax').numpy.asarray(drawn.astype(out[name].dtype))
    for name, factor in factors.items():
        out[name] = (out[name] * factor).astype(out[name].dtype)
    return out
```

```python
from contextlib import ExitStack

import numpy as np

import concourse.bass as bass
from concourse import mybir

ALU = mybir.AluOpType
ACT = mybir.ActivationFunctionType
AX = mybir.AxisListType
F32 = mybir.dt.float32
F32R = mybir.dt.float32r

P = 128
T = 256
D = 1024
KC = D // P
FF = 2816
FC = FF // P
FPAIRS = FC // 2
W2 = 2 * P
NPAIR = KC // 2
EPS = 1e-6
EXP_MAX = 2.0 ** 60
GATE_MIN = 2.0 ** -60
NEG = -1e30

HEADS = 16
HD = 64
GROUPS = 3
WINDOWS = (128, 512, 2048)
DILATIONS = (1, 4, 16)
BUCKETS = 32
MAX_DISTANCE = 2048
QKV = GROUPS * HEADS * HD
A_HEADS = 8
LEVELS = 8
KV_HEADS = 4
SWA_WINDOW = 128
ROPE_THETA = 10000.0

HALVES = {
    "k8": ((0, 4 * W2, 4), (4 * W2, 4 * W2, 4)),
    "k11": ((0, 6 * W2, 6), (6 * W2, 5 * W2, 5)),
}
SLOT = FC // 2 * W2
HALF = 6 * W2


def t5_bucket(dist):
    exact = BUCKETS // 2
    large = exact + (np.log(np.maximum(dist, 1) / exact) / np.log(MAX_DISTANCE / exact) * (BUCKETS - exact)).astype(np.int32)
    return np.where(dist < exact, dist, np.minimum(large, BUCKETS - 1)).astype(np.int32)


CONST_WIDTHS = [
    ("ident", P), ("ones", P), ("blk64", P), ("neg_suffix", P), ("neg_ones", P), ("rot", P), ("dup0", P), ("dup1", P),
    ("strict", P), ("neg_mask", P), ("hg_mask", (LEVELS - 1) * P), ("swa_mask", T), ("cos", T), ("sin", T), ("onehot", GROUPS * 3 * P),
]
CONST_AT = {}
_at = 0
for _name, _width in CONST_WIDTHS:
    CONST_AT[_name] = (_at, _width)
    _at += _width
CONST_COLS = _at


def constants():
    c = np.zeros((P, CONST_COLS), np.float32)

    def put(name, value):
        at, width = CONST_AT[name]
        c[:value.shape[0], at:at + width] = value.reshape(value.shape[0], width)

    i = np.arange(P)
    put("ident", np.eye(P))
    put("ones", np.ones((P, P)))
    put("blk64", (i[:, None] // HD == i[None, :] // HD).astype(np.float32))
    put("neg_suffix", -(i[:, None] >= i[None, :]).astype(np.float32))
    put("neg_ones", -np.ones((P, P)))
    rot = np.zeros((P, P), np.float32)
    for t in range(P):
        if t % HD < HD // 2:
            rot[t + HD // 2, t] = -1.0
        else:
            rot[t - HD // 2, t] = 1.0
    put("rot", rot)
    for half in range(2):
        put(f"dup{half}", (i[:, None] == HD * half + i[None, :] % HD).astype(np.float32))
    put("strict", (i[:, None] < i[None, :]).astype(np.float32))
    put("neg_mask", np.where(i[:, None] < i[None, :], 0.0, NEG).astype(np.float32))
    mask = np.zeros((P, LEVELS - 1, P), np.float32)
    for level in range(LEVELS - 1):
        b = 1 << level
        n = np.arange(P) % (P // 2) // b
        mask[:, level] = (i[:, None] // (2 * b) == n[None, :]) & (i[:, None] % (2 * b) < b)
    put("hg_mask", mask)
    diff = P + i[:, None] - np.arange(T)[None, :]
    put("swa_mask", np.where((diff >= 0) & (diff < SWA_WINDOW), 0.0, NEG).astype(np.float32))
    half = HD // 2
    inv_freq = np.float32(ROPE_THETA) ** (-np.arange(half, dtype=np.float32) / np.float32(half))
    angle = np.arange(T, dtype=np.float32)[None, :] * inv_freq[i % half][:, None]
    put("cos", np.cos(angle, dtype=np.float32))
    put("sin", np.sin(angle, dtype=np.float32))
    onehot = np.zeros((BUCKETS + 1, GROUPS, 3 * P), np.float32)
    dist = T - 1 - np.arange(3 * P)
    for g, (w, dil) in enumerate(zip(WINDOWS, DILATIONS)):
        valid = (dist >= 0) & (dist <= w) & (dist % dil == 0)
        bucket = t5_bucket(np.maximum(dist, 0))
        onehot[bucket[valid], g, np.nonzero(valid)[0]] = 1.0
        onehot[BUCKETS, g] = ~valid
    put("onehot", onehot)
    return c


def build_program(nc, io, upto=None):
    ctx = ExitStack()

    def sb(name, shape, dt=F32, stack=ctx):
        return stack.enter_context(nc.sbuf_tensor(name, shape, dt))

    def sem(name):
        return ctx.enter_context(nc.semaphore(name))

    LAYERS = ["ffn0", "hgrn", "ffn1", "ffn2", "dil", "ffn3", "ffn4", "stick", "ffn5", "swa_kv", "ffn6", "swa", "ffn7"]
    layers = LAYERS[:upto]
    stages = {}
    kinds = []
    fills = [NPAIR]

    def stage(name, kind, count, per_fill=1):
        assert len(kinds) % 2 == 0 and fills[0] % 2 == 0
        stages[name] = {"base": len(kinds), "count": count, "kind": kind, "fill": fills[0]}
        kinds.extend([kind] * count)
        fills[0] += count // per_fill

    for layer in layers:
        if layer.startswith("ffn"):
            stage(f"up{layer[3:]}", "k8", 2 * FPAIRS)
            stage(f"down{layer[3:]}", "k11", 2 * NPAIR, 2)
        if layer == "hgrn":
            stage("hgrn", "k8", 4 * A_HEADS // 2)
        if layer == "dil":
            stage("dil", "k8", 3 * GROUPS * HEADS // 4)
        if layer == "stick":
            stage("stick", "k8", 3 * HEADS // 4)
        if layer == "swa_kv":
            stage("swa_kv", "k8", 2)
        if layer == "swa":
            stage("swa", "k8", HEADS // 4)
        if layer in ("hgrn", "dil", "stick", "swa"):
            stage(f"{layer}_out", "k8", NPAIR)

    GAIN = {}
    rows = 0
    for name, n in (("norm_gain", 6 * KC), ("kv_norm", KC), ("ffn1_norm_2", 2 * KC), ("mix_norm_2", 2 * KC),
                    ("ffn2_norm_2", 2 * KC), ("kv_norm_2", KC), ("final_norm_2", KC)):
        GAIN[name] = rows
        rows += n
    GAIN_ROWS = rows
    NG = lambda layer, k: GAIN["norm_gain"] + (3 * layer + k) * KC
    updates = [
        ("input", [("g", NG(0, 0))]),
        ("down0", [("g", NG(0, 1))]),
        ("hgrn_out", [("g", NG(0, 2))]),
        ("down1", [("g", NG(1, 0)), ("k", GAIN["kv_norm"])]),
        ("down2", [("g", NG(1, 1))]),
        ("dil_out", [("g", NG(1, 2))]),
        ("down3", [("g", GAIN["ffn1_norm_2"])]),
        ("down4", [("g", GAIN["mix_norm_2"])]),
        ("stick_out", [("g", GAIN["ffn2_norm_2"])]),
        ("down5", [("k", GAIN["kv_norm_2"]), ("g", GAIN["ffn1_norm_2"] + KC)]),
        ("down6", [("g", GAIN["mix_norm_2"] + KC)]),
        ("swa_out", [("g", GAIN["ffn2_norm_2"] + KC)]),
        ("down7", []),
    ]
    updates = [(n, us) for n, us in updates if n == "input" or n in stages]
    updates[-1] = (updates[-1][0], [])
    update_of = {name: e for e, (name, _) in enumerate(updates)}
    LAST = len(updates) - 1
    g_before, k_before = [], []
    for e in range(LAST + 1):
        g_before.append(KC * sum(u[0] == "g" for _, us in updates[:e] for u in us))
        k_before.append(KC * sum(u[0] == "k" for _, us in updates[:e] for u in us))
    reads = {"up0": 0, "hgrn": 1, "up1": 2, "up2": 3, "dil": 4, "up3": 5, "up4": 6, "stick": 7,
             "up5": 8, "swa_kv": 9, "up6": 9, "swa": 10, "up7": 11}
    norms = reads

    raw = sb("raw", [P, 4, HALF])
    whi = sb("whi", [P, 2, SLOT], F32R)
    wlo = sb("wlo", [P, 2, SLOT], F32R)
    x = sb("x", [P, KC, T])
    xg_hi = sb("xg_hi", [P, KC, T], F32R)
    xg_lo = sb("xg_lo", [P, KC, T], F32R)
    ROW = 3 * P
    REPEAT = P // HEADS
    BIAS_STORES = 4 * GROUPS
    spare = ExitStack()
    bias_rows = sb("bias_rows", [P, GROUPS, ROW], F32, spare)
    rbx = sb("rbx", [BUCKETS + 1, GROUPS * HEADS], F32, spare)
    rbx8 = sb("rbx8", [BUCKETS + 1, GROUPS * P], F32, spare)
    onehot = sb("onehot", [BUCKETS + 1, GROUPS * ROW], F32, spare)
    rows_late = sb("rows_late", [P, P], F32, spare)
    aux_in = sb("aux_in", [P, P], F32, spare)
    spare.close()
    xk_hi = sb("xk_hi", [P, KC, T], F32R)
    xk_lo = sb("xk_lo", [P, KC, T], F32R)
    CONSTS = CONST_AT["hg_mask"][0]
    cst = sb("cst", [P, CONSTS])
    gains = sb("gains", [P, GAIN_ROWS])
    AUX = 2 * A_HEADS + 1 + 2 * GROUPS
    aux = sb("aux", [P, AUX])
    q_gain = sb("q_gain", [P, GROUPS])
    lb = sb("lb", [P, A_HEADS])
    oml = sb("oml", [P, A_HEADS])
    lbt = sb("lbt", [P, 4, A_HEADS])
    eps = sb("eps", [P, 1])
    sinks = sb("sinks", [P, HEADS])
    r = sb("r", [P, 2, T])
    ms = sb("ms", [P, T])
    ms_ln = sb("ms_ln", [P, T])
    r0 = sb("r0", [P, T])
    newton = sb("newton", [P, 2, T])
    sq = sb("sq", [P, 2 * T])
    acc = sb("acc", [P, 2 * T])

    def const(name):
        at, width = CONST_AT[name]
        return cst[:, at:at + width]

    flat = lambda t: t.rearrange("p c t -> p (c t)")
    ident, ones = const("ident"), const("ones")

    region = ExitStack()
    hT_hi = sb("hT_hi", [P, FC, T], F32R, region)
    hT_lo = sb("hT_lo", [P, FC, T], F32R, region)
    gate = sb("gate", [P, 2 * T], F32, region)
    gate_e = sb("gate_e", [P, 2 * T], F32, region)
    gate_s = sb("gate_s", [P, 2 * T], F32, region)
    gate_r = sb("gate_r", [P, 2 * T], F32, region)
    h = sb("h", [P, 2 * T], F32, region)
    kv_t = sb("kv_t", [P, 2 * T], F32, region)
    kv_v = sb("kv_v", [P, 2 * T], F32, region)
    kv_c = sb("kv_c", [P, 2 * T], F32, region)
    kv_s = sb("kv_s", [P, 2 * T], F32, region)
    kdup = sb("kdup", [P, KV_HEADS, T], F32, region)
    v2 = sb("v2", [P, 2, KV_HEADS * HD], F32, region)
    rope = sb("rope", [P, 2, T], F32, region)
    swa_mask = sb("swa_mask", [P, T], F32, region)
    region.close()
    init = ExitStack()
    x_in = sb("x_in", [P, T // P, D], F32, init)
    rows_in = sb("rows_in", [P, P], F32, init)
    fin = sb("fin", [P, KC, T], F32, init)
    out_sb = sb("out_sb", [P, T // P, D], F32, init)
    init.close()

    bias_dram = nc.dram_tensor("bias_by_distance", (GROUPS * HEADS * P * ROW,), F32, kind="Internal").ap()

    ps = ctx.enter_context(nc.psum_tensor("ps", [P, 8, 2 * T], F32))
    BANK_SUM = 2
    OUT_BANKS = {"hgrn_out": (0, 1, 6, 7), "dil_out": (0, 1, 2, 7), "stick_out": (0, 1, 2, 3), "swa_out": (0, 1, 2, 6)}

    def out_before(name):
        return (NPAIR - 1) * [n for n in OUT_BANKS if n in stages].index(name)


    w_arrived = [sem(f"w_arrived{q}") for q in range(4)]
    hi_done = sem("hi_done")
    lo_done = sem("lo_done")
    slot_done = sem("slot_done")
    evac_done = sem("evac_done")
    const_in = sem("const_in")
    const_late = sem("const_late")
    rows_arrived, late_arrived, late_turned = sem("rows_arrived"), sem("late_arrived"), sem("late_turned")
    x_arrived = sem("x_arrived")
    x_turned = sem("x_turned")
    rows_turned = sem("rows_turned")
    gains_ready = sem("gains_ready")
    aux_ready = sem("aux_ready")
    lb_steps = sem("lb_steps")
    lb_exp = sem("lb_exp")
    lb_ready = sem("lb_ready")
    eps_ready = sem("eps_ready")
    bias_in, bias_masked, bias_made, bias_copied, bias_stored = [sem(n) for n in ("bias_in", "bias_masked", "bias_made", "bias_copied", "bias_stored")]
    xhi_done = sem("xhi_done")
    xg_ready = sem("xg_ready")
    xk_ready = sem("xk_ready")
    sq_done = sem("sq_done")
    acc_done = sem("acc_done")
    ss_ready = sem("ss_ready")
    ms_ready = sem("ms_ready")
    ms_ln_done = sem("ms_ln_done")
    r0_ready = sem("r0_ready")
    newton_a = sem("newton_a")
    newton_b = sem("newton_b")
    r_ready = sem("r_ready")
    gate_exp = sem("gate_exp")
    gate_den = sem("gate_den")
    gate_ln = sem("gate_ln")
    sig_ready = sem("sig_ready")
    gs_done = sem("gs_done")
    gr_done = sem("gr_done")
    hhi_done = sem("hhi_done")
    hT_ready = sem("hT_ready")
    out_ready = sem("out_ready")
    o_ready = sem("o_ready")
    final_y = sem("final_y")
    final_turned = sem("final_turned")
    final_copied = sem("final_copied")
    out_stored = sem("out_stored")

    def at(st, i, j):
        return st["base"] + j + 2 * i, st["base"] // 2 + i, j

    def ahead_of(st, i, j):
        n, n2, par = at(st, i, j)
        if isinstance(i, int):
            return n + 2, n2 + 1, par, kinds[n + 2] if n + 2 < len(kinds) else None
        return n + 2, n2 + 1, par, st["kind"]

    def all_but_last(eng, count, body):
        with eng.Fori(0, count - 1) as i:
            body(i)
        body(count - 1)

    def bank_of(fill):
        return ps[:, fill % 2, :]

    def pair(ap):
        return ap.rearrange("p (c t) -> p c t", c=2)

    def r_of(e):
        return r[:, e % 2:e % 2 + 1, :].broadcast_to([P, 2, T])

    hT_hi_flat, hT_lo_flat = flat(hT_hi[:, :, :]), flat(hT_lo[:, :, :])
    x_flat = flat(x[:, :, :])
    xpair = lambda m: x_flat[:, 2 * T * m:2 * T * (m + 1)]
    operand = {"g": (xg_hi, xg_lo), "k": (xk_hi, xk_lo)}

    ffn_weights = [(io["ffn_w_in"][layer, k], io["ffn_w_out"][layer, k]) for layer in range(2) for k in range(2)]
    ffn_weights += [(io[f"ffn{k}_w_in_2"][layer], io[f"ffn{k}_w_out_2"][layer]) for layer in range(2) for k in (1, 2)]
    order = [name for name in stages if name in reads]
    before = dict(zip(order[1:], order))
    slot0 = lambda n: (n, n // 2, n % 2, kinds[n])
    FIRST_ROWS = GAIN["kv_norm"]
    LATE_LOADS = len(GAIN) - 1 + 5

    region = ExitStack()
    hg_raw = [sb(f"hg_raw{n}", [P, 2 * T], F32, region) for n in range(2)]
    hg_exp = [sb(f"hg_exp{n}", [P, 2 * T], F32, region) for n in range(3)]
    hg_q = sb("hg_q", [P, 2, 2 * T], F32, region)
    hg_k = sb("hg_k", [P, 2, 2 * T], F32, region)
    hg_c = sb("hg_c", [P, 2 * T], F32, region)
    hg_g = sb("hg_g", [P, 2 * T], F32, region)
    hg_v = sb("hg_v", [P, 2, T // P, 2 * P], F32, region)
    hg_E = sb("hg_E", [P, 2, LEVELS, T], F32, region)
    hg_M = sb("hg_M", [P, LEVELS, T], F32, region)
    hg_P = sb("hg_P", [P, T], F32, region)
    hg_Pc = sb("hg_Pc", [P, P], F32, region)
    hg_out = sb("hg_out", [P, KC, T], F32, region)
    hg_osq = sb("hg_osq", [P, T], F32, region)
    hg_rms = sb("hg_rms", [P, T], F32, region)
    hg_mask = sb("hg_mask", [P, LEVELS - 1, P], F32, region)
    hg_oT = [sb(f"hg_oT{n}", [P, KC, T], F32R, region) for n in range(2)]
    region.close()
    hg_mask_in, hg_zero = sem("hg_mask_in"), sem("hg_zero")
    hg_e = sem("hg_e")
    hg_d = sem("hg_d")
    hg_l = sem("hg_l")
    hg_s = sem("hg_s")
    hg_qs, hg_gs = sem("hg_qs"), sem("hg_gs")
    hg_f, hg_kk, hg_lf, hg_cum = sem("hg_f"), sem("hg_kk"), sem("hg_lf"), sem("hg_cum")
    hg_vtr, hg_vt = sem("hg_vtr"), sem("hg_vt")
    hg_dif, hg_dec = sem("hg_dif"), sem("hg_dec")
    hg_qd, hg_kd, hg_S, hg_sm, hg_Pr, hg_Pcr = [sem(n) for n in ("hg_qd", "hg_kd", "hg_S", "hg_sm", "hg_Pr", "hg_Pcr")]
    hg_o, hg_oc, hg_os2, hg_oss, hg_oln, hg_or = [sem(n) for n in ("hg_o", "hg_oc", "hg_os2", "hg_oss", "hg_oln", "hg_or")]
    hg_on, hg_og, hg_ohi = sem("hg_on"), sem("hg_og"), sem("hg_ohi")
    HG_UNITS = A_HEADS // 2
    HG_QFI = 3 * HG_UNITS
    HG_SLOTS = HG_QFI + HG_UNITS
    HG_TICKS = HG_SLOTS + NPAIR
    HG_SCORES = 3
    HG_OUT = 2
    HG_VBANK = 7
    HG_NORM = 2 * A_HEADS
    HG_START = (3, 4, 6, 7, 9, 10, 12, 13)
    HG_GATE = tuple(max(HG_QFI + u + 1, HG_START[2 * u + 1] + 5) for u in range(HG_UNITS))

    def hg_heads(t, offset):
        return [hd for hd in range(A_HEADS) if HG_START[hd] + offset == t]

    def hg_units(t, offset):
        return [u for u in range(HG_UNITS) if HG_GATE[u] + offset == t]

    def hg_slot(t):
        return (t // 3, t % 3) if t < HG_QFI else (t - HG_QFI, 3)

    def hg_cols(hd):
        return slice(T * (hd % 2), T * (hd % 2 + 1))

    def hg_half(ap, level, second):
        b = 1 << level
        return ap.rearrange("p (n b) -> p n b", b=2 * b)[:, :, b * second:b * second + b]

    hg_all = ps[:, HG_SCORES:HG_SCORES + 3, :].rearrange("p b n -> p (b n)")
    HG_OWN = (LEVELS - 1) * P
    HG_CROSS = HG_OWN + T

    region = ExitStack()
    dl_t = sb("dl_t", [P, 2, 2 * T], F32, region)
    dl_q = sb("dl_q", [P, GROUPS, 2, 2 * T], F32, region)
    dl_k = sb("dl_k", [P, 2, GROUPS, 2 * T], F32, region)
    dl_v = sb("dl_v", [P, 2, GROUPS, T // P, 4 * HD], F32, region)
    dl_bias = sb("dl_bias", [P, 2, GROUPS, T], F32, region)
    dl_S = sb("dl_S", [P, 2, 3 * GROUPS * P], F32, region)
    dl_PT = sb("dl_PT", [P, 2, 3 * GROUPS * P], F32, region)
    dl_max = sb("dl_max", [P, 2, 2], F32, region)
    dl_nmax = sb("dl_nmax", [P, 2, 2], F32, region)
    dl_sum = sb("dl_sum", [P, 2, 2], F32, region)
    dl_rcp = sb("dl_rcp", [P, 2, 2], F32, region)
    dl_oT = [sb(f"dl_oT{n}", [P, KC, T], F32R, region) for n in range(2)]
    region.close()
    dl_sq, dl_rr = sq, flat(newton[:, :, :])
    q_gain_ready = sem("q_gain_ready")
    dl_sqd, dl_ss, dl_ln, dl_rrd, dl_qkd = [sem(n) for n in ("dl_sqd", "dl_ss", "dl_ln", "dl_rrd", "dl_qkd")]
    dl_vtr, dl_vt, dl_bias_in0, dl_bias_in1 = [sem(n) for n in ("dl_vtr", "dl_vt", "dl_bias_in0", "dl_bias_in1")]
    dl_scored, dl_biased, dl_neg, dl_exp, dl_rd, dl_sc0, dl_sc1 = [
        sem(n) for n in ("dl_scored", "dl_biased", "dl_neg", "dl_exp", "dl_rd", "dl_sc0", "dl_sc1")]
    dl_turned, dl_PTd, dl_pv, dl_ohi, dl_zero = [sem(n) for n in ("dl_turned", "dl_PTd", "dl_pv", "dl_ohi", "dl_zero")]
    DL_UNIT = 3 * GROUPS
    DL_UNITS = HEADS // 4
    DL_SLOTS = DL_UNIT * DL_UNITS
    DL_TICKS = DL_SLOTS + NPAIR
    DL_BANK = 3
    DL_OUT, DL_VBANK = 6, 7
    DL_SCORES = (13, 14, 16, 18)
    DL_SCALE = (14, 15, 17, 19)
    DL_TURN = (15, 17, 19, 21)
    DL_PV = (19, 22)

    def dl_due(point, steps):
        return [len(steps) * u + a for u in range(DL_UNITS) for a, at_half in enumerate(steps) if point == 2 * DL_UNIT * u + at_half]

    def dl_projected(point):
        if point == 2 * DL_SLOTS - 1:
            return DL_SLOTS - 1
        return point // 2 - 1 if point % 2 == 0 and 1 <= point // 2 < DL_SLOTS else None

    def dl_slot(t):
        return t // DL_UNIT, t % DL_UNIT, t % DL_UNIT >= 2 * GROUPS

    def dl_qk_number(t):
        u, j, _ = dl_slot(t)
        return 2 * GROUPS * u + min(j, 2 * GROUPS)

    def dl_v_number(t):
        u, j, _ = dl_slot(t)
        return GROUPS * u + max(j - 2 * GROUPS, 0)

    def dl_blocks(ap, keys):
        at0 = 0 if keys == T else GROUPS * T
        return ap[:, at0:at0 + GROUPS * keys].rearrange("p (g k) -> p g k", g=GROUPS)

    dl_ps = ps[:, DL_BANK:DL_BANK + 3, :].rearrange("p b n -> p (b n)")[:, 0:3 * GROUPS * P]

    region = ExitStack()
    sk_q = sb("sk_q", [P, 2, 2, 2 * T], F32, region)
    sk_k = sb("sk_k", [P, 2, 2 * T], F32, region)
    sk_t = sb("sk_t", [P, 2, 2 * T], F32, region)
    sk_v = sb("sk_v", [P, 2, T // P, 4 * HD], F32, region)
    sk_e = sb("sk_e", [P, 6 * T], F32, region)
    sk_sp = sb("sk_sp", [P, 6 * T], F32, region)
    sk_w = sb("sk_w", [P, 4, 6 * T], F32, region)
    sk_oT = [sb(f"sk_oT{n}", [P, KC, T], F32R, region) for n in range(2)]
    region.close()
    sk_z, sk_abs, sk_ex, sk_ln, sk_spd, sk_sum, sk_wr = [sem(n) for n in ("sk_z", "sk_abs", "sk_ex", "sk_ln", "sk_spd", "sk_sum", "sk_wr")]
    sk_vtr, sk_vt, sk_pv, sk_ohi = [sem(n) for n in ("sk_vtr", "sk_vt", "sk_pv", "sk_ohi")]
    sk_zero = sem("sk_zero")
    SK_UNITS = HEADS // 4
    SK_QK = 2 * SK_UNITS
    SK_SLOTS = SK_QK + SK_UNITS
    SK_TICKS = SK_SLOTS + NPAIR
    SK_BANK, SK_OUT, SK_VBANK = 2, 6, 7
    sk_all = ps[:, SK_BANK:SK_BANK + 4, :].rearrange("p b n -> p (b n)")[:, T:7 * T]

    def sk_first(ap, odd):
        return ap[:, T + 2 * T * odd:3 * T + 2 * T * odd].rearrange("p (a t) -> p a t", a=2)

    def sk_second(ap, odd):
        return ap[:, 5 * T * odd:5 * T * odd + T].rearrange("p (a t) -> p a t", a=2)

    def sk_scores_at(t):
        return [u for u in range(SK_UNITS) if t == 2 * u + 2]

    def sk_sums_at(t):
        return [u for u in range(SK_UNITS) if t == 2 * u + 4]

    def sk_values_at(t):
        return [u for u in range(SK_UNITS) if t == SK_QK + u + 1]

    kv_rope_in = sem("kv_rope_in")
    kv_rot, kv_cos, kv_sin, kv_sum, kv_dup, kv_dupd, kv_vtr, kv_vt = [
        sem(n) for n in ("kv_rot", "kv_cos", "kv_sin", "kv_sum", "kv_dup", "kv_dupd", "kv_vtr", "kv_vt")]
    KV_ROT, KV_DUP, KV_VBANK = 6, 3, 7

    def rope_of(which):
        return rope[:, which:which + 1, :].broadcast_to([P, 2, T])

    region = ExitStack()
    sw_t = sb("sw_t", [P, 2, 2 * T], F32, region)
    sw_c = sb("sw_c", [P, 2, 2 * T], F32, region)
    sw_q = sb("sw_q", [P, 2, 2, 2 * T], F32, region)
    sw_s = sb("sw_s", [P, 2 * T], F32, region)
    sw_S = sb("sw_S", [P, 2, 6 * T], F32, region)
    sw_PT = sb("sw_PT", [P, 6 * T], F32, region)
    sw_max, sw_nmax, sw_sum, sw_sink, sw_den, sw_rcp = [
        sb(n, [P, 2, 2, 4], F32, region) for n in ("sw_max", "sw_nmax", "sw_sum", "sw_sink", "sw_den", "sw_rcp")]
    sw_oT = [sb(f"sw_oT{n}", [P, KC, T], F32R, region) for n in range(2)]
    region.close()
    sw_rot, sw_cos, sw_sin, sw_qr, sw_scored, sw_masked, sw_neg, sw_dm, sw_exp, sw_snk = [
        sem(n) for n in ("sw_rot", "sw_cos", "sw_sin", "sw_qr", "sw_scored", "sw_masked", "sw_neg", "sw_dm", "sw_exp", "sw_snk")]
    sw_dn, sw_rd, sw_sc0, sw_sc1, sw_turned, sw_PTd, sw_pv, sw_ohi, sw_zero = [
        sem(n) for n in ("sw_dn", "sw_rd", "sw_sc0", "sw_sc1", "sw_turned", "sw_PTd", "sw_pv", "sw_ohi", "sw_zero")]
    SW_UNITS = HEADS // 4
    SW_TICKS = SW_UNITS + NPAIR
    SW_BANK, SW_OUT = 3, 7

    def sw_scores(a, tile):
        return ps[:, SW_BANK + a // 2, T * (a % 2):T * (a % 2 + 1)] if tile else ps[:, SW_BANK + 2, P * a:P * (a + 1)]

    def sw_biased(u, a, tile):
        S = sw_S[:, u % 2, :]
        return S[:, T * a:T * (a + 1)] if tile else S[:, 4 * T + P * a:4 * T + P * (a + 1)]

    sw_turn = ps[:, SW_BANK:SW_BANK + 3, :].rearrange("p b n -> p (b n)")

    def sw_keys0(ap, a):
        return ap[:, T * a:T * (a + 1)]

    def sw_keys1(ap, a):
        return ap[:, 4 * T + P * a:4 * T + P * (a + 1)]

    def sw_at(t, offset):
        return [u for u in range(SW_UNITS) if u + offset == t]

    block = ctx.enter_context(nc.Block())

    @block.sync
    def _(sp):
        sp.dma_start(x_in[:, :, :], io["x"].rearrange("b (t p) d -> p (b t) d", p=P)).then_inc(x_arrived, 16)

        def load(n, n2, par, kind, source):
            k = 0
            for half, (_, size, chunks) in enumerate(HALVES[kind]):
                sp.wait_ge(lo_done, 2 * n + half + 1)
                sp.dma_start(raw[:, 2 * par + half, :size].rearrange("p (k w) -> p k w", w=W2),
                             source(k, k + chunks)).then_inc(w_arrived[2 * par + half], 16)
                k += chunks

        def columns(w):
            v = w.rearrange("(k p) n -> p k n", p=P)
            return lambda col, k0=0: lambda a, b: v[:, k0 + a:k0 + b, bass.ds(col, W2)]

        def ffn(f):
            w_in, w_out = [columns(w) for w in ffn_weights[f]]
            st = stages[f"up{f}"]
            with sp.Fori(0, FPAIRS) as i:
                load(*at(st, i, 0), "k8", w_in(i * W2))
                load(*at(st, i, 1), "k8", w_in(i * W2 + FF))
            st = stages[f"down{f}"]
            with sp.Fori(0, NPAIR) as i:
                load(*at(st, i, 0), "k11", w_out(i * W2))
                load(*at(st, i, 1), "k11", w_out(i * W2, FC // 2))

        def twos(name, col, skip=0, count=None):
            st = {**stages[name], "base": stages[name]["base"] + 2 * skip}
            w, first = col
            take = columns(w)
            with sp.Fori(0, (count or st["count"]) // 2) as i:
                for j in range(2):
                    load(*at(st, i, j), "k8", take(2 * W2 * i + (first + W2 * j)))

        def rows_of(name, w):
            st = stages[name]
            with sp.Fori(0, NPAIR // 2) as i:
                for j in range(2):
                    n, _, par = at(st, i, j)
                    for half in range(2):
                        sp.wait_ge(lo_done, 2 * n + half + 1)
                        sp.dma_start(raw[:, 2 * par + half, :D], w[bass.ds(4 * P * i + P * (2 * j + half), P), :]).then_inc(w_arrived[2 * par + half], 16)

        def two_units(name, sources):
            st = stages[name]
            per = len(sources)
            with sp.Fori(0, HEADS // 8) as v:
                for j, (w, first) in enumerate(2 * sources):
                    load(*at(st, per * v + j // 2, j % 2), "k8", columns(w)(2 * W2 * v + (first + W2 * (j // per))))

        def units(name, sources):
            st = stages[name]
            per = len(sources)
            with sp.Fori(0, HEADS // 4) as u:
                for j, (w, first) in enumerate(sources):
                    load(*at(st, per // 2 * u + j // 2, j % 2), "k8", columns(w)(W2 * u + first))

        for layer in layers:
            if layer.startswith("ffn"):
                ffn(int(layer[3:]))
            if layer == "hgrn":
                two_units("hgrn", [(io["a_w_in"][0], D * part) for part in range(3)])
                twos("hgrn", (io["a_w_in"][0], 3 * D), 3 * A_HEADS // 4, D // W2)
                rows_of("hgrn_out", io["a_w_out"][0])
            if layer == "dil":
                two_units("dil", [(w, D * g) for g in range(GROUPS) for w in (io["b_w_q"][0], io["w_kv"])]
                          + [(io["w_kv"], QKV + D * g) for g in range(GROUPS)])
                rows_of("dil_out", io["b_w_o"][0])
            if layer == "stick":
                units("stick", [(io["sb_w_qkv_2"][0], 0), (io["sb_w_qkv_2"][0], D)])
                twos("stick", (io["sb_w_qkv_2"][0], 2 * D), HEADS // 4, D // W2)
                rows_of("stick_out", io["sb_w_o_2"][0])
            if layer == "swa_kv":
                twos("swa_kv", (io["kv_w_2"], 0))
            if layer == "swa":
                twos("swa", (io["swa_w_q_2"][0], 0))
                rows_of("swa_out", io["swa_w_o_2"][0])
        for t in range(T // P):
            sp.wait_ge(final_copied, t + 1)
            sp.dma_start(io["out"][0, P * t:P * (t + 1), :], out_sb[:, t, :]).then_inc(out_stored, 16)
        sp.wait_ge(out_stored, 16 * (T // P))

    @block.tensor
    def _(pe):
        pe.sem_inc(slot_done, 2)

        def products(n, n2, par, kind, hi, lo, fill, bank, first=True, last=True, chunk0=0, wait_x=None, mid=None):
            if first:
                pe.wait_ge(evac_done, fill + 1)
            k = 0
            total = sum(chunks for _, _, chunks in HALVES[kind])
            for half, (_, _, chunks) in enumerate(HALVES[kind]):
                pe.wait_ge(lo_done, 2 * n + half + 5)
                for k in range(k, k + chunks):
                    if wait_x:
                        pe.wait_ge(wait_x[0], wait_x[1] + k + 1)
                    for m in range(2):
                        out = ps[:, bank, T * m:T * (m + 1)]
                        w = slice(W2 * k + P * m, W2 * k + P * (m + 1))
                        begin, end = first and k == 0 and m == 0, last and k == total - 1 and m == 1
                        nc.tensor.matmul(out, whi[:, par, w], hi[:, chunk0 + k, :], start=begin, stop=False)
                        nc.tensor.matmul(out, whi[:, par, w], lo[:, chunk0 + k, :], start=False, stop=False)
                        mm = nc.tensor.matmul(out, wlo[:, par, w], hi[:, chunk0 + k, :], start=False, stop=end)
                k += 1
                if half == 0 and mid:
                    mid()
            mm.then_inc(slot_done, 1)

        def sum_squares(e):
            pe.wait_ge(acc_done, NPAIR * (e + 1))
            nc.tensor.matmul(ps[:, BANK_SUM, 0:T], ones, acc[:, 0:T], start=True, stop=False)
            nc.tensor.matmul(ps[:, BANK_SUM, 0:T], ones, acc[:, T:2 * T], start=False, stop=True).then_inc(ss_ready, 1)

        def ffn(f):
            st, e = stages[f"up{f}"], reads[f"up{f}"]

            def body(i, wait_x=None):
                for j in range(2):
                    products(*at(st, i, j), "k8", xg_hi, xg_lo, st["fill"] + j + 2 * i, j, wait_x=wait_x)
                    if wait_x and j == 0 and norms[f"up{f}"] != norms.get(before.get(f"up{f}")):
                        sum_squares(e)

            body(0, (xg_ready, g_before[e]))
            with pe.Fori(1, FPAIRS) as i:
                body(i)
            st = stages[f"down{f}"]
            with pe.Fori(0, NPAIR // 2) as i:
                for m in range(2):
                    for j in range(2):
                        pe.wait_ge(hT_ready, FPAIRS * f + (FC // 2 * (j + 1) + 1) // 2 + 1)
                        products(*at(st, 2 * i + m, j), "k11", hT_hi, hT_lo, st["fill"] + m + 2 * i, m,
                                 first=j == 0, last=j == 1, chunk0=FC // 2 * j)

        def out_slot(name, m, oT, o_base, mid):
            st = stages[name]
            n, par, banks = st["base"] + m, m % 2, OUT_BANKS[name]

            def chunk(k, c):
                out, w = ps[:, banks[c // 2], T * (c % 2):T * (c % 2 + 1)], slice(D * (k % 2) + P * c, D * (k % 2) + P * (c + 1))
                nc.tensor.matmul(out, whi[:, par, w], oT[0][:, k, :], start=k == 0 and c % 2 == 0, stop=False)
                nc.tensor.matmul(out, whi[:, par, w], oT[1][:, k, :], start=False, stop=False)
                return nc.tensor.matmul(out, wlo[:, par, w], oT[0][:, k, :], start=False, stop=k == KC - 1 and c % 2 == 1)

            if m == 0:
                pe.wait_ge(evac_done, st["fill"] + 2)
            for half in range(2):
                k = 2 * m + half
                pe.wait_ge(lo_done, 2 * n + half + 5)
                pe.wait_ge(o_ready, o_base + k + 1)
                if m < NPAIR - 1:
                    for c in range(KC):
                        mm = chunk(k, c)
                    if half == 0:
                        mid()
            if m == NPAIR - 1:
                mid()
                for c in range(KC):
                    chunk(2 * m, c)
                    mm = chunk(2 * m + 1, c)
                    if c % 2 and c < KC - 1:
                        mm.then_inc(out_ready, 1)
            mm.then_inc(slot_done, 1)

        def hgrn():
            st, e = stages["hgrn"], reads["hgrn"]

            def early(t):
                if t % 3 == 0 and 0 < t <= HG_QFI:
                    u = t // 3 - 1
                    pe.wait_ge(evac_done, st["fill"] + t - 1 + 3)
                    if u:
                        pe.wait_ge(hg_vt, u)
                    else:
                        pe.wait_ge(aux_ready, 1)
                    for c in range(2):
                        for tt in range(T // P):
                            tr = nc.tensor.transpose(ps[:, HG_VBANK, 2 * P * tt + P * c:2 * P * tt + P * (c + 1)],
                                                     hg_raw[1][:, T * c + P * tt:T * c + P * (tt + 1)], ident)
                    tr.then_inc(hg_vtr, 1)

            def late(t):
                for hd in hg_heads(t, 5):
                    pe.wait_ge(hg_os2, hd + 1)
                    nc.tensor.matmul(ps[:, HG_OUT, T:2 * T], ones, hg_osq[:, :], start=True, stop=True).then_inc(hg_oss, 1)
                for hd in hg_heads(t, 4):
                    par, col = hd // 2 % 2, slice(P * (hd % 2), P * (hd % 2 + 1))
                    pe.wait_ge(hg_Pr, hd + 1)
                    pe.wait_ge(hg_Pcr, hd + 1)
                    pe.wait_ge(hg_vt, hd // 2 + 1)
                    if hd:
                        pe.wait_ge(hg_oln, hd)
                    o = ps[:, HG_OUT, 0:T]
                    nc.tensor.matmul(o[:, 0:P], hg_v[:, par, 0, col], hg_P[:, 0:P], start=True, stop=True)
                    nc.tensor.matmul(o[:, P:T], hg_v[:, par, 1, col], hg_P[:, P:T], start=True, stop=False)
                    nc.tensor.matmul(o[:, P:T], hg_v[:, par, 0, col], hg_Pc[:, :], start=False, stop=True).then_inc(hg_o, 1)
                for hd in hg_heads(t, 3):
                    par, first = hd // 2 % 2, T * (hd % 2)
                    pe.wait_ge(hg_qd, hd + 1)
                    pe.wait_ge(hg_kd, hd + 1)
                    if hd:
                        pe.wait_ge(hg_sm, LEVELS * hd)
                        pe.wait_ge(hg_Pcr, hd)
                    for half in range(2):
                        tok = slice(P * half, P * (half + 1))
                        for level in range(LEVELS - 1):
                            at0 = P * level + P // 2 * half
                            nc.tensor.matmul(hg_all[:, at0:at0 + P // 2], hg_E[:, hd % 2, level, tok], hg_half(hg_E[:, hd % 2, level, tok], level, 1),
                                             start=True, stop=True)
                        own = slice(first + P * half, first + P * (half + 1))
                        nc.tensor.matmul(hg_all[:, HG_OWN + P * half:HG_OWN + P * (half + 1)], hg_k[:, par, own], hg_q[:, par, own],
                                         start=True, stop=True)
                    nc.tensor.matmul(hg_all[:, HG_CROSS:HG_CROSS + P], hg_E[:, hd % 2, LEVELS - 1, 0:P], hg_E[:, hd % 2, LEVELS - 1, P:T],
                                     start=True, stop=True).then_inc(hg_S, 1)

            for t in range(HG_TICKS):
                n = st["base"] + t
                if t < HG_SLOTS:
                    products(n, n // 2, n % 2, "k8", xg_hi, xg_lo, st["fill"] + t, t % 2,
                             wait_x=(xg_ready, g_before[e]) if t == 0 else None, mid=lambda: early(t))
                else:
                    if t == HG_SLOTS:
                        pe.wait_ge(hg_vt, HG_UNITS)
                    out_slot("hgrn_out", t - HG_SLOTS, hg_oT, 0, lambda: None)
                if t == 0:
                    sum_squares(e)
                    pe.wait_ge(const_late, 16)
                    pe.wait_ge(late_arrived, 16 * LATE_LOADS)
                    late_rows = GAIN_ROWS - FIRST_ROWS
                    nc.tensor.transpose(ps[:, HG_VBANK, 0:late_rows], rows_late[0:late_rows, :], ident[0:late_rows, 0:late_rows])
                    nc.tensor.transpose(ps[:, HG_VBANK, P:P + AUX], aux_in[0:AUX, :], ident[0:AUX, 0:AUX]).then_inc(late_turned, 1)
                    pe.wait_ge(bias_masked, 2)
                    for g in range(GROUPS):
                        mm = nc.tensor.matmul(ps[:, HG_SCORES + g, 0:ROW], rbx8[:, P * g:P * (g + 1)], onehot[:, ROW * g:ROW * (g + 1)],
                                              start=True, stop=True)
                    mm.then_inc(bias_made, 1)
                late(t)


        def dil():
            st, e, ek = stages["dil"], reads["dil"], reads["dil"] - 1

            def steps(point):
                slot = dl_projected(point)
                if slot is not None and not dl_slot(slot)[2]:
                    n = dl_qk_number(slot)
                    pe.wait_ge(dl_sqd, n + 1)
                    if n:
                        pe.wait_ge(dl_ln, n)
                    nc.tensor.matmul(ps[:, BANK_SUM, :], const("blk64"), dl_sq[:, :], start=True, stop=True).then_inc(dl_ss, 1)
                elif slot is not None:
                    n = dl_v_number(slot)
                    pe.wait_ge(evac_done, st["fill"] + slot + 3)
                    if n:
                        pe.wait_ge(dl_vt, n)
                    for c in range(2):
                        for tt in range(T // P):
                            tr = nc.tensor.transpose(ps[:, DL_VBANK, 2 * P * tt + P * c:2 * P * tt + P * (c + 1)],
                                                     dl_t[:, slot % 2, T * c + P * tt:T * c + P * (tt + 1)], ident)
                    tr.then_inc(dl_vtr, 1)
                for two in dl_due(point, DL_PV):
                    u, c = divmod(two, 2)
                    pe.wait_ge(dl_PTd, 2 * two + 2)
                    pe.wait_ge(dl_vt, GROUPS * (u + 1))
                    if c == 0 and u:
                        pe.wait_ge(o_ready, 8 + 2 * u)
                    for g in range(GROUPS):
                        for tile in range(2):
                            for odd in range(2):
                                v = dl_v[:, u % 2, g, tile, HD * (2 * c + odd):HD * (2 * c + odd + 1)]
                                at0, n = (T * g, T) if tile == 0 else (GROUPS * T + P * g, P)
                                mm = nc.tensor.matmul(ps[HD * odd:HD * (odd + 1), DL_OUT, T * (c + 1) - n:T * (c + 1)], v,
                                                      dl_PT[:, odd, at0:at0 + n], start=g == 0 and tile == 0 and c == 0,
                                                      stop=g == GROUPS - 1 and tile == 1, tile_position=(0, HD * odd), skip_group_check=True)
                    mm.then_inc(dl_pv, 1)
                for hd in dl_due(point, DL_TURN):
                    u = hd // 4
                    pe.wait_ge(dl_sc0, hd + 1)
                    pe.wait_ge(dl_sc1, hd + 1)
                    pe.wait_ge(dl_biased, 2 * min(hd + 2, 4 * u + 4))
                    if hd:
                        pe.wait_ge(dl_PTd, hd)
                    S = dl_S[:, hd % 2, :]
                    for g in range(GROUPS):
                        for out, own in ((T * g, dl_blocks(S, P)[:, g, :]), (T * g + P, dl_blocks(S, T)[:, g, 0:P]),
                                         (GROUPS * T + P * g, dl_blocks(S, T)[:, g, P:T])):
                            tr = nc.tensor.transpose(dl_ps[:, out:out + P], own, ident)
                    tr.then_inc(dl_turned, 1)
                for hd in dl_due(point, DL_SCORES):
                    u, a = divmod(hd, 4)
                    pe.wait_ge(dl_qkd, 2 * GROUPS * (u + 1))
                    if hd:
                        pe.wait_ge(dl_biased, 2 * hd)
                    if hd > 1 or a > 1:
                        pe.wait_ge(dl_PTd, hd if a == 0 else hd - 1)
                    first = T * (a // 2)
                    for tile, keys in ((1, T), (0, P)):
                        for g in range(GROUPS):
                            mm = nc.tensor.matmul(dl_blocks(dl_ps, keys)[:, g, :], dl_q[:, g, a % 2, first + P * tile:first + P * (tile + 1)],
                                                  dl_k[:, u % 2, g, first:first + keys], start=True, stop=True)
                    mm.then_inc(dl_scored, 1)

            pe.wait_ge(xk_ready, k_before[ek] + KC)
            for t in range(DL_TICKS):
                if t < DL_SLOTS:
                    n = st["base"] + t
                    u, j, values = dl_slot(t)
                    hi, lo = operand["k" if values or j % 2 else "g"]
                    products(n, n // 2, n % 2, "k8", hi, lo, st["fill"] + t, t % 2,
                             wait_x=(xg_ready, g_before[e]) if t == 0 else None, mid=lambda: steps(2 * t))
                    if t == 0:
                        sum_squares(e)
                else:
                    if t == DL_SLOTS:
                        pe.wait_ge(dl_ln, 2 * GROUPS * DL_UNITS)
                        pe.wait_ge(dl_vt, GROUPS * DL_UNITS)
                    out_slot("dil_out", t - DL_SLOTS, dl_oT, 8, lambda: steps(2 * t))
                steps(2 * t + 1)


        def stick():
            st, e = stages["stick"], reads["stick"]

            def early(t):
                for u in sk_sums_at(t):
                    pe.wait_ge(sk_spd, u + 1)
                    for odd in range(2):
                        nc.tensor.matmul(sk_second(sk_all, odd), const("neg_suffix"), sk_second(sk_sp, odd),
                                         start=False, stop=True, skip_group_check=True)
                        nc.tensor.matmul(sk_first(sk_all, odd), const("neg_suffix"), sk_first(sk_sp, odd),
                                         start=False, stop=False, skip_group_check=True)
                        mm = nc.tensor.matmul(sk_first(sk_all, odd)[:, :, P:T], const("neg_ones"), sk_second(sk_sp, odd),
                                              start=False, stop=True, skip_group_check=True)
                    mm.then_inc(sk_sum, 1)
                for u in sk_values_at(t):
                    pe.wait_ge(evac_done, st["fill"] + SK_QK + u + 3)
                    if u:
                        pe.wait_ge(sk_vt, u)
                    for c in range(2):
                        for tt in range(T // P):
                            tr = nc.tensor.transpose(ps[:, SK_VBANK, 2 * P * tt + P * c:2 * P * tt + P * (c + 1)],
                                                     sk_t[:, u % 2, T * c + P * tt:T * c + P * (tt + 1)], ident)
                    tr.then_inc(sk_vtr, 1)

            def late(t):
                for u in sk_scores_at(t):
                    pe.wait_ge(evac_done, st["fill"] + 2 * u + 1 + 3)
                    if u:
                        pe.wait_ge(sk_wr, u)
                    mask = const("neg_mask").unsqueeze(1).broadcast_to([P, 2, P])
                    for c in range(2):
                        for odd in range(2):
                            q, first = sk_q[:, u % 2, odd, T * c:T * (c + 1)], T * c
                            nc.tensor.matmul(sk_first(sk_all, odd)[:, c, :], sk_k[:, u % 2, first:first + P], q,
                                             start=c == 0, stop=False, skip_group_check=True)
                            nc.tensor.matmul(sk_second(sk_all, odd)[:, c, :], sk_k[:, u % 2, first + P:first + T], q[:, P:T],
                                             start=c == 0, stop=False, skip_group_check=True)
                    for odd in range(2):
                        for out in (sk_first(sk_all, odd)[:, :, 0:P], sk_second(sk_all, odd)):
                            mm = nc.tensor.matmul(out, ident, mask, start=False, stop=True, skip_group_check=True)
                    mm.then_inc(sk_z, 1)
                for u in sk_values_at(t):
                    pe.wait_ge(sk_wr, u + 1)
                    pe.wait_ge(sk_vt, u + 1)
                    if u:
                        pe.wait_ge(o_ready, 16 + 2 * u)
                    for c in range(2):
                        for tile, weights in enumerate((sk_first, sk_second)):
                            for odd in range(2):
                                w = weights(sk_w[:, u, :], odd)[:, c, :]
                                mm = nc.tensor.matmul(ps[HD * odd:HD * (odd + 1), SK_OUT, T * c + P * tile:T * (c + 1)],
                                                      sk_v[:, u % 2, tile, HD * (2 * c + odd):HD * (2 * c + odd + 1)], w,
                                                      start=c == 0 and tile == 0, stop=tile == 1, tile_position=(0, HD * odd),
                                                      skip_group_check=True)
                    mm.then_inc(sk_pv, 1)

            for t in range(SK_TICKS):
                n = st["base"] + t
                if t < SK_SLOTS:
                    products(n, n // 2, n % 2, "k8", xg_hi, xg_lo, st["fill"] + t, t % 2,
                             wait_x=(xg_ready, g_before[e]) if t == 0 else None, mid=lambda: early(t))
                else:
                    if t == SK_SLOTS:
                        pe.wait_ge(sk_wr, SK_UNITS)
                    out_slot("stick_out", t - SK_SLOTS, sk_oT, 16, lambda: early(t))
                if t == 0:
                    sum_squares(e)
                late(t)


        def swa_kv():
            st, e = stages["swa_kv"], reads["swa_kv"]
            for j in range(2):
                products(st["base"] + j, st["base"] // 2, j, "k8", xk_hi, xk_lo, st["fill"] + j, j,
                         wait_x=(xk_ready, k_before[e]) if j == 0 else None)
                if j == 0:
                    sum_squares(e)
            pe.wait_ge(evac_done, st["fill"] + 3)
            nc.tensor.matmul(ps[:, KV_ROT, :], const("rot"), kv_t[:, :], start=True, stop=True).then_inc(kv_rot, 1)
            pe.wait_ge(evac_done, st["fill"] + 1 + 3)
            for c in range(2):
                for tt in range(T // P):
                    tr = nc.tensor.transpose(ps[:, KV_VBANK, 2 * P * tt + P * c:2 * P * tt + P * (c + 1)],
                                             kv_v[:, T * c + P * tt:T * c + P * (tt + 1)], ident)
            tr.then_inc(kv_vtr, 1)
            pe.wait_ge(kv_sum, 1)
            for u in range(KV_HEADS):
                dup = nc.tensor.matmul(ps[:, KV_DUP + u // 2, T * (u % 2):T * (u % 2 + 1)], const(f"dup{u % 2}"),
                                       kv_c[:, T * (u // 2):T * (u // 2 + 1)], start=True, stop=True)
            dup.then_inc(kv_dup, 1)


        def swa():
            st, e = stages["swa"], reads["swa"]

            def early(t):
                for u in sw_at(t, 1):
                    pe.wait_ge(evac_done, st["fill"] + u + 3)
                    if u:
                        pe.wait_ge(sw_sin, u)
                    if u > 2:
                        pe.wait_ge(o_ready, 24 + 2 * (u - 2))
                    nc.tensor.matmul(ps[:, SW_OUT, :], const("rot"), sw_t[:, u % 2, :], start=True, stop=True).then_inc(sw_rot, 1)
                for u in sw_at(t, 3):
                    pe.wait_ge(sw_sc0, u + 1)
                    pe.wait_ge(sw_sc1, u + 1)
                    if u + 1 < SW_UNITS:
                        pe.wait_ge(sw_masked, 8 * (u + 2))
                    for a in range(4):
                        for tile in range(2):
                            nc.tensor.transpose(sw_keys0(sw_turn, a)[:, P * tile:P * (tile + 1)], sw_biased(u, a, tile)[:, 0:P], ident)
                        tr = nc.tensor.transpose(sw_keys1(sw_turn, a), sw_biased(u, a, 1)[:, P:T], ident)
                    tr.then_inc(sw_turned, 1)

            def late(t):
                for u in sw_at(t, 3):
                    pe.wait_ge(sw_PTd, u + 1)
                    if u:
                        pe.wait_ge(o_ready, 24 + 2 * u)
                    pe.wait_ge(sw_sin, min(u + 3, SW_UNITS))
                    for c in range(2):
                        for tile, probs in enumerate((sw_keys0, sw_keys1)):
                            for odd in range(2):
                                mm = nc.tensor.matmul(ps[HD * odd:HD * (odd + 1), SW_OUT, T * c + P * tile:T * (c + 1)],
                                                      v2[:, tile, HD * u:HD * (u + 1)], probs(sw_PT, 2 * c + odd),
                                                      start=c == 0 and tile == 0, stop=tile == 1, tile_position=(0, HD * odd),
                                                      skip_group_check=True)
                    mm.then_inc(sw_pv, 1)
                for u in sw_at(t, 1):
                    pe.wait_ge(sw_qr, u + 1)
                    if u > 1:
                        pe.wait_ge(sw_PTd, u - 1)
                    if u:
                        pe.wait_ge(sw_masked, 8 * u)
                    for a in range(4):
                        for tile, keys in ((1, T), (0, P)):
                            first = T * (a // 2) + P * tile
                            mm = nc.tensor.matmul(sw_scores(a, tile), sw_q[:, u % 2, a % 2, first:first + P], kdup[:, u, 0:keys],
                                                  start=True, stop=True)
                    mm.then_inc(sw_scored, 1)

            pe.wait_ge(kv_dupd, 1)
            pe.wait_ge(kv_vt, 1)
            for t in range(SW_TICKS):
                if t < SW_UNITS:
                    n = st["base"] + t
                    products(n, n // 2, n % 2, "k8", xg_hi, xg_lo, st["fill"] + t, t % 2,
                             wait_x=(xg_ready, g_before[e]) if t == 0 else None, mid=lambda: early(t))
                    if t == 0:
                        sum_squares(e)
                else:
                    out_slot("swa_out", t - SW_UNITS, sw_oT, 24, lambda: early(t))
                late(t)

        pe.wait_ge(const_in, 16)
        pe.wait_ge(rows_arrived, 16)
        nc.tensor.transpose(ps[:, BANK_SUM, 0:FIRST_ROWS], rows_in[0:FIRST_ROWS, :], ident[0:FIRST_ROWS, 0:FIRST_ROWS]).then_inc(rows_turned, 1)
        pe.wait_ge(x_arrived, 16)
        for m in range(NPAIR):
            pe.wait_ge(evac_done, m + 1)
            for c in range(2):
                for t in range(T // P):
                    tr = nc.tensor.transpose(ps[:, m % 2, T * c + P * t:T * c + P * (t + 1)],
                                             x_in[:, t, P * (2 * m + c):P * (2 * m + c + 1)], ident)
            tr.then_inc(x_turned, 1)
        pe.wait_ge(gains_ready, 1)
        for layer in layers:
            if layer.startswith("ffn"):
                ffn(int(layer[3:]))
            if layer == "hgrn":
                hgrn()
            if layer == "dil":
                dil()
            if layer == "stick":
                stick()
            if layer == "swa_kv":
                swa_kv()
            if layer == "swa":
                swa()
        sum_squares(LAST)
        for t in range(T // P):
            for c in range(KC):
                pe.wait_ge(final_y, c + 1)
                tr = nc.tensor.transpose(ps[:, 4 + 2 * t + c // 4, P * (c % 4):P * (c % 4 + 1)],
                                         fin[:, c, P * t:P * (t + 1)], ident)
            tr.then_inc(final_turned, 1)

    @block.scalar
    def _(act):
        own = CONST_AT["blk64"][0]
        act.dma_start(cst[:, 0:own], io["consts"][:, 0:own]).then_inc(const_in, 16)
        rows = lambda name, n: bass.AP(io[name].tensor, 0, [[P, n], [1, P]])
        act.dma_start(rows_in[0:FIRST_ROWS, :], rows("norm_gain", FIRST_ROWS)).then_inc(rows_arrived, 16)
        nc.scalar.preload_act_table_set("natural_log_exp_and_others")

        def split_high(n, n2, par, kind, halves=(0, 1)):
            if kind is None:
                return
            act.wait_ge(slot_done, n + 1)
            for half in halves:
                off, size, _ = HALVES[kind][half]
                act.wait_ge(w_arrived[2 * par + half], 16 * n2 + 16)
                nc.scalar.activation(whi[:, par, off:off + size], raw[:, 2 * par + half, :size], ACT.Copy).then_inc(hi_done, 1)

        def high_x(e, m, fill):
            act.wait_ge(evac_done, fill + 3)
            for which, col in updates[e][1]:
                for c in range(2 * m, 2 * m + 2):
                    nc.scalar.activation(operand[which][0][:, c, :], x[:, c, :], ACT.Copy,
                                         scale=gains[:, col + c:col + c + 1]).then_inc(xhi_done, 1)

        def norm(e):
            act.wait_ge(ms_ready, e + 1)
            nc.scalar.activation(ms_ln[:, :], ms[:, :], ACT.Ln).then_inc(ms_ln_done, 1)
            act.wait_ge(ms_ln_done, e + 1)
            nc.scalar.activation(r0[:, :], ms_ln[:, :], ACT.Exp, scale=-0.5).then_inc(r0_ready, 1)

        def stage_norm(name):
            if norms[name] != norms.get(before.get(name)):
                norm(norms[name])

        def ffn(f):
            stage_norm(f"up{f}")
            st = stages[f"up{f}"]

            def body(i):
                p = FPAIRS * f + i
                split_high(*ahead_of(st, i, 0), (0,))
                act.wait_ge(evac_done, st["fill"] + 2 * i + 3)
                nc.scalar.activation(gate_e[:, :], gate[:, :], ACT.Exp, scale=-1.0).then_inc(gate_exp, 1)
                split_high(*ahead_of(st, i, 0), (1,))
                act.wait_ge(gate_den, p + 1)
                nc.scalar.activation(gate_e[:, :], gate_e[:, :], ACT.Ln).then_inc(gate_ln, 1)
                act.wait_ge(gate_ln, p + 1)
                act.wait_ge(gs_done, p + 1)
                nc.scalar.activation(gate_s[:, :], gate_e[:, :], ACT.Exp, scale=-1.0).then_inc(sig_ready, 1)
                split_high(*ahead_of(st, i, 1))
                act.wait_ge(evac_done, st["fill"] + 2 * i + 4)
                nc.scalar.activation(hT_hi_flat[:, bass.ds(2 * T * i, 2 * T)], h[:, :], ACT.Copy).then_inc(hhi_done, 1)

            all_but_last(act, FPAIRS, body)
            st = stages[f"down{f}"]
            for m in range(NPAIR):
                split_high(*ahead_of(st, m, 0))
                high_x(update_of[f"down{f}"], m, st["fill"] + m)
                split_high(*ahead_of(st, m, 1))

        def out_slot(name, m):
            st = stages[name]
            for pair_of in range(NPAIR) if m == NPAIR - 1 else ():
                high_x(update_of[name], pair_of, st["fill"] + pair_of)
            split_high(*ahead_of(st, m // 2, m % 2))

        def hgrn():
            st = stages["hgrn"]

            def sigmoid_exp(n, out, source, scale):
                nc.scalar.activation(out, source, ACT.Exp, scale=scale).then_inc(hg_e, 1)

            def sigmoid_end(n, tile):
                act.wait_ge(hg_d, n)
                nc.scalar.activation(tile, tile, ACT.Ln).then_inc(hg_l, 1)
                act.wait_ge(hg_l, n)
                nc.scalar.activation(tile, tile, ACT.Exp, scale=-1.0).then_inc(hg_s, 1)

            def late(t):
                for hd in hg_heads(t, 1):
                    act.wait_ge(hg_dif, hd + 1)
                    nc.scalar.activation(hg_E[:, hd % 2, :, :], hg_E[:, hd % 2, :, :], ACT.Exp).then_inc(hg_dec, 1)
                for hd in hg_heads(t, 5):
                    act.wait_ge(hg_oss, hd + 1)
                    if hd:
                        act.wait_ge(hg_on, hd)
                    nc.scalar.activation(hg_rms[:, :], ps[:, HG_OUT, T:2 * T], ACT.Ln, scale=1.0 / P, bias=eps[:, :]).then_inc(hg_oln, 1)
                    act.wait_ge(hg_oln, hd + 1)
                    nc.scalar.activation(hg_rms[:, :], hg_rms[:, :], ACT.Exp, scale=-0.5).then_inc(hg_or, 1)
                for u in hg_units(t, 1):
                    act.wait_ge(hg_og, u + 1)
                    nc.scalar.activation(hg_oT[0][:, 2 * u:2 * u + 2, :], hg_out[:, 2 * u:2 * u + 2, :], ACT.Copy).then_inc(hg_ohi, 1)
                for hd in hg_heads(t, 4):
                    act.wait_ge(hg_o, hd + 1)
                    nc.scalar.activation(hg_out[:, hd, :], ps[:, HG_OUT, 0:T], ACT.Copy).then_inc(hg_oc, 1)

            def store_bias(g, quarter):
                rows = REPEAT // 2
                act.dma_start(bass.AP(bias_dram.tensor, HEADS * P * ROW * g + rows * ROW * quarter, [[4 * rows * ROW, P], [ROW, rows], [1, ROW]]),
                              bias_rows[:, g:g + 1, :].broadcast_to([P, rows, ROW])).then_inc(bias_stored, 16)

            at_mask = CONST_AT["hg_mask"][0]
            act.dma_start(hg_mask[:, :, :].rearrange("p l t -> p (l t)"), io["consts"][:, at_mask:at_mask + (LEVELS - 1) * P]).then_inc(hg_mask_in, 16)
            stage_norm("hgrn")
            for t in range(HG_TICKS):
                if t == 1:
                    act.wait_ge(lb_steps, 2)
                    nc.scalar.activation(lbt[:, 0:2, :], lbt[:, 0:2, :], ACT.Exp).then_inc(lb_exp, 1)
                    act.wait_ge(bias_copied, 1)
                if 0 < t <= BIAS_STORES:
                    store_bias((t - 1) // 4, (t - 1) % 4)
                if t < HG_SLOTS:
                    u, j = hg_slot(t)
                    n = st["base"] + t
                    split_high(n + 2, (n + 2) // 2, n % 2, kinds[n + 2])
                    if t % 3 == 0 and 0 < t <= HG_QFI:
                        v = t // 3 - 1
                        act.wait_ge(hg_vtr, v + 1)
                        if v > 1:
                            act.wait_ge(hg_o, 2 * v - 2)
                        nc.scalar.activation(hg_v[:, v % 2, :, :], ps[:, HG_VBANK, :].rearrange("p (a b) -> p a b", a=2), ACT.Copy).then_inc(hg_vt, 1)
                    if j != 2:
                        act.wait_ge(evac_done, st["fill"] + t + 3)
                    if j == 0:
                        if u:
                            act.wait_ge(hg_qs, u)
                        sigmoid_exp(3 * u + 1, hg_exp[0][:, :], hg_raw[0][:, :], -1.0)
                    if j == 1:
                        if u:
                            act.wait_ge(hg_cum, 2 * u)
                            act.wait_ge(hg_kk, 2 * u)
                        sigmoid_exp(3 * u + 2, hg_exp[1][:, :], hg_raw[1][:, :], -1.0)
                        sigmoid_exp(3 * u + 3, hg_exp[2][:, :], hg_raw[1][:, :], 1.0)
                    if j == 3:
                        act.wait_ge(hg_qs, HG_UNITS)
                        if u:
                            act.wait_ge(hg_gs, u)
                        sigmoid_exp(HG_QFI + u + 1, hg_exp[0][:, :], hg_raw[u % 2][:, :], -1.0)
                    late(t)
                    if j == 0:
                        sigmoid_end(3 * u + 1, hg_exp[0][:, :])
                    if j == 1:
                        sigmoid_end(3 * u + 2, hg_exp[1][:, :])
                        sigmoid_end(3 * u + 3, hg_exp[2][:, :])
                    if j == 2:
                        act.wait_ge(hg_f, 2 * u + 2)
                        nc.scalar.activation(hg_exp[1][:, :], hg_exp[1][:, :], ACT.Ln).then_inc(hg_lf, 1)
                    if j == 3:
                        sigmoid_end(HG_QFI + u + 1, hg_exp[0][:, :])
                elif t < HG_TICKS - 1:
                    out_slot("hgrn_out", t - HG_SLOTS)
                    late(t)
                else:
                    late(t)
                    out_slot("hgrn_out", t - HG_SLOTS)
            act.wait_ge(bias_stored, 16 * BIAS_STORES)


        def dil():
            st = stages["dil"]

            def load_bias(hd):
                src = bass.AP(bias_dram.tensor, hd * P * ROW + P - 1, [[ROW - 1, P], [HEADS * P * ROW, GROUPS], [1, T]])
                act.dma_start(dl_bias[:, hd % 2, :, :], src).then_inc((dl_bias_in0, dl_bias_in1)[hd % 2], 16)

            def steps(point):
                slot = dl_projected(point)
                if slot is not None and not dl_slot(slot)[2]:
                    n = dl_qk_number(slot)
                    act.wait_ge(dl_ss, n + 1)
                    if n:
                        act.wait_ge(dl_qkd, n)
                    nc.scalar.activation(dl_rr[:, :], ps[:, BANK_SUM, :], ACT.Ln, scale=1.0 / HD, bias=eps[:, :]).then_inc(dl_ln, 1)
                    act.wait_ge(dl_ln, n + 1)
                    nc.scalar.activation(dl_rr[:, :], dl_rr[:, :], ACT.Exp, scale=-0.5).then_inc(dl_rrd, 1)
                elif slot is not None:
                    n, u = dl_v_number(slot), dl_slot(slot)[0]
                    act.wait_ge(dl_vtr, n + 1)
                    if u > 1:
                        act.wait_ge(dl_pv, 2 * (u - 1))
                    nc.scalar.activation(dl_v[:, u % 2, n % GROUPS, :, :], ps[:, DL_VBANK, :].rearrange("p (a b) -> p a b", a=2),
                                         ACT.Copy).then_inc(dl_vt, 1)
                for two in dl_due(point, DL_PV):
                    u, c = divmod(two, 2)
                    if c == 1:
                        act.wait_ge(dl_pv, two + 1)
                        nc.scalar.activation(flat(dl_oT[0][:, 2 * u:2 * u + 2, :]), ps[:, DL_OUT, :], ACT.Copy).then_inc(dl_ohi, 1)
                for hd in dl_due(point, DL_TURN):
                    act.wait_ge(dl_turned, hd + 1)
                    if hd > 1:
                        act.wait_ge(dl_pv, hd // 2)
                    nc.scalar.activation(dl_PT[:, hd % 2, :], dl_ps, ACT.Copy).then_inc(dl_PTd, 1)
                for hd in dl_due(point, DL_SCORES):
                    act.wait_ge(dl_neg, hd + 1)
                    S = dl_S[:, hd % 2, :]
                    for tile, keys in ((1, T), (0, P)):
                        ex = nc.scalar.activation(dl_blocks(S, keys), dl_blocks(S, keys), ACT.Exp, bias=dl_nmax[:, hd % 2, tile:tile + 1],
                                                  accum_out=dl_sum[:, hd % 2, tile:tile + 1])
                    ex.then_inc(dl_exp, 1)
                    if hd + 2 < HEADS:
                        load_bias(hd + 2)

            act.wait_ge(bias_stored, 16 * BIAS_STORES)
            for hd in range(2):
                load_bias(hd)
            stage_norm("dil")
            for t in range(DL_TICKS):
                steps(2 * t)
                if t < DL_SLOTS:
                    n = st["base"] + t
                    split_high(n + 2, (n + 2) // 2, n % 2, kinds[n + 2])
                else:
                    out_slot("dil_out", t - DL_SLOTS)
                steps(2 * t + 1)


        def stick():
            st = stages["stick"]

            def early(t):
                for u in sk_sums_at(t):
                    act.wait_ge(sk_sum, u + 1)
                    nc.scalar.activation(sk_w[:, u, :], sk_all, ACT.Exp).then_inc(sk_wr, 1)
                for u in sk_values_at(t):
                    act.wait_ge(sk_vtr, u + 1)
                    if u > 1:
                        act.wait_ge(sk_pv, u - 1)
                    nc.scalar.activation(sk_v[:, u % 2, :, :], ps[:, SK_VBANK, :].rearrange("p (a b) -> p a b", a=2), ACT.Copy).then_inc(sk_vt, 1)

            def late(t):
                for u in sk_scores_at(t):
                    act.wait_ge(sk_z, u + 1)
                    if u:
                        act.wait_ge(sk_spd, u)
                    nc.scalar.activation(sk_e[:, :], sk_all, ACT.Abs).then_inc(sk_abs, 1)
                    act.wait_ge(sk_abs, u + 1)
                    nc.scalar.activation(sk_e[:, :], sk_e[:, :], ACT.Exp, scale=-1.0).then_inc(sk_ex, 1)
                    act.wait_ge(sk_ex, u + 1)
                    nc.scalar.activation(sk_e[:, :], sk_e[:, :], ACT.Ln, bias=1.0).then_inc(sk_ln, 1)
                for u in sk_values_at(t):
                    act.wait_ge(sk_pv, u + 1)
                    nc.scalar.activation(flat(sk_oT[0][:, 2 * u:2 * u + 2, :]), ps[:, SK_OUT, :], ACT.Copy).then_inc(sk_ohi, 1)

            stage_norm("stick")
            for t in range(SK_TICKS):
                n = st["base"] + t
                early(t)
                if t < SK_SLOTS:
                    split_high(n + 2, (n + 2) // 2, n % 2, kinds[n + 2])
                else:
                    out_slot("stick_out", t - SK_SLOTS)
                late(t)


        def swa_kv():
            st = stages["swa_kv"]
            cos = CONST_AT["cos"][0]
            act.dma_start(rope[:, :, :].rearrange("p a t -> p (a t)"), io["consts"][:, cos:cos + 2 * T]).then_inc(kv_rope_in, 16)
            mask = CONST_AT["swa_mask"][0]
            act.dma_start(swa_mask[:, :], io["consts"][:, mask:mask + T]).then_inc(kv_rope_in, 16)
            stage_norm("swa_kv")
            for j in range(2):
                split_high(*ahead_of(st, 0, j))
            act.wait_ge(kv_vtr, 1)
            nc.scalar.activation(v2[:, :, :], ps[:, KV_VBANK, :].rearrange("p (a b) -> p a b", a=2), ACT.Copy).then_inc(kv_vt, 1)
            act.wait_ge(kv_dup, 1)
            nc.scalar.activation(flat(kdup[:, :, :]), ps[:, KV_DUP:KV_DUP + 2, :].rearrange("p b n -> p (b n)"), ACT.Copy).then_inc(kv_dupd, 1)


        def swa():
            st = stages["swa"]

            def early(t):
                for u in sw_at(t, 3):
                    act.wait_ge(sw_turned, u + 1)
                    if u:
                        act.wait_ge(sw_pv, u)
                    nc.scalar.activation(sw_PT[:, :], sw_turn, ACT.Copy).then_inc(sw_PTd, 1)

            def late(t):
                for u in sw_at(t, 3):
                    act.wait_ge(sw_pv, u + 1)
                    nc.scalar.activation(flat(sw_oT[0][:, 2 * u:2 * u + 2, :]), ps[:, SW_OUT, :], ACT.Copy).then_inc(sw_ohi, 1)
                for u in sw_at(t, 1):
                    act.wait_ge(sw_neg, u + 1)
                    for a in range(4):
                        for tile in range(2):
                            S = sw_biased(u, a, tile)
                            nc.scalar.activation(S, S, ACT.Exp, bias=sw_nmax[:, u % 2, tile, a:a + 1],
                                                 accum_out=sw_sum[:, u % 2, tile, a:a + 1]).then_inc(sw_exp, 1)
                    act.wait_ge(sw_dm, u + 1)
                    nc.scalar.activation(sw_sink[:, u % 2, :, :], sw_sink[:, u % 2, :, :], ACT.Exp).then_inc(sw_snk, 1)

            stage_norm("swa")
            for t in range(SW_TICKS):
                early(t)
                if t < SW_UNITS:
                    split_high(*ahead_of(st, t // 2, t % 2))
                else:
                    out_slot("swa_out", t - SW_UNITS)
                late(t)

        for n in range(2):
            split_high(*slot0(n))
        act.wait_ge(gains_ready, 1)
        for m in range(NPAIR):
            high_x(0, m, m)
        act.dma_start(cst[:, own:], io["consts"][:, own:CONSTS]).then_inc(const_late, 16)
        for name in GAIN:
            if name != "norm_gain":
                n = int(np.prod(io[name].shape)) // P
                first = GAIN[name] - FIRST_ROWS
                act.dma_start(rows_late[first:first + n, :], rows(name, n)).then_inc(late_arrived, 16)
        act.dma_start(aux_in[0:2 * A_HEADS, :], rows("a_lb_logits", 2 * A_HEADS)).then_inc(late_arrived, 16)
        act.dma_start(aux_in[2 * A_HEADS:2 * A_HEADS + 1, :], io["a_out_gain"]).then_inc(late_arrived, 16)
        for n, name in enumerate(("k_gain", "b_q_gain")):
            src = bass.AP(io[name].tensor, 0, [[HD, GROUPS], [0, 2], [1, HD]])
            first = 2 * A_HEADS + 1 + GROUPS * n
            act.dma_start(aux_in[first:first + GROUPS, :].rearrange("g (a d) -> g a d", a=2), src).then_inc(late_arrived, 16)
        act.dma_start(sinks[:, :], bass.AP(io["swa_sinks_2"].tensor, 0, [[0, P], [1, HEADS]])).then_inc(late_arrived, 16)
        act.dma_start(rbx[0:BUCKETS, :], io["rel_bias"]).then_inc(bias_in, 16)
        at_onehot = CONST_AT["onehot"][0]
        act.dma_start(onehot[:, :], io["consts"][0:BUCKETS + 1, at_onehot:]).then_inc(bias_in, 16)
        for layer in layers:
            if layer.startswith("ffn"):
                ffn(int(layer[3:]))
            if layer == "hgrn":
                hgrn()
            if layer == "dil":
                dil()
            if layer == "stick":
                stick()
            if layer == "swa_kv":
                swa_kv()
            if layer == "swa":
                swa()
        norm(LAST)
        for t in range(T // P):
            act.wait_ge(final_turned, t + 1)
            nc.scalar.activation(out_sb[:, t, :], ps[:, 4 + 2 * t:6 + 2 * t, :].rearrange("p b n -> p (b n)"), ACT.Copy).then_inc(final_copied, 1)

    @block.vector
    def _(dve):
        dve.sem_inc(lo_done, 4)
        dve.sem_inc(evac_done, 2)

        def split_low(n, n2, par, kind, halves=(0, 1)):
            if kind is None:
                return
            for half in halves:
                off, size, _ = HALVES[kind][half]
                dve.wait_ge(hi_done, 2 * n + half + 1)
                nc.vector.tensor_tensor(wlo[:, par, off:off + size], raw[:, 2 * par + half, :size],
                                        whi[:, par, off:off + size].bitcast(F32), ALU.subtract).then_inc(lo_done, 1)

        def update_x(e, m, source, scale):
            if e == 0:
                op = nc.vector.tensor_copy(xpair(m), source)
            else:
                op = nc.vector.scalar_tensor_tensor(xpair(m), source, scale, xpair(m), ALU.mult, ALU.add)
            op.then_inc(evac_done, 1)

        def low_x(e, m):
            uses = updates[e][1]
            for n, (which, col) in enumerate(uses):
                ready = xg_ready if which == "g" else xk_ready
                for c in range(2):
                    dve.wait_ge(xhi_done, g_before[e] + k_before[e] + 2 * (len(uses) * m + n) + c + 1)
                    hi, lo = [o[:, 2 * m + c, :] for o in operand[which]]
                    nc.vector.scalar_tensor_tensor(lo, x[:, 2 * m + c, :], gains[:, col + 2 * m + c:col + 2 * m + c + 1],
                                                   hi.bitcast(F32), ALU.mult, ALU.subtract).then_inc(ready, 1)

        def norm(e):
            dve.wait_ge(ss_ready, e + 1)
            nc.vector.tensor_scalar(ms[:, :], ps[:, BANK_SUM, 0:T], 1.0 / D, EPS, ALU.mult, ALU.add).then_inc(ms_ready, 1)
            dve.wait_ge(r0_ready, e + 1)
            nc.vector.scalar_tensor_tensor(newton[:, 0, :], r0[:, :], -0.5, r0[:, :], ALU.mult, ALU.mult).then_inc(newton_a, 1)
            dve.wait_ge(newton_a, e + 1)
            nc.vector.tensor_tensor(newton[:, 1, :], newton[:, 0, :], ms[:, :], ALU.mult).then_inc(newton_b, 1)
            dve.wait_ge(newton_b, e + 1)
            nc.vector.scalar_tensor_tensor(r[:, e % 2, :], newton[:, 1, :], 1.5, r0[:, :], ALU.add, ALU.mult).then_inc(r_ready, 1)
            dve.wait_ge(r_ready, e + 1)

        def stage_norm(name):
            if norms[name] != norms.get(before.get(name)):
                norm(norms[name])

        def scaled(out, fill, e, factor=None):
            if factor is None:
                op = nc.vector.tensor_tensor(pair(out), pair(bank_of(fill)), r_of(e), ALU.mult)
            else:
                op = nc.vector.scalar_tensor_tensor(pair(out), pair(bank_of(fill)), factor, r_of(e), ALU.mult, ALU.mult)
            op.then_inc(evac_done, 1)

        def ffn(f):
            stage_norm(f"up{f}")
            st, e = stages[f"up{f}"], reads[f"up{f}"]

            def body(i):
                p = FPAIRS * f + i
                dve.wait_ge(slot_done, at(st, i, 0)[0] + 3)
                dve.wait_ge(gs_done, p + 1)
                scaled(gate[:, :], 0, e)
                split_low(*ahead_of(st, i, 0), (0,))
                dve.wait_ge(gate_exp, p + 1)
                nc.vector.tensor_scalar(gate_e[:, :], gate_e[:, :], EXP_MAX, 1.0, ALU.min, ALU.add).then_inc(gate_den, 1)
                split_low(*ahead_of(st, i, 0), (1,))
                dve.wait_ge(slot_done, at(st, i, 1)[0] + 3)
                dve.wait_ge(gr_done, p + 1)
                dve.wait_ge(hT_ready, p + 1)
                nc.vector.tensor_tensor(h[:, :], bank_of(1), gate_r[:, :], ALU.mult).then_inc(evac_done, 1)
                split_low(*ahead_of(st, i, 1))

            all_but_last(dve, FPAIRS, body)
            st, e = stages[f"down{f}"], update_of[f"down{f}"]
            for m in range(NPAIR):
                split_low(*ahead_of(st, m, 0))
                dve.wait_ge(slot_done, at(st, m, 1)[0] + 3)
                update_x(e, m, bank_of(st["fill"] + m), 0.5)
                low_x(e, m)
                split_low(*ahead_of(st, m, 1))

        def out_slot(name, m):
            st, e = stages[name], update_of[name]
            for pair_of in range(NPAIR) if m == NPAIR - 1 else ():
                if pair_of < NPAIR - 1:
                    dve.wait_ge(out_ready, out_before(name) + pair_of + 1)
                else:
                    dve.wait_ge(slot_done, st["base"] + m + 3)
                update_x(e, pair_of, ps[:, OUT_BANKS[name][pair_of], :], 1.0)
                low_x(e, pair_of)
            split_low(*ahead_of(st, m // 2, m % 2))

        def hgrn():
            st, e = stages["hgrn"], reads["hgrn"]

            def sigmoid_one(n, tile):
                dve.wait_ge(hg_e, n)
                nc.vector.tensor_scalar(tile, tile, EXP_MAX, 1.0, ALU.min, ALU.add).then_inc(hg_d, 1)

            def late(t):
                for u in hg_units(t, 1):
                    dve.wait_ge(hg_ohi, u + 1)
                    nc.vector.tensor_tensor(hg_oT[1][:, 2 * u:2 * u + 2, :], hg_out[:, 2 * u:2 * u + 2, :],
                                            hg_oT[0][:, 2 * u:2 * u + 2, :].bitcast(F32), ALU.subtract).then_inc(o_ready, 2)
                for hd in hg_heads(t, 5):
                    dve.wait_ge(hg_or, hd + 1)
                    nc.vector.scalar_tensor_tensor(hg_out[:, hd, :], hg_out[:, hd, :], aux[:, HG_NORM:HG_NORM + 1], hg_rms[:, :],
                                                   ALU.mult, ALU.mult).then_inc(hg_on, 1)
                for hd in hg_heads(t, 3):
                    if hd == 0:
                        dve.wait_ge(hg_mask_in, 16)
                        dve.wait_ge(hg_zero, 1)
                    dve.wait_ge(hg_S, hd + 1)
                    for level in range(LEVELS - 1):
                        b = 1 << level
                        nc.vector.tensor_tensor(hg_half(hg_M[:, level, :], level, 1), hg_all[:, P * level:P * (level + 1)].rearrange("p (n b) -> p n b", b=b),
                                                hg_mask[:, level, :].rearrange("p (n b) -> p n b", b=b), ALU.mult).then_inc(hg_sm, 1)
                    nc.vector.tensor_tensor(hg_M[:, LEVELS - 1, :].rearrange("p (a t) -> p a t", a=2),
                                            hg_all[:, HG_OWN:HG_OWN + T].rearrange("p (a t) -> p a t", a=2),
                                            ident.unsqueeze(1).broadcast_to([P, 2, P]), ALU.mult).then_inc(hg_sm, 1)
                    if hd:
                        dve.wait_ge(hg_o, hd)
                    nc.vector.tensor_copy(hg_Pc[:, :], hg_all[:, HG_CROSS:HG_CROSS + P]).then_inc(hg_Pcr, 1)
                    dve.wait_ge(hg_sm, LEVELS * (hd + 1))
                    nc.vector.tensor_reduce(hg_P[:, :], hg_M[:, :, :].rearrange("p l t -> p t l"), AX.X, ALU.add).then_inc(hg_Pr, 1)
                for hd in hg_heads(t, 2):
                    q = hg_q[:, hd // 2 % 2, hg_cols(hd)]
                    dve.wait_ge(hg_dec, hd + 1)
                    dve.wait_ge(hg_qs, hd // 2 + 1)
                    for level in range(LEVELS):
                        op = nc.vector.tensor_tensor(hg_half(hg_E[:, hd % 2, level, :], level, 1), hg_half(hg_E[:, hd % 2, level, :], level, 1),
                                                     hg_half(q, level, 1), ALU.mult)
                    op.then_inc(hg_qd, 1)

            nc.vector.memset(rbx[BUCKETS:BUCKETS + 1, :], NEG).then_inc(bias_masked, 1)
            dve.wait_ge(bias_in, 32)
            dve.wait_ge(bias_masked, 1)
            nc.vector.tensor_copy(rbx8[:, :].rearrange("p (n k) -> p n k", k=REPEAT), rbx[:, :].unsqueeze(2).broadcast_to([BUCKETS + 1, GROUPS * HEADS, REPEAT])).then_inc(bias_masked, 1)
            stage_norm("hgrn")
            for t in range(HG_TICKS):
                if t < HG_SLOTS:
                    u, j = hg_slot(t)
                    n = st["base"] + t
                    if t == 1:
                        dve.wait_ge(lb_exp, 1)
                        nc.vector.tensor_tensor(lbt[:, 2, :], lbt[:, 0, :], lbt[:, 1, :], ALU.add).then_inc(lb_ready, 1)
                        dve.wait_ge(lb_ready, 2)
                        nc.vector.reciprocal(lbt[:, 3, :], lbt[:, 2, :]).then_inc(lb_ready, 1)
                        dve.wait_ge(lb_ready, 3)
                        nc.vector.tensor_tensor(lbt[:, 2, :], lbt[:, 0, :], lbt[:, 3, :], ALU.mult).then_inc(lb_ready, 1)
                        nc.vector.tensor_tensor(oml[:, :], lbt[:, 1, :], lbt[:, 3, :], ALU.mult).then_inc(lb_ready, 1)
                        dve.wait_ge(lb_ready, 5)
                        nc.vector.tensor_scalar(lb[:, :], lbt[:, 2, :], GATE_MIN, None, ALU.max).then_inc(lb_ready, 1)
                        dve.wait_ge(lb_ready, 6)
                    if j == 2:
                        dve.wait_ge(hg_s, 3 * u + 3)
                        if u > 1:
                            dve.wait_ge(hg_S, 2 * u - 2)
                        for a in range(2):
                            hd, cols = 2 * u + a, slice(T * a, T * (a + 1))
                            nc.vector.tensor_scalar(hg_exp[1][:, cols], hg_exp[1][:, cols], oml[:, hd:hd + 1], lb[:, hd:hd + 1],
                                                    ALU.mult, ALU.add).then_inc(hg_f, 1)
                            nc.vector.tensor_scalar(hg_k[:, u % 2, cols], hg_exp[2][:, cols], oml[:, hd:hd + 1], None,
                                                    ALU.mult).then_inc(hg_kk, 1)
                    if t % 3 == 0 and 0 < t <= HG_QFI:
                        v = t // 3 - 1
                        dve.wait_ge(hg_lf, v + 1)
                        if v:
                            dve.wait_ge(hg_dif, 2 * v)
                        for a in range(2):
                            cols = slice(T * a, T * (a + 1))
                            nc.vector.tensor_tensor_scan(hg_c[:, cols], ones[:, 0:1].broadcast_to([P, T]),
                                                         hg_exp[1][:, cols], 0.0, ALU.mult, ALU.add).then_inc(hg_cum, 1)
                    dve.wait_ge(slot_done, n + 3)
                    if j == 0 and u:
                        dve.wait_ge(hg_qs, u)
                    if j == 1 and u:
                        dve.wait_ge(hg_vtr, u)
                    if j == 2:
                        dve.wait_ge(hg_e, 3 * u + 3)
                    if j == 3:
                        dve.wait_ge(hg_qs if u == 0 else hg_vtr if u == 1 else hg_gs, HG_UNITS if u < 2 else u - 1)
                    scaled(hg_raw[(0, 1, 1, u % 2)[j]][:, :], st["fill"] + t, e)
                    split_low(n + 2, (n + 2) // 2, n % 2, kinds[n + 2])
                    if j == 0:
                        sigmoid_one(3 * u + 1, hg_exp[0][:, :])
                    if j == 1:
                        sigmoid_one(3 * u + 2, hg_exp[1][:, :])
                        sigmoid_one(3 * u + 3, hg_exp[2][:, :])
                    if j == 3:
                        sigmoid_one(HG_QFI + u + 1, hg_exp[0][:, :])
                    if t == 0:
                        dve.wait_ge(late_turned, 1)
                        nc.vector.tensor_copy(gains[:, FIRST_ROWS:GAIN_ROWS], ps[:, HG_VBANK, 0:GAIN_ROWS - FIRST_ROWS])
                        nc.vector.tensor_copy(aux[:, :], ps[:, HG_VBANK, P:P + AUX]).then_inc(aux_ready, 1)
                        dve.wait_ge(aux_ready, 1)
                        l0, l1 = aux[:, 0:A_HEADS], aux[:, A_HEADS:2 * A_HEADS]
                        nc.vector.tensor_tensor(lbt[:, 2, :], l0, l1, ALU.max).then_inc(lb_ready, 1)
                        dve.wait_ge(lb_ready, 1)
                        nc.vector.tensor_tensor(lbt[:, 0, :], l0, lbt[:, 2, :], ALU.subtract).then_inc(lb_steps, 1)
                        nc.vector.tensor_tensor(lbt[:, 1, :], l1, lbt[:, 2, :], ALU.subtract).then_inc(lb_steps, 1)
                        dve.wait_ge(bias_made, 1)
                        nc.vector.tensor_copy(bias_rows[:, :, :], ps[:, HG_SCORES:HG_SCORES + GROUPS, 0:ROW]).then_inc(bias_copied, 1)
                    late(t)
                elif t < HG_TICKS - 1:
                    out_slot("hgrn_out", t - HG_SLOTS)
                    late(t)
                else:
                    late(t)
                    out_slot("hgrn_out", t - HG_SLOTS)


        def dil():
            st, e, ek = stages["dil"], reads["dil"], reads["dil"] - 1

            def steps(point):
                slot = dl_projected(point)
                if slot is not None and not dl_slot(slot)[2]:
                    n, (u, j, _) = dl_qk_number(slot), dl_slot(slot)
                    g = j // 2
                    dve.wait_ge(dl_rrd, n + 1)
                    if j % 2 == 0:
                        if u:
                            dve.wait_ge(dl_scored, 4 * u)
                        for odd in range(2):
                            rows = slice(HD * odd, HD * (odd + 1))
                            op = nc.vector.scalar_tensor_tensor(dl_q[rows, g, odd, :], dl_t[rows, slot % 2, :], q_gain[rows, g:g + 1],
                                                                dl_rr[rows, :], ALU.mult, ALU.mult)
                    else:
                        if u > 1:
                            dve.wait_ge(dl_scored, 4 * (u - 1))
                        op = nc.vector.scalar_tensor_tensor(dl_k[:, u % 2, g, :], dl_t[:, slot % 2, :], aux[:, HG_NORM + 1 + g:HG_NORM + 2 + g],
                                                            dl_rr[:, :], ALU.mult, ALU.mult)
                    op.then_inc(dl_qkd, 1)
                for two in dl_due(point, DL_PV):
                    u, c = divmod(two, 2)
                    if c == 1:
                        dve.wait_ge(dl_ohi, u + 1)
                        nc.vector.tensor_tensor(flat(dl_oT[1][:, 2 * u:2 * u + 2, :]), ps[:, DL_OUT, :],
                                                flat(dl_oT[0][:, 2 * u:2 * u + 2, :]).bitcast(F32), ALU.subtract).then_inc(o_ready, 2)
                for hd in dl_due(point, DL_SCALE):
                    dve.wait_ge(dl_exp, hd + 1)
                    nc.vector.reciprocal(dl_rcp[:, hd % 2, :], dl_sum[:, hd % 2, :]).then_inc(dl_rd, 1)
                    dve.wait_ge(dl_rd, hd + 1)
                    own = dl_S[:, hd % 2, 0:GROUPS * T]
                    nc.vector.tensor_scalar(own, own, dl_rcp[:, hd % 2, 1:2], None, ALU.mult).then_inc(dl_sc1, 1)
                for hd in dl_due(point, DL_SCORES):
                    dve.wait_ge(dl_scored, hd + 1)
                    dve.wait_ge((dl_bias_in0, dl_bias_in1)[hd % 2], 16 * (hd // 2 + 1))
                    if hd > 1:
                        dve.wait_ge(dl_turned, hd - 1)
                    S = dl_S[:, hd % 2, :]
                    for tile, keys in ((1, T), (0, P)):
                        nc.vector.tensor_tensor_reduce(dl_blocks(S, keys), dl_blocks(dl_ps, keys), dl_bias[:, hd % 2, :, T - keys:T],
                                                       1.0, -3.0e38, ALU.add, ALU.max, dl_max[:, hd % 2, tile:tile + 1]).then_inc(dl_biased, 1)
                    dve.wait_ge(dl_biased, 2 * hd + 2)
                    nc.vector.tensor_scalar(dl_nmax[:, hd % 2, :], dl_max[:, hd % 2, :], -1.0, None, ALU.mult).then_inc(dl_neg, 1)

            nc.vector.tensor_scalar(q_gain[:, :], aux[:, HG_NORM + 1 + GROUPS:HG_NORM + 1 + 2 * GROUPS], HD ** -0.5, None, ALU.mult).then_inc(q_gain_ready, 1)
            dve.wait_ge(q_gain_ready, 1)
            dve.wait_ge(dl_zero, 1)
            stage_norm("dil")
            for t in range(DL_TICKS):
                steps(2 * t)
                if t < DL_SLOTS:
                    n = st["base"] + t
                    u, j, values = dl_slot(t)
                    dve.wait_ge(slot_done, n + 3)
                    if t > 1:
                        if dl_slot(t - 2)[2]:
                            dve.wait_ge(dl_vtr, dl_v_number(t - 2) + 1)
                        else:
                            dve.wait_ge(dl_sqd, dl_qk_number(t - 2) + 1)
                    scaled(dl_t[:, t % 2, :], st["fill"] + t, ek if values or j % 2 else e)
                    split_low(n + 2, (n + 2) // 2, n % 2, kinds[n + 2])
                else:
                    out_slot("dil_out", t - DL_SLOTS)
                steps(2 * t + 1)


        def stick():
            st, e = stages["stick"], reads["stick"]

            def late(t):
                for u in sk_scores_at(t):
                    dve.wait_ge(sk_ln, u + 1)
                    if u:
                        dve.wait_ge(sk_sum, u)
                    nc.vector.scalar_tensor_tensor(sk_sp[:, :], sk_all, 0.0, sk_e[:, :], ALU.max, ALU.add).then_inc(sk_spd, 1)
                for u in sk_values_at(t):
                    dve.wait_ge(sk_ohi, u + 1)
                    nc.vector.tensor_tensor(flat(sk_oT[1][:, 2 * u:2 * u + 2, :]), ps[:, SK_OUT, :],
                                            flat(sk_oT[0][:, 2 * u:2 * u + 2, :]).bitcast(F32), ALU.subtract).then_inc(o_ready, 2)

            stage_norm("stick")
            dve.wait_ge(sk_zero, 1)
            for t in range(SK_TICKS):
                n = st["base"] + t
                if t >= SK_SLOTS:
                    out_slot("stick_out", t - SK_SLOTS)
                    late(t)
                    continue
                dve.wait_ge(slot_done, n + 3)
                if t < SK_QK:
                    u = t // 2
                    if u > 1:
                        dve.wait_ge(sk_z, u - 1)
                    if t % 2 == 0:
                        for odd in range(2):
                            rows = slice(HD * odd, HD * (odd + 1))
                            op = nc.vector.scalar_tensor_tensor(pair(sk_q[rows, u % 2, odd, :]), pair(bank_of(st["fill"] + t)[rows, :]), HD ** -0.5,
                                                                r_of(e)[rows, :, :], ALU.mult, ALU.mult)
                        op.then_inc(evac_done, 1)
                    else:
                        scaled(sk_k[:, u % 2, :], st["fill"] + t, e)
                else:
                    u = t - SK_QK
                    if u > 1:
                        dve.wait_ge(sk_vtr, u - 1)
                    scaled(sk_t[:, u % 2, :], st["fill"] + t, e)
                split_low(n + 2, (n + 2) // 2, n % 2, kinds[n + 2])
                late(t)


        def swa_kv():
            st, e = stages["swa_kv"], reads["swa_kv"]
            stage_norm("swa_kv")
            for j, tile in enumerate((kv_t, kv_v)):
                dve.wait_ge(slot_done, st["base"] + j + 3)
                scaled(tile[:, :], st["fill"] + j, e)
                if j == 0:
                    split_low(*ahead_of(st, 0, j))
            dve.wait_ge(kv_rope_in, 32)
            dve.wait_ge(kv_rot, 1)
            nc.vector.tensor_tensor(pair(kv_s[:, :]), pair(ps[:, KV_ROT, :]), rope_of(1), ALU.mult).then_inc(kv_sin, 1)
            dve.wait_ge(kv_cos, 1)
            dve.wait_ge(kv_sin, 1)
            nc.vector.tensor_tensor(kv_c[:, :], kv_c[:, :], kv_s[:, :], ALU.add).then_inc(kv_sum, 1)
            split_low(*ahead_of(st, 0, 1))


        def swa():
            st, e = stages["swa"], reads["swa"]

            def early(t):
                for u in sw_at(t, 1):
                    dve.wait_ge(sw_rot, u + 1)
                    if u:
                        dve.wait_ge(sw_qr, u)
                    nc.vector.tensor_tensor(pair(sw_s[:, :]), pair(ps[:, SW_OUT, :]), rope_of(1), ALU.mult).then_inc(sw_sin, 1)
                    dve.wait_ge(sw_cos, u + 1)
                    dve.wait_ge(sw_sin, u + 1)
                    if u > 1:
                        dve.wait_ge(sw_scored, u - 1)
                    for odd in range(2):
                        rows = slice(HD * odd, HD * (odd + 1))
                        op = nc.vector.tensor_tensor(sw_q[rows, u % 2, odd, :], sw_c[rows, u % 2, :], sw_s[rows, :], ALU.add)
                    op.then_inc(sw_qr, 1)

            def late(t):
                for u in sw_at(t, 3):
                    dve.wait_ge(sw_ohi, u + 1)
                    nc.vector.tensor_tensor(flat(sw_oT[1][:, 2 * u:2 * u + 2, :]), ps[:, SW_OUT, :],
                                            flat(sw_oT[0][:, 2 * u:2 * u + 2, :]).bitcast(F32), ALU.subtract).then_inc(o_ready, 2)
                for u in sw_at(t, 1):
                    dve.wait_ge(sw_scored, u + 1)
                    if u > 1:
                        dve.wait_ge(sw_turned, u - 1)
                    for a in range(4):
                        for tile in range(2):
                            keys = T if tile else P
                            nc.vector.tensor_tensor_reduce(sw_biased(u, a, tile), sw_scores(a, tile), swa_mask[:, T - keys:T], 1.0,
                                                           sinks[:, 4 * u + a:4 * u + a + 1], ALU.add, ALU.max,
                                                           sw_max[:, u % 2, tile, a:a + 1]).then_inc(sw_masked, 1)
                    dve.wait_ge(sw_masked, 8 * u + 8)
                    nc.vector.tensor_scalar(sw_nmax[:, u % 2, :, :], sw_max[:, u % 2, :, :], -1.0, None, ALU.mult).then_inc(sw_neg, 1)
                    dve.wait_ge(sw_neg, u + 1)
                    nc.vector.tensor_tensor(sw_sink[:, u % 2, :, :], sw_nmax[:, u % 2, :, :],
                                            sinks[:, 4 * u:4 * u + 4].unsqueeze(1).broadcast_to([P, 2, 4]), ALU.add).then_inc(sw_dm, 1)

            def last(t):
                for u in sw_at(t, 1):
                    dve.wait_ge(sw_snk, u + 1)
                    dve.wait_ge(sw_exp, 8 * u + 8)
                    nc.vector.tensor_tensor(sw_den[:, u % 2, :, :], sw_sum[:, u % 2, :, :], sw_sink[:, u % 2, :, :], ALU.add).then_inc(sw_dn, 1)
                    dve.wait_ge(sw_dn, u + 1)
                    nc.vector.reciprocal(sw_rcp[:, u % 2, :, :], sw_den[:, u % 2, :, :]).then_inc(sw_rd, 1)
                    dve.wait_ge(sw_rd, u + 1)
                    own = sw_S[:, u % 2, 0:4 * T].rearrange("p (a k) -> p a k", a=4)
                    nc.vector.tensor_tensor(own, own, sw_rcp[:, u % 2, 1, :].unsqueeze(2).broadcast_to([P, 4, T]), ALU.mult).then_inc(sw_sc1, 1)

            stage_norm("swa")
            dve.wait_ge(sw_zero, 1)
            for t in range(SW_TICKS):
                early(t)
                if t < SW_UNITS:
                    dve.wait_ge(slot_done, st["base"] + t + 3)
                    if t > 1:
                        dve.wait_ge(sw_rot, t - 1)
                        dve.wait_ge(sw_cos, t - 1)
                    scaled(sw_t[:, t % 2, :], st["fill"] + t, e, HD ** -0.5)
                    split_low(*ahead_of(st, t // 2, t % 2))
                else:
                    out_slot("swa_out", t - SW_UNITS)
                late(t)
                last(t)

        nc.vector.memset(eps[:, :], EPS).then_inc(eps_ready, 1)
        dve.wait_ge(rows_turned, 1)
        nc.vector.tensor_copy(gains[:, 0:FIRST_ROWS], ps[:, BANK_SUM, 0:FIRST_ROWS]).then_inc(gains_ready, 1)
        for m in range(NPAIR):
            dve.wait_ge(x_turned, m + 1)
            update_x(0, m, bank_of(m), 1.0)
            low_x(0, m)
            if m < 2:
                split_low(*slot0(m))
        for layer in layers:
            if layer.startswith("ffn"):
                ffn(int(layer[3:]))
            if layer == "hgrn":
                hgrn()
            if layer == "dil":
                dil()
            if layer == "stick":
                stick()
            if layer == "swa_kv":
                swa_kv()
            if layer == "swa":
                swa()
        norm(LAST)
        for c in range(KC):
            col = GAIN["final_norm_2"] + c
            nc.vector.scalar_tensor_tensor(fin[:, c, :], x[:, c, :], gains[:, col:col + 1], r[:, LAST % 2, :],
                                           ALU.mult, ALU.mult).then_inc(final_y, 1)

    @block.gpsimd
    def _(pool):
        pool.sem_inc(gs_done, 1)
        pool.sem_inc(hT_ready, 1)

        def squares(e, m, fill):
            pool.wait_ge(evac_done, fill + 3)
            if m == 0:
                if e:
                    pool.wait_ge(ss_ready, e)
                nc.gpsimd.tensor_tensor(acc[:, :], xpair(m), xpair(m), ALU.mult).then_inc(acc_done, 1)
            else:
                pool.wait_ge(acc_done, NPAIR * e + m)
                nc.gpsimd.tensor_tensor(sq[:, :], xpair(m), xpair(m), ALU.mult).then_inc(sq_done, 1)
                pool.wait_ge(sq_done, (NPAIR - 1) * e + m)
                nc.gpsimd.tensor_tensor(acc[:, :], acc[:, :], sq[:, :], ALU.add).then_inc(acc_done, 1)

        def ffn(f):
            st, e = stages[f"up{f}"], reads[f"up{f}"]
            pool.wait_ge(r_ready, e + 1)
            with pool.Fori(0, FPAIRS) as i:
                p = FPAIRS * f + i
                pool.wait_ge(sig_ready, p + 1)
                nc.gpsimd.tensor_tensor(gate_s[:, :], gate[:, :], gate_s[:, :], ALU.mult).then_inc(gs_done, 1)
                pool.wait_ge(gs_done, p + 2)
                pool.wait_ge(evac_done, st["fill"] + 2 * i + 2)
                nc.gpsimd.tensor_tensor(pair(gate_r[:, :]), pair(gate_s[:, :]), r_of(e), ALU.mult).then_inc(gr_done, 1)
                pool.wait_ge(hhi_done, p + 1)
                lo = hT_lo_flat[:, bass.ds(2 * T * i, 2 * T)]
                nc.gpsimd.tensor_tensor(lo, h[:, :], hT_hi_flat[:, bass.ds(2 * T * i, 2 * T)].bitcast(F32),
                                        ALU.subtract).then_inc(hT_ready, 1)
            for m in range(NPAIR):
                squares(update_of[f"down{f}"], m, stages[f"down{f}"]["fill"] + m)

        def out_stage(name):
            for m in range(NPAIR):
                squares(update_of[name], m, stages[name]["fill"] + m)

        def hgrn():
            nc.gpsimd.memset(hg_M[:, :, :], 0.0).then_inc(hg_zero, 1)
            for t in range(HG_TICKS):
                for u in range(HG_UNITS):
                    if t == HG_QFI + u + 1:
                        pool.wait_ge(hg_s, HG_QFI + u + 1)
                        if u:
                            pool.wait_ge(hg_og, u)
                        nc.gpsimd.tensor_tensor(hg_g[:, :], hg_raw[u % 2][:, :], hg_exp[0][:, :], ALU.mult).then_inc(hg_gs, 1)
                for hd in hg_heads(t, 2):
                    k = hg_k[:, hd // 2 % 2, hg_cols(hd)]
                    pool.wait_ge(hg_dec, hd + 1)
                    pool.wait_ge(hg_kk, hd + 1)
                    for level in range(LEVELS):
                        op = nc.gpsimd.tensor_tensor(hg_half(hg_E[:, hd % 2, level, :], level, 0), hg_half(hg_E[:, hd % 2, level, :], level, 0),
                                                     hg_half(k, level, 0), ALU.mult)
                    op.then_inc(hg_kd, 1)
                if t % 3 == 2 and t < HG_QFI:
                    u = t // 3
                    pool.wait_ge(hg_s, 3 * u + 1)
                    if u > 1:
                        pool.wait_ge(hg_S, 2 * u - 2)
                    nc.gpsimd.tensor_tensor(hg_q[:, u % 2, :], hg_raw[0][:, :], hg_exp[0][:, :], ALU.mult).then_inc(hg_qs, 1)
                for hd in hg_heads(t, 0):
                    c = hg_c[:, hg_cols(hd)]
                    pool.wait_ge(hg_cum, hd + 1)
                    if hd > 1:
                        pool.wait_ge(hg_S, hd - 1)
                    for level in range(LEVELS):
                        b = 1 << level
                        first, second = hg_half(c, level, 0), hg_half(c, level, 1)
                        middle = first[:, :, b - 1:b].broadcast_to([P, T // (2 * b), b])
                        nc.gpsimd.tensor_tensor(hg_half(hg_E[:, hd % 2, level, :], level, 0), middle, first, ALU.subtract)
                        op = nc.gpsimd.tensor_tensor(hg_half(hg_E[:, hd % 2, level, :], level, 1), second, middle, ALU.subtract)
                    op.then_inc(hg_dif, 1)
                for hd in hg_heads(t, 4):
                    pool.wait_ge(hg_oc, hd + 1)
                    if hd:
                        pool.wait_ge(hg_oss, hd)
                    nc.gpsimd.tensor_tensor(hg_osq[:, :], hg_out[:, hd, :], hg_out[:, hd, :], ALU.mult).then_inc(hg_os2, 1)
                for u in hg_units(t, 0):
                    pool.wait_ge(hg_on, 2 * u + 2)
                    pool.wait_ge(hg_gs, u + 1)
                    out = flat(hg_out[:, 2 * u:2 * u + 2, :])
                    nc.gpsimd.tensor_tensor(out, out, hg_g[:, :], ALU.mult).then_inc(hg_og, 1)
            out_stage("hgrn_out")


        def dil():
            st = stages["dil"]
            nc.gpsimd.memset(dl_q[:, :, :, :], 0.0).then_inc(dl_zero, 1)
            for point in range(2 * DL_TICKS):
                t, half = divmod(point, 2)
                for hd in dl_due(point, DL_SCALE):
                    pool.wait_ge(dl_rd, hd + 1)
                    own = dl_S[:, hd % 2, GROUPS * T:]
                    nc.gpsimd.tensor_tensor(own, own, dl_rcp[:, hd % 2, 0:1].broadcast_to([P, GROUPS * P]), ALU.mult).then_inc(dl_sc0, 1)
                if half and t < DL_SLOTS and not dl_slot(t)[2]:
                    n = dl_qk_number(t)
                    pool.wait_ge(evac_done, st["fill"] + t + 3)
                    if n:
                        pool.wait_ge(dl_ss, n)
                    nc.gpsimd.tensor_tensor(dl_sq[:, :], dl_t[:, t % 2, :], dl_t[:, t % 2, :], ALU.mult).then_inc(dl_sqd, 1)
            out_stage("dil_out")


        def stick():
            nc.gpsimd.memset(sk_q[:, :, :, :], 0.0).then_inc(sk_zero, 1)
            out_stage("stick_out")


        def swa_kv():
            st = stages["swa_kv"]
            pool.wait_ge(evac_done, st["fill"] + 3)
            pool.wait_ge(kv_rope_in, 32)
            nc.gpsimd.tensor_tensor(pair(kv_c[:, :]), pair(kv_t[:, :]), rope_of(0), ALU.mult).then_inc(kv_cos, 1)


        def swa():
            st = stages["swa"]
            nc.gpsimd.memset(sw_q[:, :, :, :], 0.0).then_inc(sw_zero, 1)
            for u in range(SW_UNITS + 1):
                if u < SW_UNITS:
                    pool.wait_ge(evac_done, st["fill"] + u + 3)
                    if u > 1:
                        pool.wait_ge(sw_qr, u - 1)
                    nc.gpsimd.tensor_tensor(pair(sw_c[:, u % 2, :]), pair(sw_t[:, u % 2, :]), rope_of(0), ALU.mult).then_inc(sw_cos, 1)
                if u:
                    pool.wait_ge(sw_rd, u)
                    own = sw_S[:, (u - 1) % 2, 4 * T:6 * T].rearrange("p (a k) -> p a k", a=4)
                    nc.gpsimd.tensor_tensor(own, own, sw_rcp[:, (u - 1) % 2, 0, :].unsqueeze(2).broadcast_to([P, 4, P]), ALU.mult).then_inc(sw_sc0, 1)
            out_stage("swa_out")

        for m in range(NPAIR):
            squares(0, m, m)
        for layer in layers:
            if layer.startswith("ffn"):
                ffn(int(layer[3:]))
            if layer == "hgrn":
                hgrn()
            if layer == "dil":
                dil()
            if layer == "stick":
                stick()
            if layer == "swa_kv":
                swa_kv()
            if layer == "swa":
                swa()
    ctx.close()


INPUTS = [
    "x", "norm_gain", "ffn_w_in", "ffn_w_out", "a_w_in", "a_lb_logits", "a_out_gain", "a_w_out", "kv_norm", "w_kv",
    "k_gain", "b_w_q", "b_q_gain", "b_w_o", "rel_bias", "ffn1_norm_2", "ffn1_w_in_2", "ffn1_w_out_2",
    "mix_norm_2", "ffn2_norm_2", "ffn2_w_in_2", "ffn2_w_out_2", "sb_w_qkv_2", "sb_w_o_2", "kv_norm_2", "kv_w_2",
    "swa_w_q_2", "swa_sinks_2", "swa_w_o_2", "final_norm_2",
]


def kernel(**inputs):
    import concourse.bacc as bacc
    from concourse.bass_utils import run_bass_kernel_spmd

    nc = bacc.Bacc("TRN2", target_bir_lowering=False, num_devices=1)
    arrays = {name: np.ascontiguousarray(inputs[name]) for name in INPUTS}
    arrays["consts"] = constants()
    io = {name: nc.dram_tensor(f"in_{name}", a.shape, F32, kind="ExternalInput").ap() for name, a in arrays.items()}
    io["out"] = nc.dram_tensor("out", (1, T, D), F32, kind="ExternalOutput").ap()
    build_program(nc, io)
    result = run_bass_kernel_spmd(nc, [{f"in_{name}": a for name, a in arrays.items()}], core_ids=[0])
    return result.results[0]["out"]
```

```python
from contextlib import ExitStack

import numpy as np

import concourse.bass as bass
from concourse import mybir

ALU = mybir.AluOpType
ACT = mybir.ActivationFunctionType
AX = mybir.AxisListType
F32 = mybir.dt.float32
F32R = mybir.dt.float32r

P = 128
T = 256
D = 1024
KC = D // P
FF = 2816
FC = FF // P
FPAIRS = FC // 2
W2 = 2 * P
NPAIR = KC // 2
EPS = 1e-6
EXP_MAX = 2.0 ** 60
GATE_MIN = 2.0 ** -60
NEG = -1e30

HEADS = 16
HD = 64
GROUPS = 3
WINDOWS = (128, 512, 2048)
DILATIONS = (1, 4, 16)
BUCKETS = 32
MAX_DISTANCE = 2048
QKV = GROUPS * HEADS * HD
A_HEADS = 8
LEVELS = 8
KV_HEADS = 4
SWA_WINDOW = 128
ROPE_THETA = 10000.0

HALVES = {
    "k8": ((0, 4 * W2, 4), (4 * W2, 4 * W2, 4)),
    "k11": ((0, 6 * W2, 6), (6 * W2, 5 * W2, 5)),
}
SLOT = FC // 2 * W2
HALF = 6 * W2


def t5_bucket(dist):
    exact = BUCKETS // 2
    large = exact + (np.log(np.maximum(dist, 1) / exact) / np.log(MAX_DISTANCE / exact) * (BUCKETS - exact)).astype(np.int32)
    return np.where(dist < exact, dist, np.minimum(large, BUCKETS - 1)).astype(np.int32)


CONST_WIDTHS = [
    ("ident", P), ("ones", P), ("blk64", P), ("neg_suffix", P), ("neg_ones", P), ("rot", P), ("dup0", P), ("dup1", P),
    ("neg_mask", P), ("hg_mask", (LEVELS - 1) * P), ("swa_mask", T), ("cos", T), ("sin", T), ("onehot", GROUPS * 3 * P),
]
CONST_AT = {}
_at = 0
for _name, _width in CONST_WIDTHS:
    CONST_AT[_name] = (_at, _width)
    _at += _width
CONST_COLS = _at


def constants():
    c = np.zeros((P, CONST_COLS), np.float32)

    def put(name, value):
        at, width = CONST_AT[name]
        c[:value.shape[0], at:at + width] = value.reshape(value.shape[0], width)

    i = np.arange(P)
    put("ident", np.eye(P))
    put("ones", np.ones((P, P)))
    put("blk64", (i[:, None] // HD == i[None, :] // HD).astype(np.float32))
    put("neg_suffix", -(i[:, None] >= i[None, :]).astype(np.float32))
    put("neg_ones", -np.ones((P, P)))
    rot = np.zeros((P, P), np.float32)
    for t in range(P):
        if t % HD < HD // 2:
            rot[t + HD // 2, t] = -1.0
        else:
            rot[t - HD // 2, t] = 1.0
    put("rot", rot)
    for half in range(2):
        put(f"dup{half}", (i[:, None] == HD * half + i[None, :] % HD).astype(np.float32))
    put("neg_mask", np.where(i[:, None] < i[None, :], 0.0, NEG).astype(np.float32))
    mask = np.zeros((P, LEVELS - 1, P), np.float32)
    for level in range(LEVELS - 1):
        b = 1 << level
        n = np.arange(P) % (P // 2) // b
        mask[:, level] = (i[:, None] // (2 * b) == n[None, :]) & (i[:, None] % (2 * b) < b)
    put("hg_mask", mask)
    diff = P + i[:, None] - np.arange(T)[None, :]
    put("swa_mask", np.where((diff >= 0) & (diff < SWA_WINDOW), 0.0, NEG).astype(np.float32))
    half = HD // 2
    inv_freq = np.float32(ROPE_THETA) ** (-np.arange(half, dtype=np.float32) / np.float32(half))
    angle = np.arange(T, dtype=np.float32)[None, :] * inv_freq[i % half][:, None]
    put("cos", np.cos(angle, dtype=np.float32))
    put("sin", np.sin(angle, dtype=np.float32))
    onehot = np.zeros((BUCKETS + 1, GROUPS, 3 * P), np.float32)
    dist = T - 1 - np.arange(3 * P)
    for g, (w, dil) in enumerate(zip(WINDOWS, DILATIONS)):
        valid = (dist >= 0) & (dist <= w) & (dist % dil == 0)
        bucket = t5_bucket(np.maximum(dist, 0))
        onehot[bucket[valid], g, np.nonzero(valid)[0]] = 1.0
        onehot[BUCKETS, g] = ~valid
    put("onehot", onehot)
    return c


def build_program(nc, io, upto=None):
    ctx = ExitStack()

    def sb(name, shape, dt=F32, stack=ctx):
        return stack.enter_context(nc.sbuf_tensor(name, shape, dt))

    def sem(name):
        return ctx.enter_context(nc.semaphore(name))

    LAYERS = ["ffn0", "hgrn", "ffn1", "ffn2", "dil", "ffn3", "ffn4", "stick", "ffn5", "swa_kv", "ffn6", "swa", "ffn7"]
    layers = LAYERS[:upto]
    stages = {}
    kinds = []
    fills = [NPAIR]

    def stage(name, kind, count, per_fill=1):
        assert len(kinds) % 2 == 0 and fills[0] % 2 == 0
        stages[name] = {"base": len(kinds), "count": count, "kind": kind, "fill": fills[0]}
        kinds.extend([kind] * count)
        fills[0] += count // per_fill

    for layer in layers:
        if layer.startswith("ffn"):
            stage(f"up{layer[3:]}", "k8", 2 * FPAIRS)
            stage(f"down{layer[3:]}", "k11", 2 * NPAIR, 2)
        if layer == "hgrn":
            stage("hgrn", "k8", 4 * A_HEADS // 2)
        if layer == "dil":
            stage("dil", "k8", 3 * GROUPS * HEADS // 4)
        if layer == "stick":
            stage("stick", "k8", 3 * HEADS // 4)
        if layer == "swa_kv":
            stage("swa_kv", "k8", 2)
        if layer == "swa":
            stage("swa", "k8", HEADS // 4)
        if layer in ("hgrn", "dil", "stick", "swa"):
            stage(f"{layer}_out", "k8", NPAIR)

    GAIN = {}
    rows = 0
    for name, n in (("norm_gain", 6 * KC), ("kv_norm", KC), ("ffn1_norm_2", 2 * KC), ("mix_norm_2", 2 * KC),
                    ("ffn2_norm_2", 2 * KC), ("kv_norm_2", KC), ("final_norm_2", KC)):
        GAIN[name] = rows
        rows += n
    GAIN_ROWS = rows
    NG = lambda layer, k: GAIN["norm_gain"] + (3 * layer + k) * KC
    updates = [
        ("input", [("g", NG(0, 0))]),
        ("down0", [("g", NG(0, 1))]),
        ("hgrn_out", [("g", NG(0, 2))]),
        ("down1", [("g", NG(1, 0)), ("k", GAIN["kv_norm"])]),
        ("down2", [("g", NG(1, 1))]),
        ("dil_out", [("g", NG(1, 2))]),
        ("down3", [("g", GAIN["ffn1_norm_2"])]),
        ("down4", [("g", GAIN["mix_norm_2"])]),
        ("stick_out", [("g", GAIN["ffn2_norm_2"])]),
        ("down5", [("k", GAIN["kv_norm_2"]), ("g", GAIN["ffn1_norm_2"] + KC)]),
        ("down6", [("g", GAIN["mix_norm_2"] + KC)]),
        ("swa_out", [("g", GAIN["ffn2_norm_2"] + KC)]),
        ("down7", []),
    ]
    updates = [(n, us) for n, us in updates if n == "input" or n in stages]
    updates[-1] = (updates[-1][0], [])
    update_of = {name: e for e, (name, _) in enumerate(updates)}
    LAST = len(updates) - 1
    g_before, k_before = [], []
    for e in range(LAST + 1):
        g_before.append(KC * sum(u[0] == "g" for _, us in updates[:e] for u in us))
        k_before.append(KC * sum(u[0] == "k" for _, us in updates[:e] for u in us))
    reads = {"up0": 0, "hgrn": 1, "up1": 2, "up2": 3, "dil": 4, "up3": 5, "up4": 6, "stick": 7,
             "up5": 8, "swa_kv": 9, "up6": 9, "swa": 10, "up7": 11}
    norms = reads

    raw = sb("raw", [P, 4, HALF])
    whi = sb("whi", [P, 2, SLOT], F32R)
    wlo = sb("wlo", [P, 2, SLOT], F32R)
    x = sb("x", [P, KC, T])
    xg = sb("xg", [P, KC, 2, T], F32R)
    xg_hi, xg_lo = [xg[:, :, n, :] for n in range(2)]
    ROW = 3 * P
    REPEAT = P // HEADS
    BIAS_STORES = 4 * GROUPS
    spare = ExitStack()
    bias_rows = sb("bias_rows", [P, GROUPS, ROW], F32, spare)
    rbx = sb("rbx", [BUCKETS + 1, GROUPS * HEADS], F32, spare)
    rbx8 = sb("rbx8", [BUCKETS + 1, GROUPS * P], F32, spare)
    onehot = sb("onehot", [BUCKETS + 1, GROUPS * ROW], F32, spare)
    rows_late = sb("rows_late", [P, P], F32, spare)
    aux_in = sb("aux_in", [P, P], F32, spare)
    spare.close()
    last = ExitStack()
    fin = sb("fin", [P, KC, T], F32, last)
    last.close()
    xk_hi = sb("xk_hi", [P, KC, T], F32R)
    xk_lo = sb("xk_lo", [P, KC, T], F32R)
    CONSTS = CONST_AT["hg_mask"][0]
    cst = sb("cst", [P, CONSTS])
    gains = sb("gains", [P, GAIN_ROWS])
    AUX = 2 * A_HEADS + 1 + 2 * GROUPS
    aux = sb("aux", [P, AUX])
    q_gain = sb("q_gain", [P, GROUPS])
    lb = sb("lb", [P, A_HEADS])
    oml = sb("oml", [P, A_HEADS])
    ln_oml = sb("ln_oml", [P, A_HEADS])
    lbt = sb("lbt", [P, 4, A_HEADS])
    eps = sb("eps", [P, 1])
    sinks = sb("sinks", [P, HEADS])
    r = sb("r", [P, 2, T])
    ms = sb("ms", [P, T])
    ms_ln = sb("ms_ln", [P, T])
    r0 = sb("r0", [P, T])
    newton = sb("newton", [P, 2, T])
    sq = sb("sq", [P, 2 * T])
    acc = sb("acc", [P, 2 * T])
    sq_last = newton.rearrange("p c t -> p (c t)")

    def const(name):
        at, width = CONST_AT[name]
        return cst[:, at:at + width]

    flat = lambda t: t.rearrange("p c t -> p (c t)")
    ident, ones = const("ident"), const("ones")

    region = ExitStack()
    hT = sb("hT", [P, FC, 2, T], F32R, region)
    gate = sb("gate", [P, 2 * T], F32, region)
    gate_e = sb("gate_e", [P, 2 * T], F32, region)
    gate_s = sb("gate_s", [P, 2 * T], F32, region)
    gate_r = sb("gate_r", [P, 2 * T], F32, region)
    h = sb("h", [P, 2 * T], F32, region)
    kv_t = sb("kv_t", [P, 2 * T], F32, region)
    kv_v = sb("kv_v", [P, 2 * T], F32, region)
    kv_c = sb("kv_c", [P, 2 * T], F32, region)
    kv_s = sb("kv_s", [P, 2 * T], F32, region)
    kdup = sb("kdup", [P, KV_HEADS, T], F32, region)
    v2 = sb("v2", [P, 2, KV_HEADS * HD], F32, region)
    rope = sb("rope", [P, 2, T], F32, region)
    swa_mask = sb("swa_mask", [P, T], F32, region)
    region.close()
    init = ExitStack()
    x_in = sb("x_in", [P, T // P, D], F32, init)
    rows_in = sb("rows_in", [P, P], F32, init)
    out_sb = sb("out_sb", [P, T // P, D], F32, init)
    init.close()

    bias_dram = nc.dram_tensor("bias_by_distance", (GROUPS * HEADS * P * ROW,), F32, kind="Internal").ap()

    ps = ctx.enter_context(nc.psum_tensor("ps", [P, 8, 2 * T], F32))
    UP_BANKS, DOWN_BANKS = (3, 0), (3, 5)
    X_BANKS = (0, 1, 5, 6)
    OUT_TURNED = (0, 1, 2, 7)
    BANK_LAST = 3
    BANK_SUM = 2
    OUT_BANKS = {"hgrn_out": (0, 1, 6, 7), "dil_out": (0, 1, 2, 7), "stick_out": (0, 1, 2, 5), "swa_out": (0, 1, 2, 6)}

    def out_before(name):
        return (NPAIR - 1) * [n for n in OUT_BANKS if n in stages].index(name)


    w_arrived = [sem(f"w_arrived{q}") for q in range(4)]
    hi_done = sem("hi_done")
    lo_done = sem("lo_done")
    slot_done = sem("slot_done")
    evac_done = sem("evac_done")
    const_in = sem("const_in")
    const_late = sem("const_late")
    rows_arrived, late_arrived, late_turned = sem("rows_arrived"), sem("late_arrived"), sem("late_turned")
    x_arrived = sem("x_arrived")
    x_turned = sem("x_turned")
    rows_turned = sem("rows_turned")
    gains_ready = sem("gains_ready")
    aux_ready = sem("aux_ready")
    lb_steps = sem("lb_steps")
    lb_exp = sem("lb_exp")
    lb_ready = sem("lb_ready")
    eps_ready = sem("eps_ready")
    bias_in, bias_masked, bias_made, bias_copied, bias_stored = [sem(n) for n in ("bias_in", "bias_masked", "bias_made", "bias_copied", "bias_stored")]
    xhi_done = sem("xhi_done")
    xg_ready = sem("xg_ready")
    xk_ready = sem("xk_ready")
    sq_done = sem("sq_done")
    sq_last_done = sem("sq_last_done")
    acc_done = sem("acc_done")
    ss_ready = sem("ss_ready")
    ms_ready = sem("ms_ready")
    ms_ln_done = sem("ms_ln_done")
    r0_ready = sem("r0_ready")
    newton_a = sem("newton_a")
    newton_b = sem("newton_b")
    r_ready = sem("r_ready")
    gate_copied = sem("gate_copied")
    h_copied, h_made = sem("h_copied"), sem("h_made")
    gate_made = sem("gate_made")
    half_added = sem("half_added")
    gate_exp = sem("gate_exp")
    gate_den = sem("gate_den")
    gate_ln = sem("gate_ln")
    sig_ready = sem("sig_ready")
    gr_done = sem("gr_done")
    gs_done = sem("gs_done")
    hhi_done = sem("hhi_done")
    hT_ready = sem("hT_ready")
    out_ready = sem("out_ready")
    o_ready = sem("o_ready")
    final_y = sem("final_y")
    final_turned = sem("final_turned")
    final_copied = [sem(f"final_copied{t}") for t in range(T // P)]
    out_stored = sem("out_stored")

    def at(st, i, j):
        return st["base"] + j + 2 * i, st["base"] // 2 + i, j

    def ahead_of(st, i, j):
        n, n2, par = at(st, i, j)
        if isinstance(i, int):
            return n + 2, n2 + 1, par, kinds[n + 2] if n + 2 < len(kinds) else None
        return n + 2, n2 + 1, par, st["kind"]

    def first_to_last(eng, count, body):
        body(0)
        with eng.Fori(1, count - 1) as i:
            body(i)
        body(count - 1)

    def bank_of(fill):
        return ps[:, fill % 2, :]

    def pair(ap):
        return ap.rearrange("p (c t) -> p c t", c=2)

    def r_of(e):
        return r[:, e % 2:e % 2 + 1, :].broadcast_to([P, 2, T])

    def hidden(i, part):
        return hT[:, bass.ds(2 * i, 2), part, :]

    def wide(bank, part):
        return ps[:, bank:bank + 2, T * part:T * (part + 1)]
    x_flat = flat(x[:, :, :])
    xpair = lambda m: x_flat[:, 2 * T * m:2 * T * (m + 1)]
    operand = {"g": (xg_hi, xg_lo), "k": (xk_hi, xk_lo)}

    ffn_weights = [(io["ffn_w_in"][layer, k], io["ffn_w_out"][layer, k]) for layer in range(2) for k in range(2)]
    ffn_weights += [(io[f"ffn{k}_w_in_2"][layer], io[f"ffn{k}_w_out_2"][layer]) for layer in range(2) for k in (1, 2)]
    order = [name for name in stages if name in reads]
    before = dict(zip(order[1:], order))
    slot0 = lambda n: (n, n // 2, n % 2, kinds[n])
    FIRST_ROWS = GAIN["kv_norm"]
    LATE_LOADS = len(GAIN) - 1 + 5

    region = ExitStack()
    hg_raw = [sb(f"hg_raw{n}", [P, 2 * T], F32, region) for n in range(2)]
    hg_exp = [sb(f"hg_exp{n}", [P, 2 * T], F32, region) for n in range(3)]
    hg_q = sb("hg_q", [P, 2, 2 * T], F32, region)
    hg_k = sb("hg_k", [P, 2, 2 * T], F32, region)
    hg_c = sb("hg_c", [P, 2 * T], F32, region)
    hg_ck = sb("hg_ck", [P, 2 * T], F32, region)
    hg_g = sb("hg_g", [P, 2 * T], F32, region)
    hg_v = sb("hg_v", [P, 2, T // P, 2 * P], F32, region)
    hg_E = sb("hg_E", [P, 2, LEVELS, T], F32, region)
    hg_M = sb("hg_M", [P, LEVELS, T], F32, region)
    hg_P = sb("hg_P", [P, T], F32, region)
    hg_Pc = sb("hg_Pc", [P, P], F32, region)
    hg_out = sb("hg_out", [P, KC, T], F32, region)
    hg_rms = sb("hg_rms", [P, T], F32, region)
    hg_mask = sb("hg_mask", [P, LEVELS - 1, P], F32, region)
    hg_oT = [sb(f"hg_oT{n}", [P, KC, T], F32R, region) for n in range(2)]
    region.close()
    hg_osq = sq[:, 0:T]
    hg_mask_in, hg_zero = sem("hg_mask_in"), sem("hg_zero")
    hg_e = sem("hg_e")
    hg_d = sem("hg_d")
    hg_l = sem("hg_l")
    hg_s = sem("hg_s")
    hg_qs, hg_gs = sem("hg_qs"), sem("hg_gs")
    hg_f, hg_ln, hg_lf, hg_cum, hg_ckd = [sem(n) for n in ("hg_f", "hg_ln", "hg_lf", "hg_cum", "hg_ckd")]
    hg_vtr, hg_vt = sem("hg_vtr"), sem("hg_vt")
    hg_dif, hg_dec = sem("hg_dif"), sem("hg_dec")
    hg_qd, hg_S, hg_sm, hg_Pr, hg_Pcr = [sem(n) for n in ("hg_qd", "hg_S", "hg_sm", "hg_Pr", "hg_Pcr")]
    hg_o, hg_oc, hg_os2, hg_oss, hg_oln, hg_or = [sem(n) for n in ("hg_o", "hg_oc", "hg_os2", "hg_oss", "hg_oln", "hg_or")]
    hg_on, hg_og, hg_ohi = sem("hg_on"), sem("hg_og"), sem("hg_ohi")
    HG_UNITS = A_HEADS // 2
    HG_QFI = 3 * HG_UNITS
    HG_SLOTS = HG_QFI + HG_UNITS
    HG_TICKS = HG_SLOTS + NPAIR
    HG_SCORES = 3
    HG_OUT = 2
    HG_VBANK = 7
    HG_NORM = 2 * A_HEADS
    HG_START = (3, 4, 6, 7, 9, 10, 12, 13)
    HG_GATE = tuple(max(HG_QFI + u + 1, HG_START[2 * u + 1] + 5) for u in range(HG_UNITS))

    def hg_heads(t, offset):
        return [hd for hd in range(A_HEADS) if HG_START[hd] + offset == t]

    def hg_units(t, offset):
        return [u for u in range(HG_UNITS) if HG_GATE[u] + offset == t]

    def hg_split(t):
        return [u for u in range(HG_UNITS) if HG_GATE[u] + (u < HG_UNITS - 1) == t]

    def hg_slot(t):
        return (t // 3, t % 3) if t < HG_QFI else (t - HG_QFI, 3)

    def hg_sums(hd):
        return ps[:, HG_VBANK if HG_START[hd] + 5 < HG_SLOTS else HG_OUT, T:2 * T]

    def hg_cols(hd):
        return slice(T * (hd % 2), T * (hd % 2 + 1))

    def hg_half(ap, level, second):
        b = 1 << level
        return ap.rearrange("p (n b) -> p n b", b=2 * b)[:, :, b * second:b * second + b]

    hg_all = ps[:, HG_SCORES:HG_SCORES + 3, :].rearrange("p b n -> p (b n)")
    HG_OWN = (LEVELS - 1) * P
    HG_CROSS = HG_OWN + T

    region = ExitStack()
    dl_t = sb("dl_t", [P, 2, 2 * T], F32, region)
    dl_q = sb("dl_q", [P, GROUPS, 2, 2 * T], F32, region)
    dl_k = sb("dl_k", [P, 2, GROUPS, 2 * T], F32, region)
    dl_v = sb("dl_v", [P, 2, GROUPS, T // P, 4 * HD], F32, region)
    dl_bias = sb("dl_bias", [P, 2, GROUPS, T], F32, region)
    dl_S = sb("dl_S", [P, 2, 3 * GROUPS * P], F32, region)
    dl_PT = sb("dl_PT", [P, 2, 3 * GROUPS * P], F32, region)
    dl_max = sb("dl_max", [P, 2, 2], F32, region)
    dl_nmax = sb("dl_nmax", [P, 2, 2], F32, region)
    dl_sum = sb("dl_sum", [P, 2, 2], F32, region)
    dl_rcp = sb("dl_rcp", [P, 2, 2], F32, region)
    dl_oT = [sb(f"dl_oT{n}", [P, KC, T], F32R, region) for n in range(2)]
    region.close()
    dl_sq, dl_rr = sq, flat(newton[:, :, :])
    q_gain_ready = sem("q_gain_ready")
    dl_sqd, dl_ss, dl_ln, dl_rrd, dl_qkd = [sem(n) for n in ("dl_sqd", "dl_ss", "dl_ln", "dl_rrd", "dl_qkd")]
    dl_vtr, dl_vt, dl_bias_in0, dl_bias_in1 = [sem(n) for n in ("dl_vtr", "dl_vt", "dl_bias_in0", "dl_bias_in1")]
    dl_scored, dl_biased, dl_neg, dl_exp, dl_rd, dl_sc0, dl_sc1 = [
        sem(n) for n in ("dl_scored", "dl_biased", "dl_neg", "dl_exp", "dl_rd", "dl_sc0", "dl_sc1")]
    dl_turned, dl_PTd, dl_pv, dl_ohi, dl_zero = [sem(n) for n in ("dl_turned", "dl_PTd", "dl_pv", "dl_ohi", "dl_zero")]
    DL_UNIT = 3 * GROUPS
    DL_UNITS = HEADS // 4
    DL_SLOTS = DL_UNIT * DL_UNITS
    DL_TICKS = DL_SLOTS + NPAIR
    DL_BANK = 3
    DL_OUT, DL_VBANK = 6, 7
    DL_SCORES = (13, 14, 16, 18)
    DL_SCALE = (14, 15, 17, 19)
    DL_TURN = (15, 17, 19, 21)
    DL_PV = (19, 22)

    def dl_due(point, steps):
        return [len(steps) * u + a for u in range(DL_UNITS) for a, at_half in enumerate(steps) if point == 2 * DL_UNIT * u + at_half]

    def dl_projected(point):
        if point == 2 * DL_SLOTS - 1:
            return DL_SLOTS - 1
        if point == 3:
            return 0
        return point // 2 - 1 if point % 2 == 0 and 2 <= point // 2 < DL_SLOTS else None

    def dl_slot(t):
        return t // DL_UNIT, t % DL_UNIT, t % DL_UNIT >= 2 * GROUPS

    def dl_qk_number(t):
        u, j, _ = dl_slot(t)
        return 2 * GROUPS * u + min(j, 2 * GROUPS)

    def dl_v_number(t):
        u, j, _ = dl_slot(t)
        return GROUPS * u + max(j - 2 * GROUPS, 0)

    def dl_blocks(ap, keys):
        at0 = 0 if keys == T else GROUPS * T
        return ap[:, at0:at0 + GROUPS * keys].rearrange("p (g k) -> p g k", g=GROUPS)

    dl_ps = ps[:, DL_BANK:DL_BANK + 3, :].rearrange("p b n -> p (b n)")[:, 0:3 * GROUPS * P]

    region = ExitStack()
    sk_q = sb("sk_q", [P, 2, 2, 2 * T], F32, region)
    sk_k = sb("sk_k", [P, 2, 2 * T], F32, region)
    sk_t = sb("sk_t", [P, 2, 2 * T], F32, region)
    sk_v = sb("sk_v", [P, 2, T // P, 4 * HD], F32, region)
    sk_e = sb("sk_e", [P, 6 * T], F32, region)
    sk_sp = sb("sk_sp", [P, 6 * T], F32, region)
    sk_w = sb("sk_w", [P, 4, 6 * T], F32, region)
    sk_oT = [sb(f"sk_oT{n}", [P, KC, T], F32R, region) for n in range(2)]
    sk_mask = sb("sk_mask", [P, P], F32R, region)
    sk_ident = sb("sk_ident", [P, P], F32R, region)
    region.close()
    sk_const = sem("sk_const")
    sk_z, sk_abs, sk_ex, sk_ln, sk_spd, sk_sum, sk_wr = [sem(n) for n in ("sk_z", "sk_abs", "sk_ex", "sk_ln", "sk_spd", "sk_sum", "sk_wr")]
    sk_vtr, sk_vt, sk_pv, sk_ohi = [sem(n) for n in ("sk_vtr", "sk_vt", "sk_pv", "sk_ohi")]
    sk_zero = sem("sk_zero")
    SK_UNITS = HEADS // 4
    SK_QK = 2 * SK_UNITS
    SK_SLOTS = SK_QK + SK_UNITS
    SK_TICKS = SK_SLOTS + NPAIR
    SK_BANK, SK_OUT, SK_VBANK = 2, 6, 7
    sk_all = ps[:, SK_BANK:SK_BANK + 4, :].rearrange("p b n -> p (b n)")[:, T:7 * T]

    def sk_first(ap, odd):
        return ap[:, T + 2 * T * odd:3 * T + 2 * T * odd].rearrange("p (a t) -> p a t", a=2)

    def sk_second(ap, odd):
        return ap[:, 5 * T * odd:5 * T * odd + T].rearrange("p (a t) -> p a t", a=2)

    def sk_scores_at(t):
        return [u for u in range(SK_UNITS) if t == 2 * u + 2]

    def sk_sums_at(t):
        return [u for u in range(SK_UNITS) if t == 2 * u + 4]

    def sk_values_at(t):
        return [u for u in range(SK_UNITS) if t == SK_QK + u + 1]

    kv_rope_in = sem("kv_rope_in")
    kv_rot, kv_cos, kv_sin, kv_sum, kv_dup, kv_dupd, kv_vtr, kv_vt = [
        sem(n) for n in ("kv_rot", "kv_cos", "kv_sin", "kv_sum", "kv_dup", "kv_dupd", "kv_vtr", "kv_vt")]
    KV_ROT, KV_DUP, KV_VBANK = 6, 5, 7

    def rope_of(which):
        return rope[:, which:which + 1, :].broadcast_to([P, 2, T])

    region = ExitStack()
    sw_t = sb("sw_t", [P, 2, 2 * T], F32, region)
    sw_c = sb("sw_c", [P, 2, 2 * T], F32, region)
    sw_q = sb("sw_q", [P, 2, 2, 2 * T], F32, region)
    sw_s = sb("sw_s", [P, 2 * T], F32, region)
    sw_S = sb("sw_S", [P, 2, 6 * T], F32, region)
    sw_PT = sb("sw_PT", [P, 6 * T], F32, region)
    sw_max, sw_nmax, sw_sum, sw_sink, sw_den, sw_rcp = [
        sb(n, [P, 2, 2, 4], F32, region) for n in ("sw_max", "sw_nmax", "sw_sum", "sw_sink", "sw_den", "sw_rcp")]
    sw_oT = [sb(f"sw_oT{n}", [P, KC, T], F32R, region) for n in range(2)]
    region.close()
    sw_rot, sw_cos, sw_sin, sw_qr, sw_scored, sw_masked, sw_neg, sw_dm, sw_exp, sw_snk = [
        sem(n) for n in ("sw_rot", "sw_cos", "sw_sin", "sw_qr", "sw_scored", "sw_masked", "sw_neg", "sw_dm", "sw_exp", "sw_snk")]
    sw_dn, sw_rd, sw_sc0, sw_sc1, sw_turned, sw_PTd, sw_pv, sw_ohi, sw_zero = [
        sem(n) for n in ("sw_dn", "sw_rd", "sw_sc0", "sw_sc1", "sw_turned", "sw_PTd", "sw_pv", "sw_ohi", "sw_zero")]
    SW_UNITS = HEADS // 4
    SW_TICKS = SW_UNITS + NPAIR
    SW_BANK, SW_OUT = 3, 7

    def sw_scores(a, tile):
        return ps[:, SW_BANK + a // 2, T * (a % 2):T * (a % 2 + 1)] if tile else ps[:, SW_BANK + 2, P * a:P * (a + 1)]

    def sw_biased(u, a, tile):
        S = sw_S[:, u % 2, :]
        return S[:, T * a:T * (a + 1)] if tile else S[:, 4 * T + P * a:4 * T + P * (a + 1)]

    sw_turn = ps[:, SW_BANK:SW_BANK + 3, :].rearrange("p b n -> p (b n)")

    def sw_keys0(ap, a):
        return ap[:, T * a:T * (a + 1)]

    def sw_keys1(ap, a):
        return ap[:, 4 * T + P * a:4 * T + P * (a + 1)]

    def sw_at(t, offset):
        return [u for u in range(SW_UNITS) if u + offset == t]

    block = ctx.enter_context(nc.Block())

    @block.sync
    def _(sp):
        sp.dma_start(x_in[:, :, :], io["x"].rearrange("b (t p) d -> p (b t) d", p=P)).then_inc(x_arrived, 16)

        def load(n, n2, par, kind, source):
            k = 0
            for half, (_, size, chunks) in enumerate(HALVES[kind]):
                sp.wait_ge(lo_done, 2 * n + half + 1)
                sp.dma_start(raw[:, 2 * par + half, :size].rearrange("p (k w) -> p k w", w=W2),
                             source(k, k + chunks)).then_inc(w_arrived[2 * par + half], 16)
                k += chunks

        def columns(w):
            v = w.rearrange("(k p) n -> p k n", p=P)
            return lambda col, k0=0: lambda a, b: v[:, k0 + a:k0 + b, bass.ds(col, W2)]

        def ffn(f):
            w_in, w_out = [columns(w) for w in ffn_weights[f]]
            st = stages[f"up{f}"]
            with sp.Fori(0, FPAIRS) as i:
                load(*at(st, i, 0), "k8", w_in(i * W2))
                load(*at(st, i, 1), "k8", w_in(i * W2 + FF))
            st = stages[f"down{f}"]
            with sp.Fori(0, NPAIR) as i:
                load(*at(st, i, 0), "k11", w_out(i * W2))
                load(*at(st, i, 1), "k11", w_out(i * W2, FC // 2))

        def twos(name, col, skip=0, count=None):
            st = {**stages[name], "base": stages[name]["base"] + 2 * skip}
            w, first = col
            take = columns(w)
            with sp.Fori(0, (count or st["count"]) // 2) as i:
                for j in range(2):
                    load(*at(st, i, j), "k8", take(2 * W2 * i + (first + W2 * j)))

        def rows_of(name, w):
            st = stages[name]
            with sp.Fori(0, NPAIR // 2) as i:
                for j in range(2):
                    n, _, par = at(st, i, j)
                    for half in range(2):
                        sp.wait_ge(lo_done, 2 * n + half + 1)
                        sp.dma_start(raw[:, 2 * par + half, :D], w[bass.ds(4 * P * i + P * (2 * j + half), P), :]).then_inc(w_arrived[2 * par + half], 16)

        def two_units(name, sources):
            st = stages[name]
            per = len(sources)
            with sp.Fori(0, HEADS // 8) as v:
                for j, (w, first) in enumerate(2 * sources):
                    load(*at(st, per * v + j // 2, j % 2), "k8", columns(w)(2 * W2 * v + (first + W2 * (j // per))))

        def units(name, sources):
            st = stages[name]
            per = len(sources)
            with sp.Fori(0, HEADS // 4) as u:
                for j, (w, first) in enumerate(sources):
                    load(*at(st, per // 2 * u + j // 2, j % 2), "k8", columns(w)(W2 * u + first))

        for layer in layers:
            if layer.startswith("ffn"):
                ffn(int(layer[3:]))
            if layer == "hgrn":
                two_units("hgrn", [(io["a_w_in"][0], D * part) for part in range(3)])
                twos("hgrn", (io["a_w_in"][0], 3 * D), 3 * A_HEADS // 4, D // W2)
                rows_of("hgrn_out", io["a_w_out"][0])
            if layer == "dil":
                two_units("dil", [(w, D * g) for g in range(GROUPS) for w in (io["b_w_q"][0], io["w_kv"])]
                          + [(io["w_kv"], QKV + D * g) for g in range(GROUPS)])
                rows_of("dil_out", io["b_w_o"][0])
            if layer == "stick":
                units("stick", [(io["sb_w_qkv_2"][0], 0), (io["sb_w_qkv_2"][0], D)])
                twos("stick", (io["sb_w_qkv_2"][0], 2 * D), HEADS // 4, D // W2)
                rows_of("stick_out", io["sb_w_o_2"][0])
            if layer == "swa_kv":
                twos("swa_kv", (io["kv_w_2"], 0))
            if layer == "swa":
                twos("swa", (io["swa_w_q_2"][0], 0))
                rows_of("swa_out", io["swa_w_o_2"][0])
        for t in range(T // P):
            sp.wait_ge(final_copied[t], t + 1)
            sp.dma_start(io["out"][0, P * t:P * (t + 1), :], out_sb[:, t, :]).then_inc(out_stored, 16)
        sp.wait_ge(out_stored, 16 * (T // P))

    @block.tensor
    def _(pe):
        pe.sem_inc(slot_done, 2)

        def products(n, n2, par, kind, hi, lo, fill, bank, wait_x=None, mid=None):
            pe.wait_ge(evac_done, fill + 1)
            k = 0
            total = sum(chunks for _, _, chunks in HALVES[kind])
            for half, (_, _, chunks) in enumerate(HALVES[kind]):
                pe.wait_ge(lo_done, 2 * n + half + 5)
                for k in range(k, k + chunks):
                    if wait_x:
                        pe.wait_ge(wait_x[0], wait_x[1] + k + 1)
                    for m in range(2):
                        out = ps[:, bank, T * m:T * (m + 1)]
                        w = slice(W2 * k + P * m, W2 * k + P * (m + 1))
                        nc.tensor.matmul(out, whi[:, par, w], hi[:, k, :], start=k == 0 and m == 0, stop=False)
                        nc.tensor.matmul(out, whi[:, par, w], lo[:, k, :], start=False, stop=False)
                        mm = nc.tensor.matmul(out, wlo[:, par, w], hi[:, k, :], start=False, stop=k == total - 1 and m == 1)
                k += 1
                if half == 0 and mid:
                    mid()
            mm.then_inc(slot_done, 1)

        def wide_products(n, n2, par, kind, moving, fill, bank, waits, first=True, last=True, chunk0=0, mid=None):
            if first:
                pe.wait_ge(evac_done, fill + 1)
            k = 0
            total = sum(chunks for _, _, chunks in HALVES[kind])
            for half, (_, _, chunks) in enumerate(HALVES[kind]):
                pe.wait_ge(lo_done, 2 * n + half + 5)
                for k in range(k, k + chunks):
                    if k in waits:
                        pe.wait_ge(*waits[k])
                    both = moving[:, chunk0 + k, :, :].rearrange("p s t -> p (s t)")
                    for m in range(2):
                        out = ps[:, bank + m, :]
                        w = slice(W2 * k + P * m, W2 * k + P * (m + 1))
                        nc.tensor.matmul(out, whi[:, par, w], both, start=first and k == 0, stop=False)
                        mm = nc.tensor.matmul(out[:, 0:T], wlo[:, par, w], both[:, 0:T], start=False, stop=last and k == total - 1)
                k += 1
                if half == 0 and mid:
                    mid()
            mm.then_inc(slot_done, 1)

        def sum_squares(e):
            pe.wait_ge(acc_done, NPAIR * (e + 1))
            nc.tensor.matmul(ps[:, BANK_SUM, 0:T], ones, acc[:, 0:T], start=True, stop=False)
            nc.tensor.matmul(ps[:, BANK_SUM, 0:T], ones, acc[:, T:2 * T], start=False, stop=True).then_inc(ss_ready, 1)

        def ffn(f):
            st, e = stages[f"up{f}"], reads[f"up{f}"]

            def body(i, waits):
                for j in range(2):
                    sums = waits and j == 1 and norms[f"up{f}"] != norms.get(before.get(f"up{f}"))
                    wide_products(*at(st, i, j), "k8", xg, st["fill"] + j + 2 * i, UP_BANKS[j], waits,
                                  mid=(lambda: sum_squares(e)) if sums else None)

            body(0, {k: (xg_ready, g_before[e] + k + 1) for k in range(KC)})
            with pe.Fori(1, FPAIRS) as i:
                body(i, {})
            st = stages[f"down{f}"]
            with pe.Fori(0, NPAIR // 2) as i:
                for m in range(2):
                    for j in range(2):
                        k0, k1 = FC // 2 * j, FC // 2 * (j + 1)
                        needs = {2 * q: (hT_ready, FPAIRS * f + q + 2) for q in range(FPAIRS) if k0 <= 2 * q + 1 and 2 * q < k1}
                        waits = {max(k - k0, 0): w for k, w in needs.items()}
                        wide_products(*at(st, 2 * i + m, j), "k11", hT, st["fill"] + m + 2 * i, DOWN_BANKS[m], waits,
                                      first=j == 0, last=j == 1, chunk0=FC // 2 * j)

        def out_slot(name, m, oT, o_base, mid):
            st = stages[name]
            n, par, banks = st["base"] + m, m % 2, OUT_BANKS[name]

            def chunk(k, c):
                out, w = ps[:, banks[c // 2], T * (c % 2):T * (c % 2 + 1)], slice(D * (k % 2) + P * c, D * (k % 2) + P * (c + 1))
                nc.tensor.matmul(out, whi[:, par, w], oT[0][:, k, :], start=k == 0 and c % 2 == 0, stop=False)
                nc.tensor.matmul(out, whi[:, par, w], oT[1][:, k, :], start=False, stop=False)
                return nc.tensor.matmul(out, wlo[:, par, w], oT[0][:, k, :], start=False, stop=k == KC - 1 and c % 2 == 1)

            if m == 0:
                pe.wait_ge(evac_done, st["fill"] + 2)
            for half in range(2):
                k = 2 * m + half
                pe.wait_ge(lo_done, 2 * n + half + 5)
                pe.wait_ge(o_ready, o_base + k + 1)
                if m < NPAIR - 1:
                    for c in range(KC):
                        mm = chunk(k, c)
                    if half == 0:
                        mid()
            if m == NPAIR - 1:
                mid()
                for c in range(KC):
                    chunk(2 * m, c)
                    mm = chunk(2 * m + 1, c)
                    if c % 2 and c < KC - 1:
                        mm.then_inc(out_ready, 1)
            mm.then_inc(slot_done, 1)

        def hgrn():
            st, e = stages["hgrn"], reads["hgrn"]

            def early(t):
                if t % 3 == 0 and 0 < t <= HG_QFI:
                    u = t // 3 - 1
                    pe.wait_ge(evac_done, st["fill"] + t - 1 + 3)
                    if u:
                        pe.wait_ge(hg_vt, u)
                        done = sum(start + 5 < t for start in HG_START)
                        if done:
                            pe.wait_ge(hg_oln, done)
                    else:
                        pe.wait_ge(aux_ready, 1)
                    for c in range(2):
                        for tt in range(T // P):
                            tr = nc.tensor.transpose(ps[:, HG_VBANK, 2 * P * tt + P * c:2 * P * tt + P * (c + 1)],
                                                     hg_raw[1][:, T * c + P * tt:T * c + P * (tt + 1)], ident)
                    tr.then_inc(hg_vtr, 1)

            def late(t):
                for hd in hg_heads(t, 5):
                    pe.wait_ge(hg_os2, hd + 1)
                    pe.wait_ge(hg_vt, min(HG_START[hd] + 5, HG_QFI) // 3)
                    if HG_START[hd] + 5 >= HG_SLOTS:
                        pe.wait_ge(hg_oc, hd + 1)
                    if hd:
                        pe.wait_ge(hg_oln, hd)
                    nc.tensor.matmul(hg_sums(hd), ones, hg_osq[:, :], start=True, stop=True).then_inc(hg_oss, 1)
                for hd in hg_heads(t, 4):
                    par, col = hd // 2 % 2, slice(P * (hd % 2), P * (hd % 2 + 1))
                    pe.wait_ge(hg_Pr, hd + 1)
                    pe.wait_ge(hg_Pcr, hd + 1)
                    pe.wait_ge(hg_vt, hd // 2 + 1)
                    if hd:
                        pe.wait_ge(hg_oc, hd)
                        if HG_START[hd - 1] + 5 >= HG_SLOTS:
                            pe.wait_ge(hg_oln, hd)
                    o = ps[:, HG_OUT, 0:T]
                    nc.tensor.matmul(o[:, 0:P], hg_v[:, par, 0, col], hg_P[:, 0:P], start=True, stop=True)
                    nc.tensor.matmul(o[:, P:T], hg_v[:, par, 1, col], hg_P[:, P:T], start=True, stop=False)
                    nc.tensor.matmul(o[:, P:T], hg_v[:, par, 0, col], hg_Pc[:, :], start=False, stop=True).then_inc(hg_o, 1)
                for hd in hg_heads(t, 3):
                    par, first = hd // 2 % 2, T * (hd % 2)
                    pe.wait_ge(hg_qd, hd + 1)
                    pe.wait_ge(hg_s, 3 * (hd // 2) + 3)
                    if hd:
                        pe.wait_ge(hg_sm, LEVELS * hd)
                        pe.wait_ge(hg_Pcr, hd)
                    for half in range(2):
                        tok = slice(P * half, P * (half + 1))
                        for level in range(LEVELS - 1):
                            at0 = P * level + P // 2 * half
                            nc.tensor.matmul(hg_all[:, at0:at0 + P // 2], hg_E[:, hd % 2, level, tok], hg_half(hg_E[:, hd % 2, level, tok], level, 1),
                                             start=True, stop=True)
                        own = slice(first + P * half, first + P * (half + 1))
                        nc.tensor.matmul(hg_all[:, HG_OWN + P * half:HG_OWN + P * (half + 1)], hg_k[:, par, own], hg_q[:, par, own],
                                         start=True, stop=True)
                    nc.tensor.matmul(hg_all[:, HG_CROSS:HG_CROSS + P], hg_E[:, hd % 2, LEVELS - 1, 0:P], hg_E[:, hd % 2, LEVELS - 1, P:T],
                                     start=True, stop=True).then_inc(hg_S, 1)

            for t in range(HG_TICKS):
                n = st["base"] + t
                if t < HG_SLOTS:
                    products(n, n // 2, n % 2, "k8", xg_hi, xg_lo, st["fill"] + t, t % 2,
                             wait_x=(xg_ready, g_before[e]) if t == 0 else None, mid=lambda: early(t))
                else:
                    if t == HG_SLOTS:
                        pe.wait_ge(hg_vt, HG_UNITS)
                        pe.wait_ge(hg_oln, sum(start + 5 < HG_SLOTS for start in HG_START))
                    out_slot("hgrn_out", t - HG_SLOTS, hg_oT, 0, lambda: late(t))
                    continue
                if t == 0:
                    sum_squares(e)
                    pe.wait_ge(const_late, 16)
                    pe.wait_ge(late_arrived, 16 * LATE_LOADS)
                    late_rows = GAIN_ROWS - FIRST_ROWS
                    nc.tensor.transpose(ps[:, HG_VBANK, 0:late_rows], rows_late[0:late_rows, :], ident[0:late_rows, 0:late_rows])
                    nc.tensor.transpose(ps[:, HG_VBANK, P:P + AUX], aux_in[0:AUX, :], ident[0:AUX, 0:AUX]).then_inc(late_turned, 1)
                    pe.wait_ge(bias_masked, 2)
                    for g in range(GROUPS):
                        mm = nc.tensor.matmul(ps[:, HG_SCORES + g, 0:ROW], rbx8[:, P * g:P * (g + 1)], onehot[:, ROW * g:ROW * (g + 1)],
                                              start=True, stop=True)
                    mm.then_inc(bias_made, 1)
                late(t)


        def dil():
            st, e, ek = stages["dil"], reads["dil"], reads["dil"] - 1

            def steps(point):
                slot = dl_projected(point)
                if slot is not None and not dl_slot(slot)[2]:
                    n = dl_qk_number(slot)
                    pe.wait_ge(dl_sqd, n + 1)
                    if n:
                        pe.wait_ge(dl_ln, n)
                    nc.tensor.matmul(ps[:, BANK_SUM, :], const("blk64"), dl_sq[:, :], start=True, stop=True).then_inc(dl_ss, 1)
                elif slot is not None:
                    n = dl_v_number(slot)
                    pe.wait_ge(evac_done, st["fill"] + slot + 3)
                    if n:
                        pe.wait_ge(dl_vt, n)
                    for c in range(2):
                        for tt in range(T // P):
                            tr = nc.tensor.transpose(ps[:, DL_VBANK, 2 * P * tt + P * c:2 * P * tt + P * (c + 1)],
                                                     dl_t[:, slot % 2, T * c + P * tt:T * c + P * (tt + 1)], ident)
                    tr.then_inc(dl_vtr, 1)
                for two in dl_due(point, DL_PV):
                    u, c = divmod(two, 2)
                    pe.wait_ge(dl_PTd, 2 * two + 2)
                    pe.wait_ge(dl_vt, GROUPS * (u + 1))
                    if c == 0 and u:
                        pe.wait_ge(o_ready, 8 + 2 * u)
                    for g in range(GROUPS):
                        for tile in range(2):
                            for odd in range(2):
                                v = dl_v[:, u % 2, g, tile, HD * (2 * c + odd):HD * (2 * c + odd + 1)]
                                at0, n = (T * g, T) if tile == 0 else (GROUPS * T + P * g, P)
                                mm = nc.tensor.matmul(ps[HD * odd:HD * (odd + 1), DL_OUT, T * (c + 1) - n:T * (c + 1)], v,
                                                      dl_PT[:, odd, at0:at0 + n], start=g == 0 and tile == 0 and c == 0,
                                                      stop=g == GROUPS - 1 and tile == 1, tile_position=(0, HD * odd), skip_group_check=True)
                    mm.then_inc(dl_pv, 1)
                for hd in dl_due(point, DL_TURN):
                    u = hd // 4
                    pe.wait_ge(dl_sc0, hd + 1)
                    pe.wait_ge(dl_sc1, hd + 1)
                    pe.wait_ge(dl_biased, 2 * min(hd + 2, 4 * u + 4))
                    if hd:
                        pe.wait_ge(dl_PTd, hd)
                    S = dl_S[:, hd % 2, :]
                    for g in range(GROUPS):
                        for out, own in ((T * g, dl_blocks(S, P)[:, g, :]), (T * g + P, dl_blocks(S, T)[:, g, 0:P]),
                                         (GROUPS * T + P * g, dl_blocks(S, T)[:, g, P:T])):
                            tr = nc.tensor.transpose(dl_ps[:, out:out + P], own, ident)
                    tr.then_inc(dl_turned, 1)
                for hd in dl_due(point, DL_SCORES):
                    u, a = divmod(hd, 4)
                    pe.wait_ge(dl_qkd, 2 * GROUPS * (u + 1))
                    if hd:
                        pe.wait_ge(dl_biased, 2 * hd)
                    if hd > 1 or a > 1:
                        pe.wait_ge(dl_PTd, hd if a == 0 else hd - 1)
                    first = T * (a // 2)
                    for tile, keys in ((1, T), (0, P)):
                        for g in range(GROUPS):
                            mm = nc.tensor.matmul(dl_blocks(dl_ps, keys)[:, g, :], dl_q[:, g, a % 2, first + P * tile:first + P * (tile + 1)],
                                                  dl_k[:, u % 2, g, first:first + keys], start=True, stop=True)
                    mm.then_inc(dl_scored, 1)

            pe.wait_ge(xk_ready, k_before[ek] + KC)
            for t in range(DL_TICKS):
                if t < DL_SLOTS:
                    n = st["base"] + t
                    u, j, values = dl_slot(t)
                    hi, lo = operand["k" if values or j % 2 else "g"]
                    products(n, n // 2, n % 2, "k8", hi, lo, st["fill"] + t, t % 2,
                             wait_x=(xg_ready, g_before[e]) if t == 0 else None, mid=lambda: steps(2 * t))
                    if t == 0:
                        sum_squares(e)
                else:
                    if t == DL_SLOTS:
                        pe.wait_ge(dl_ln, 2 * GROUPS * DL_UNITS)
                        pe.wait_ge(dl_vt, GROUPS * DL_UNITS)
                    out_slot("dil_out", t - DL_SLOTS, dl_oT, 8, lambda: steps(2 * t))
                steps(2 * t + 1)


        def stick():
            st, e = stages["stick"], reads["stick"]

            def early(t):
                for u in sk_sums_at(t):
                    pe.wait_ge(sk_spd, u + 1)
                    for odd in range(2):
                        nc.tensor.matmul(sk_second(sk_all, odd), const("neg_suffix"), sk_second(sk_sp, odd),
                                         start=False, stop=True, skip_group_check=True)
                        nc.tensor.matmul(sk_first(sk_all, odd), const("neg_suffix"), sk_first(sk_sp, odd),
                                         start=False, stop=False, skip_group_check=True)
                        mm = nc.tensor.matmul(sk_first(sk_all, odd)[:, :, P:T], const("neg_ones"), sk_second(sk_sp, odd),
                                              start=False, stop=True, skip_group_check=True)
                    mm.then_inc(sk_sum, 1)
                for u in sk_values_at(t):
                    pe.wait_ge(evac_done, st["fill"] + SK_QK + u + 3)
                    if u:
                        pe.wait_ge(sk_vt, u)
                    for c in range(2):
                        for tt in range(T // P):
                            tr = nc.tensor.transpose(ps[:, SK_VBANK, 2 * P * tt + P * c:2 * P * tt + P * (c + 1)],
                                                     sk_t[:, u % 2, T * c + P * tt:T * c + P * (tt + 1)], ident)
                    tr.then_inc(sk_vtr, 1)

            def late(t):
                for u in sk_scores_at(t):
                    pe.wait_ge(evac_done, st["fill"] + 2 * u + 1 + 3)
                    if u:
                        pe.wait_ge(sk_wr, u)
                    mask = sk_mask[:, :].unsqueeze(1).broadcast_to([P, 2, P])
                    pe.wait_ge(sk_const, 2)
                    for c in range(2):
                        for odd in range(2):
                            q, first = sk_q[:, u % 2, odd, T * c:T * (c + 1)], T * c
                            nc.tensor.matmul(sk_first(sk_all, odd)[:, c, :], sk_k[:, u % 2, first:first + P], q,
                                             start=c == 0, stop=False, skip_group_check=True)
                            nc.tensor.matmul(sk_second(sk_all, odd)[:, c, :], sk_k[:, u % 2, first + P:first + T], q[:, P:T],
                                             start=c == 0, stop=False, skip_group_check=True)
                    for odd in range(2):
                        for out in (sk_first(sk_all, odd)[:, :, 0:P], sk_second(sk_all, odd)):
                            mm = nc.tensor.matmul(out, sk_ident[:, :], mask, start=False, stop=True, skip_group_check=True)
                    mm.then_inc(sk_z, 1)
                for u in sk_values_at(t):
                    pe.wait_ge(sk_wr, u + 1)
                    pe.wait_ge(sk_vt, u + 1)
                    if u:
                        pe.wait_ge(o_ready, 16 + 2 * u)
                    for c in range(2):
                        for tile, weights in enumerate((sk_first, sk_second)):
                            for odd in range(2):
                                w = weights(sk_w[:, u, :], odd)[:, c, :]
                                mm = nc.tensor.matmul(ps[HD * odd:HD * (odd + 1), SK_OUT, T * c + P * tile:T * (c + 1)],
                                                      sk_v[:, u % 2, tile, HD * (2 * c + odd):HD * (2 * c + odd + 1)], w,
                                                      start=c == 0 and tile == 0, stop=tile == 1, tile_position=(0, HD * odd),
                                                      skip_group_check=True)
                    mm.then_inc(sk_pv, 1)

            for t in range(SK_TICKS):
                n = st["base"] + t
                if t < SK_SLOTS:
                    products(n, n // 2, n % 2, "k8", xg_hi, xg_lo, st["fill"] + t, t % 2,
                             wait_x=(xg_ready, g_before[e]) if t == 0 else None, mid=lambda: early(t))
                else:
                    if t == SK_SLOTS:
                        pe.wait_ge(sk_wr, SK_UNITS)
                    out_slot("stick_out", t - SK_SLOTS, sk_oT, 16, lambda: early(t))
                if t == 0:
                    sum_squares(e)
                late(t)


        def swa_kv():
            st, e = stages["swa_kv"], reads["swa_kv"]
            for j in range(2):
                products(st["base"] + j, st["base"] // 2, j, "k8", xk_hi, xk_lo, st["fill"] + j, j,
                         wait_x=(xk_ready, k_before[e]) if j == 0 else None)
                if j == 0:
                    sum_squares(e)
            pe.wait_ge(evac_done, st["fill"] + 3)
            nc.tensor.matmul(ps[:, KV_ROT, :], const("rot"), kv_t[:, :], start=True, stop=True).then_inc(kv_rot, 1)
            pe.wait_ge(evac_done, st["fill"] + 1 + 3)
            for c in range(2):
                for tt in range(T // P):
                    tr = nc.tensor.transpose(ps[:, KV_VBANK, 2 * P * tt + P * c:2 * P * tt + P * (c + 1)],
                                             kv_v[:, T * c + P * tt:T * c + P * (tt + 1)], ident)
            tr.then_inc(kv_vtr, 1)
            pe.wait_ge(kv_sum, 1)
            for u in range(KV_HEADS):
                dup = nc.tensor.matmul(ps[:, KV_DUP + u // 2, T * (u % 2):T * (u % 2 + 1)], const(f"dup{u % 2}"),
                                       kv_c[:, T * (u // 2):T * (u // 2 + 1)], start=True, stop=True)
            dup.then_inc(kv_dup, 1)


        def swa():
            st, e = stages["swa"], reads["swa"]

            def early(t):
                for u in sw_at(t, 1):
                    pe.wait_ge(evac_done, st["fill"] + u + 3)
                    if u:
                        pe.wait_ge(sw_sin, u)
                    if u > 2:
                        pe.wait_ge(o_ready, 24 + 2 * (u - 2))
                    nc.tensor.matmul(ps[:, SW_OUT, :], const("rot"), sw_t[:, u % 2, :], start=True, stop=True).then_inc(sw_rot, 1)
                for u in sw_at(t, 3):
                    pe.wait_ge(sw_sc0, u + 1)
                    pe.wait_ge(sw_sc1, u + 1)
                    if u + 1 < SW_UNITS:
                        pe.wait_ge(sw_masked, 8 * (u + 2))
                    for a in range(4):
                        for tile in range(2):
                            nc.tensor.transpose(sw_keys0(sw_turn, a)[:, P * tile:P * (tile + 1)], sw_biased(u, a, tile)[:, 0:P], ident)
                        tr = nc.tensor.transpose(sw_keys1(sw_turn, a), sw_biased(u, a, 1)[:, P:T], ident)
                    tr.then_inc(sw_turned, 1)

            def late(t):
                for u in sw_at(t, 3):
                    pe.wait_ge(sw_PTd, u + 1)
                    if u:
                        pe.wait_ge(o_ready, 24 + 2 * u)
                    pe.wait_ge(sw_sin, min(u + 3, SW_UNITS))
                    for c in range(2):
                        for tile, probs in enumerate((sw_keys0, sw_keys1)):
                            for odd in range(2):
                                mm = nc.tensor.matmul(ps[HD * odd:HD * (odd + 1), SW_OUT, T * c + P * tile:T * (c + 1)],
                                                      v2[:, tile, HD * u:HD * (u + 1)], probs(sw_PT, 2 * c + odd),
                                                      start=c == 0 and tile == 0, stop=tile == 1, tile_position=(0, HD * odd),
                                                      skip_group_check=True)
                    mm.then_inc(sw_pv, 1)
                for u in sw_at(t, 1):
                    pe.wait_ge(sw_qr, u + 1)
                    if u > 1:
                        pe.wait_ge(sw_PTd, u - 1)
                    if u:
                        pe.wait_ge(sw_masked, 8 * u)
                    for a in range(4):
                        for tile, keys in ((1, T), (0, P)):
                            first = T * (a // 2) + P * tile
                            mm = nc.tensor.matmul(sw_scores(a, tile), sw_q[:, u % 2, a % 2, first:first + P], kdup[:, u, 0:keys],
                                                  start=True, stop=True)
                    mm.then_inc(sw_scored, 1)

            pe.wait_ge(kv_dupd, 1)
            pe.wait_ge(kv_vt, 1)
            for t in range(SW_TICKS):
                if t < SW_UNITS:
                    n = st["base"] + t
                    products(n, n // 2, n % 2, "k8", xg_hi, xg_lo, st["fill"] + t, t % 2,
                             wait_x=(xg_ready, g_before[e]) if t == 0 else None, mid=lambda: early(t))
                    if t == 0:
                        sum_squares(e)
                else:
                    out_slot("swa_out", t - SW_UNITS, sw_oT, 24, lambda: early(t))
                late(t)

        pe.wait_ge(const_in, 16)
        pe.wait_ge(rows_arrived, 16)
        nc.tensor.transpose(ps[:, BANK_SUM, 0:FIRST_ROWS], rows_in[0:FIRST_ROWS, :], ident[0:FIRST_ROWS, 0:FIRST_ROWS]).then_inc(rows_turned, 1)
        pe.wait_ge(x_arrived, 16)
        for m in range(NPAIR):
            for c in range(2):
                for t in range(T // P):
                    tr = nc.tensor.transpose(ps[:, X_BANKS[m], T * c + P * t:T * c + P * (t + 1)],
                                             x_in[:, t, P * (2 * m + c):P * (2 * m + c + 1)], ident)
            tr.then_inc(x_turned, 1)
        pe.wait_ge(gains_ready, 1)
        for layer in layers:
            if layer.startswith("ffn"):
                ffn(int(layer[3:]))
            if layer == "hgrn":
                hgrn()
            if layer == "dil":
                dil()
            if layer == "stick":
                stick()
            if layer == "swa_kv":
                swa_kv()
            if layer == "swa":
                swa()
        for c in range(KC):
            pe.wait_ge(final_y, c + 1)
            for t in range(T // P):
                tr = nc.tensor.transpose(ps[:, OUT_TURNED[2 * t + c // 4], P * (c % 4):P * (c % 4 + 1)],
                                         fin[:, c, P * t:P * (t + 1)], ident)
        tr.then_inc(final_turned, 1)
        pe.wait_ge(acc_done, NPAIR * (LAST + 1))
        for t in range(T // P):
            for c in range(2):
                mm = nc.tensor.matmul(ps[:, BANK_LAST, t:t + 1], acc[:, T * c + P * t:T * c + P * (t + 1)], ones[:, 0:1],
                                      start=c == 0, stop=c == 1)
        mm.then_inc(ss_ready, 1)

    @block.scalar
    def _(act):
        own = CONST_AT["blk64"][0]
        act.dma_start(cst[:, 0:own], io["consts"][:, 0:own]).then_inc(const_in, 16)
        rows = lambda name, n: bass.AP(io[name].tensor, 0, [[P, n], [1, P]])
        act.dma_start(rows_in[0:FIRST_ROWS, :], rows("norm_gain", FIRST_ROWS)).then_inc(rows_arrived, 16)
        nc.scalar.preload_act_table_set("natural_log_exp_and_others")

        def split_high(n, n2, par, kind, halves=(0, 1)):
            if kind is None:
                return
            act.wait_ge(slot_done, n + 1)
            for half in halves:
                off, size, _ = HALVES[kind][half]
                act.wait_ge(w_arrived[2 * par + half], 16 * n2 + 16)
                nc.scalar.activation(whi[:, par, off:off + size], raw[:, 2 * par + half, :size], ACT.Copy).then_inc(hi_done, 1)

        def high_x(e, m, fill):
            act.wait_ge(evac_done, fill + 3)
            for which, col in updates[e][1]:
                for c in range(2 * m, 2 * m + 2):
                    nc.scalar.activation(operand[which][0][:, c, :], x[:, c, :], ACT.Copy,
                                         scale=gains[:, col + c:col + c + 1]).then_inc(xhi_done, 1)
            for c in range(2 * m, 2 * m + 2) if e == LAST else ():
                col = GAIN["final_norm_2"] + c
                nc.scalar.activation(fin[:, c, :], x[:, c, :], ACT.Copy, scale=gains[:, col:col + 1]).then_inc(final_y, 1)
            if m == NPAIR - 1:
                act.wait_ge(acc_done, NPAIR * e)
                nc.scalar.activation(sq_last[:, :], xpair(m), ACT.Square).then_inc(sq_last_done, 1)

        def norm(e, cols=T):
            act.wait_ge(ms_ready, e + 1)
            nc.scalar.activation(ms_ln[:, 0:cols], ms[:, 0:cols], ACT.Ln).then_inc(ms_ln_done, 1)
            act.wait_ge(ms_ln_done, e + 1)
            nc.scalar.activation(r0[:, 0:cols], ms_ln[:, 0:cols], ACT.Exp, scale=-0.5).then_inc(r0_ready, 1)

        def stage_norm(name):
            if norms[name] != norms.get(before.get(name)):
                norm(norms[name])

        def ffn(f):
            st = stages[f"up{f}"]

            def body(i):
                p = FPAIRS * f + i
                split_high(*ahead_of(st, i, 0), (0,))
                first = isinstance(i, int) and i == 0
                act.wait_ge(slot_done, at(st, i, 0)[0] + 3)
                act.wait_ge(gr_done, p + 1)
                nc.scalar.activation(pair(gate[:, :]), wide(UP_BANKS[0], 0), ACT.Copy).then_inc(gate_copied, 1)
                if first:
                    split_high(*ahead_of(st, i, 0), (1,))
                    stage_norm(f"up{f}")
                    split_high(*ahead_of(st, i, 1), (0,))
                act.wait_ge(gate_made, p + 1)
                nc.scalar.activation(gate_e[:, :], gate[:, :], ACT.Exp, scale=-1.0).then_inc(gate_exp, 1)
                if not first:
                    split_high(*ahead_of(st, i, 0), (1,))
                act.wait_ge(gate_den, p + 1)
                nc.scalar.activation(gate_e[:, :], gate_e[:, :], ACT.Ln).then_inc(gate_ln, 1)
                act.wait_ge(gate_ln, p + 1)
                nc.scalar.activation(gate_s[:, :], gate_e[:, :], ACT.Exp, scale=-1.0).then_inc(sig_ready, 1)
                if not first:
                    split_high(*ahead_of(st, i, 1), (0,))
                act.wait_ge(slot_done, at(st, i, 1)[0] + 3)
                act.wait_ge(hT_ready, p + 1)
                nc.scalar.activation(pair(h[:, :]), wide(UP_BANKS[1], 0), ACT.Copy).then_inc(h_copied, 1)
                split_high(*ahead_of(st, i, 1), (1,))
                act.wait_ge(h_made, p + 1)
                nc.scalar.activation(hidden(i, 0), pair(h[:, :]), ACT.Copy).then_inc(hhi_done, 1)

            first_to_last(act, FPAIRS, body)
            st = stages[f"down{f}"]
            for m in range(NPAIR):
                split_high(*ahead_of(st, m, 0))
                split_high(*ahead_of(st, m, 1), (0,) if f else ())
                high_x(update_of[f"down{f}"], m, st["fill"] + m)
                split_high(*ahead_of(st, m, 1), (1,) if f else (0, 1))

        def out_slot(name, m):
            st = stages[name]
            for pair_of in range(NPAIR) if m == NPAIR - 1 else ():
                high_x(update_of[name], pair_of, st["fill"] + pair_of)
            split_high(*ahead_of(st, m // 2, m % 2))

        def hgrn():
            st = stages["hgrn"]

            def sigmoid_exp(n, out, source, scale):
                nc.scalar.activation(out, source, ACT.Exp, scale=scale).then_inc(hg_e, 1)

            def sigmoid_end(n, tile):
                act.wait_ge(hg_d, n)
                nc.scalar.activation(tile, tile, ACT.Ln).then_inc(hg_l, 1)
                act.wait_ge(hg_l, n)
                nc.scalar.activation(tile, tile, ACT.Exp, scale=-1.0).then_inc(hg_s, 1)

            def decays(t):
                for hd in hg_heads(t, 1):
                    act.wait_ge(hg_dif, hd + 1)
                    nc.scalar.activation(hg_E[:, hd % 2, :, :], hg_E[:, hd % 2, :, :], ACT.Exp).then_inc(hg_dec, 1)

            def late(t):
                for hd in hg_heads(t, 5):
                    act.wait_ge(hg_oss, hd + 1)
                    if hd:
                        act.wait_ge(hg_on, hd)
                    nc.scalar.activation(hg_rms[:, :], hg_sums(hd), ACT.Ln, scale=1.0 / P, bias=eps[:, :]).then_inc(hg_oln, 1)
                    act.wait_ge(hg_oln, hd + 1)
                    nc.scalar.activation(hg_rms[:, :], hg_rms[:, :], ACT.Exp, scale=-0.5).then_inc(hg_or, 1)
                for u in hg_split(t):
                    act.wait_ge(hg_og, u + 1)
                    nc.scalar.activation(hg_oT[0][:, 2 * u:2 * u + 2, :], hg_out[:, 2 * u:2 * u + 2, :], ACT.Copy).then_inc(hg_ohi, 1)
                for hd in hg_heads(t, 4):
                    act.wait_ge(hg_o, hd + 1)
                    nc.scalar.activation(hg_out[:, hd, :], ps[:, HG_OUT, 0:T], ACT.Copy).then_inc(hg_oc, 1)

            def store_bias(g, quarter):
                rows = REPEAT // 2
                act.dma_start(bass.AP(bias_dram.tensor, HEADS * P * ROW * g + rows * ROW * quarter, [[4 * rows * ROW, P], [ROW, rows], [1, ROW]]),
                              bias_rows[:, g:g + 1, :].broadcast_to([P, rows, ROW])).then_inc(bias_stored, 16)

            at_mask = CONST_AT["hg_mask"][0]
            act.dma_start(hg_mask[:, :, :].rearrange("p l t -> p (l t)"), io["consts"][:, at_mask:at_mask + (LEVELS - 1) * P]).then_inc(hg_mask_in, 16)
            for t in range(HG_TICKS):
                if t == 1:
                    act.wait_ge(lb_steps, 2)
                    nc.scalar.activation(lbt[:, 0:2, :], lbt[:, 0:2, :], ACT.Exp).then_inc(lb_exp, 1)
                    act.wait_ge(bias_copied, 1)
                if 0 < t <= BIAS_STORES:
                    store_bias((t - 1) // 4, (t - 1) % 4)
                if t < HG_SLOTS:
                    u, j = hg_slot(t)
                    n = st["base"] + t
                    if t % 3 == 0 and 0 < t <= HG_QFI:
                        v = t // 3 - 1
                        act.wait_ge(hg_vtr, v + 1)
                        if v > 1:
                            act.wait_ge(hg_o, 2 * v - 2)
                        nc.scalar.activation(hg_v[:, v % 2, :, :], ps[:, HG_VBANK, :].rearrange("p (a b) -> p a b", a=2), ACT.Copy).then_inc(hg_vt, 1)
                    if j == 2:
                        act.wait_ge(hg_f, 2 * u + 2)
                        nc.scalar.activation(hg_exp[1][:, :], hg_exp[1][:, :], ACT.Ln).then_inc(hg_lf, 1)
                    if t == 0:
                        split_high(*ahead_of(st, 0, 0), (0,))
                        stage_norm("hgrn")
                    split_high(n + 2, (n + 2) // 2, n % 2, kinds[n + 2], (0, 1) if t else (1,))
                    if j != 2:
                        act.wait_ge(evac_done, st["fill"] + t + 3)
                    if j == 0:
                        if u:
                            act.wait_ge(hg_qs, u)
                        sigmoid_exp(3 * u + 1, hg_exp[0][:, :], hg_raw[0][:, :], -1.0)
                    if j == 1:
                        if u:
                            act.wait_ge(hg_cum, 2 * u)
                            act.wait_ge(hg_ckd, 2 * u)
                        sigmoid_exp(3 * u + 2, hg_exp[1][:, :], hg_raw[1][:, :], -1.0)
                        sigmoid_exp(3 * u + 3, hg_exp[2][:, :], hg_raw[1][:, :], 1.0)
                    if j == 3:
                        act.wait_ge(hg_qs, HG_UNITS)
                        if u:
                            act.wait_ge(hg_gs, u)
                        sigmoid_exp(HG_QFI + u + 1, hg_exp[0][:, :], hg_raw[u % 2][:, :], -1.0)
                    if t == HG_START[0] + 1:
                        decays(t)
                    late(t)
                    if j == 0:
                        sigmoid_end(3 * u + 1, hg_exp[0][:, :])
                    if j == 1:
                        sigmoid_end(3 * u + 2, hg_exp[1][:, :])
                        if u == 0:
                            act.wait_ge(lb_ready, 7)
                            nc.scalar.activation(ln_oml[:, :], lbt[:, 3, :], ACT.Ln).then_inc(hg_ln, 1)
                            act.wait_ge(hg_ln, 1)
                        if u > 1:
                            act.wait_ge(hg_S, 2 * u - 2)
                        act.wait_ge(hg_d, 3 * u + 3)
                        nc.scalar.activation(hg_exp[2][:, :], hg_exp[2][:, :], ACT.Ln).then_inc(hg_l, 1)
                        act.wait_ge(hg_l, 3 * u + 3)
                        for a in range(2):
                            cols = slice(T * a, T * (a + 1))
                            ex = nc.scalar.activation(hg_k[:, u % 2, cols], hg_exp[2][:, cols], ACT.Exp, scale=-1.0, bias=ln_oml[:, 2 * u + a:2 * u + a + 1])
                        ex.then_inc(hg_s, 1)
                    if j == 3:
                        sigmoid_end(HG_QFI + u + 1, hg_exp[0][:, :])
                    if t != HG_START[0] + 1:
                        decays(t)
                else:
                    late(t)
                    out_slot("hgrn_out", t - HG_SLOTS)
            act.wait_ge(bias_stored, 16 * BIAS_STORES)


        def dil():
            st = stages["dil"]

            def load_bias(hd):
                src = bass.AP(bias_dram.tensor, hd * P * ROW + P - 1, [[ROW - 1, P], [HEADS * P * ROW, GROUPS], [1, T]])
                act.dma_start(dl_bias[:, hd % 2, :, :], src).then_inc((dl_bias_in0, dl_bias_in1)[hd % 2], 16)

            def steps(point):
                slot = dl_projected(point)
                if slot is not None and not dl_slot(slot)[2]:
                    n = dl_qk_number(slot)
                    act.wait_ge(dl_ss, n + 1)
                    if n:
                        act.wait_ge(dl_qkd, n)
                    nc.scalar.activation(dl_rr[:, :], ps[:, BANK_SUM, :], ACT.Ln, scale=1.0 / HD, bias=eps[:, :]).then_inc(dl_ln, 1)
                    act.wait_ge(dl_ln, n + 1)
                    nc.scalar.activation(dl_rr[:, :], dl_rr[:, :], ACT.Exp, scale=-0.5).then_inc(dl_rrd, 1)
                elif slot is not None:
                    n, u = dl_v_number(slot), dl_slot(slot)[0]
                    act.wait_ge(dl_vtr, n + 1)
                    if u > 1:
                        act.wait_ge(dl_pv, 2 * (u - 1))
                    nc.scalar.activation(dl_v[:, u % 2, n % GROUPS, :, :], ps[:, DL_VBANK, :].rearrange("p (a b) -> p a b", a=2),
                                         ACT.Copy).then_inc(dl_vt, 1)
                for two in dl_due(point, DL_PV):
                    u, c = divmod(two, 2)
                    if c == 1:
                        act.wait_ge(dl_pv, two + 1)
                        nc.scalar.activation(flat(dl_oT[0][:, 2 * u:2 * u + 2, :]), ps[:, DL_OUT, :], ACT.Copy).then_inc(dl_ohi, 1)
                for hd in dl_due(point, DL_TURN):
                    act.wait_ge(dl_turned, hd + 1)
                    if hd > 1:
                        act.wait_ge(dl_pv, hd // 2)
                    nc.scalar.activation(dl_PT[:, hd % 2, :], dl_ps, ACT.Copy).then_inc(dl_PTd, 1)
                for hd in dl_due(point, DL_SCORES):
                    act.wait_ge(dl_neg, hd + 1)
                    S = dl_S[:, hd % 2, :]
                    for tile, keys in ((1, T), (0, P)):
                        ex = nc.scalar.activation(dl_blocks(S, keys), dl_blocks(S, keys), ACT.Exp, bias=dl_nmax[:, hd % 2, tile:tile + 1],
                                                  accum_out=dl_sum[:, hd % 2, tile:tile + 1])
                    ex.then_inc(dl_exp, 1)
                    if hd + 2 < HEADS:
                        load_bias(hd + 2)

            act.wait_ge(bias_stored, 16 * BIAS_STORES)
            for hd in range(2):
                load_bias(hd)
            for t in range(DL_TICKS):
                steps(2 * t)
                if t < DL_SLOTS:
                    n = st["base"] + t
                    if t == 0:
                        split_high(*ahead_of(st, 0, 0), (0,))
                        stage_norm("dil")
                    split_high(n + 2, (n + 2) // 2, n % 2, kinds[n + 2], (0, 1) if t else (1,))
                else:
                    out_slot("dil_out", t - DL_SLOTS)
                steps(2 * t + 1)


        def stick():
            st = stages["stick"]

            def early(t):
                for u in sk_sums_at(t):
                    act.wait_ge(sk_sum, u + 1)
                    nc.scalar.activation(sk_w[:, u, :], sk_all, ACT.Exp).then_inc(sk_wr, 1)
                for u in sk_values_at(t):
                    act.wait_ge(sk_vtr, u + 1)
                    if u > 1:
                        act.wait_ge(sk_pv, u - 1)
                    nc.scalar.activation(sk_v[:, u % 2, :, :], ps[:, SK_VBANK, :].rearrange("p (a b) -> p a b", a=2), ACT.Copy).then_inc(sk_vt, 1)

            def late(t):
                for u in sk_scores_at(t):
                    act.wait_ge(sk_z, u + 1)
                    if u:
                        act.wait_ge(sk_spd, u)
                    nc.scalar.activation(sk_e[:, :], sk_all, ACT.Abs).then_inc(sk_abs, 1)
                    act.wait_ge(sk_abs, u + 1)
                    nc.scalar.activation(sk_e[:, :], sk_e[:, :], ACT.Exp, scale=-1.0).then_inc(sk_ex, 1)
                    act.wait_ge(sk_ex, u + 1)
                    nc.scalar.activation(sk_e[:, :], sk_e[:, :], ACT.Ln, bias=1.0).then_inc(sk_ln, 1)
                for u in sk_values_at(t):
                    act.wait_ge(sk_pv, u + 1)
                    nc.scalar.activation(flat(sk_oT[0][:, 2 * u:2 * u + 2, :]), ps[:, SK_OUT, :], ACT.Copy).then_inc(sk_ohi, 1)

            for t in range(SK_TICKS):
                n = st["base"] + t
                early(t)
                if t < SK_SLOTS:
                    if t == 0:
                        split_high(*ahead_of(st, 0, 0), (0,))
                        stage_norm("stick")
                        for tile, name in ((sk_mask, "neg_mask"), (sk_ident, "ident")):
                            nc.scalar.activation(tile[:, :], const(name), ACT.Copy).then_inc(sk_const, 1)
                    split_high(n + 2, (n + 2) // 2, n % 2, kinds[n + 2], (0, 1) if t else (1,))
                else:
                    out_slot("stick_out", t - SK_SLOTS)
                late(t)


        def swa_kv():
            st = stages["swa_kv"]
            cos = CONST_AT["cos"][0]
            act.dma_start(rope[:, :, :].rearrange("p a t -> p (a t)"), io["consts"][:, cos:cos + 2 * T]).then_inc(kv_rope_in, 16)
            mask = CONST_AT["swa_mask"][0]
            act.dma_start(swa_mask[:, :], io["consts"][:, mask:mask + T]).then_inc(kv_rope_in, 16)
            for j in range(2):
                split_high(*ahead_of(st, 0, j), (0,))
                if j == 0:
                    stage_norm("swa_kv")
                split_high(*ahead_of(st, 0, j), (1,))
            act.wait_ge(kv_vtr, 1)
            nc.scalar.activation(v2[:, :, :], ps[:, KV_VBANK, :].rearrange("p (a b) -> p a b", a=2), ACT.Copy).then_inc(kv_vt, 1)
            act.wait_ge(kv_dup, 1)
            nc.scalar.activation(flat(kdup[:, :, :]), ps[:, KV_DUP:KV_DUP + 2, :].rearrange("p b n -> p (b n)"), ACT.Copy).then_inc(kv_dupd, 1)


        def swa():
            st = stages["swa"]

            def early(t):
                for u in sw_at(t, 3):
                    act.wait_ge(sw_turned, u + 1)
                    if u:
                        act.wait_ge(sw_pv, u)
                    nc.scalar.activation(sw_PT[:, :], sw_turn, ACT.Copy).then_inc(sw_PTd, 1)

            def late(t):
                for u in sw_at(t, 3):
                    act.wait_ge(sw_pv, u + 1)
                    nc.scalar.activation(flat(sw_oT[0][:, 2 * u:2 * u + 2, :]), ps[:, SW_OUT, :], ACT.Copy).then_inc(sw_ohi, 1)
                for u in sw_at(t, 1):
                    act.wait_ge(sw_neg, u + 1)
                    for a in range(4):
                        for tile in range(2):
                            S = sw_biased(u, a, tile)
                            nc.scalar.activation(S, S, ACT.Exp, bias=sw_nmax[:, u % 2, tile, a:a + 1],
                                                 accum_out=sw_sum[:, u % 2, tile, a:a + 1]).then_inc(sw_exp, 1)
                    act.wait_ge(sw_dm, u + 1)
                    nc.scalar.activation(sw_sink[:, u % 2, :, :], sw_sink[:, u % 2, :, :], ACT.Exp).then_inc(sw_snk, 1)

            for t in range(SW_TICKS):
                early(t)
                if t < SW_UNITS:
                    if t == 0:
                        split_high(*ahead_of(st, 0, 0), (0,))
                        stage_norm("swa")
                    split_high(*ahead_of(st, t // 2, t % 2), (0, 1) if t else (1,))
                elif t < SW_UNITS + 2:
                    out_slot("swa_out", t - SW_UNITS)
                late(t)
                if t >= SW_UNITS + 2:
                    out_slot("swa_out", t - SW_UNITS)

        act.wait_ge(gains_ready, 1)
        act.wait_ge(eps_ready, 1)
        for half in range(2):
            split_high(*slot0(0), (half,))
            for m in range(2 * half, 2 * half + 2):
                high_x(0, m, m)
        split_high(*slot0(1))
        act.dma_start(cst[:, own:], io["consts"][:, own:CONSTS]).then_inc(const_late, 16)
        for name in GAIN:
            if name != "norm_gain":
                n = int(np.prod(io[name].shape)) // P
                first = GAIN[name] - FIRST_ROWS
                act.dma_start(rows_late[first:first + n, :], rows(name, n)).then_inc(late_arrived, 16)
        act.dma_start(aux_in[0:2 * A_HEADS, :], rows("a_lb_logits", 2 * A_HEADS)).then_inc(late_arrived, 16)
        act.dma_start(aux_in[2 * A_HEADS:2 * A_HEADS + 1, :], io["a_out_gain"]).then_inc(late_arrived, 16)
        for n, name in enumerate(("k_gain", "b_q_gain")):
            src = bass.AP(io[name].tensor, 0, [[HD, GROUPS], [0, 2], [1, HD]])
            first = 2 * A_HEADS + 1 + GROUPS * n
            act.dma_start(aux_in[first:first + GROUPS, :].rearrange("g (a d) -> g a d", a=2), src).then_inc(late_arrived, 16)
        act.dma_start(sinks[:, :], bass.AP(io["swa_sinks_2"].tensor, 0, [[0, P], [1, HEADS]])).then_inc(late_arrived, 16)
        act.dma_start(rbx[0:BUCKETS, :], io["rel_bias"]).then_inc(bias_in, 16)
        at_onehot = CONST_AT["onehot"][0]
        act.dma_start(onehot[:, :], io["consts"][0:BUCKETS + 1, at_onehot:]).then_inc(bias_in, 16)
        for layer in layers:
            if layer.startswith("ffn"):
                ffn(int(layer[3:]))
            if layer == "hgrn":
                hgrn()
            if layer == "dil":
                dil()
            if layer == "stick":
                stick()
            if layer == "swa_kv":
                swa_kv()
            if layer == "swa":
                swa()
        norm(LAST, T // P)
        act.wait_ge(final_turned, 1)
        act.wait_ge(r_ready, LAST + 1)
        nc.scalar.activation(out_sb[:, 0, :], ps[:, OUT_TURNED[0]:OUT_TURNED[0] + 2, :].rearrange("p b n -> p (b n)"), ACT.Copy,
                             scale=r[:, LAST % 2, 0:1]).then_inc(final_copied[0], 1)

    @block.vector
    def _(dve):
        dve.sem_inc(lo_done, 4)
        dve.sem_inc(evac_done, 2)

        def split_low(n, n2, par, kind, halves=(0, 1)):
            if kind is None:
                return
            for half in halves:
                off, size, _ = HALVES[kind][half]
                dve.wait_ge(hi_done, 2 * n + half + 1)
                nc.vector.tensor_tensor(wlo[:, par, off:off + size], raw[:, 2 * par + half, :size],
                                        whi[:, par, off:off + size].bitcast(F32), ALU.subtract).then_inc(lo_done, 1)

        def update_x(e, m, source, scale):
            if e == 0:
                op = nc.vector.tensor_copy(xpair(m), source)
            else:
                op = nc.vector.scalar_tensor_tensor(xpair(m), source, scale, xpair(m), ALU.mult, ALU.add)
            op.then_inc(evac_done, 1)

        def low_x(e, m):
            uses = updates[e][1]
            for n, (which, col) in enumerate(uses):
                ready = xg_ready if which == "g" else xk_ready
                for c in range(2):
                    dve.wait_ge(xhi_done, g_before[e] + k_before[e] + 2 * (len(uses) * m + n) + c + 1)
                    hi, lo = [o[:, 2 * m + c, :] for o in operand[which]]
                    nc.vector.scalar_tensor_tensor(lo, x[:, 2 * m + c, :], gains[:, col + 2 * m + c:col + 2 * m + c + 1],
                                                   hi.bitcast(F32), ALU.mult, ALU.subtract).then_inc(ready, 1)

        def norm(e, between=None, cols=T, bank=BANK_SUM):
            dve.wait_ge(ss_ready, e + 1)
            nc.vector.tensor_scalar(ms[:, 0:cols], ps[:, bank, 0:cols], 1.0 / D, EPS, ALU.mult, ALU.add).then_inc(ms_ready, 1)
            if between:
                between()
            dve.wait_ge(r0_ready, e + 1)
            nc.vector.scalar_tensor_tensor(newton[:, 0, 0:cols], r0[:, 0:cols], -0.5, r0[:, 0:cols], ALU.mult, ALU.mult).then_inc(newton_a, 1)
            dve.wait_ge(newton_a, e + 1)
            nc.vector.tensor_tensor(newton[:, 1, 0:cols], newton[:, 0, 0:cols], ms[:, 0:cols], ALU.mult).then_inc(newton_b, 1)
            dve.wait_ge(newton_b, e + 1)
            nc.vector.scalar_tensor_tensor(r[:, e % 2, 0:cols], newton[:, 1, 0:cols], 1.5, r0[:, 0:cols], ALU.add, ALU.mult).then_inc(r_ready, 1)
            dve.wait_ge(r_ready, e + 1)

        def stage_norm(name, between=None):
            if norms[name] != norms.get(before.get(name)):
                norm(norms[name], between)
            elif between:
                between()

        def scaled(out, fill, e, factor=None):
            if factor is None:
                op = nc.vector.tensor_tensor(pair(out), pair(bank_of(fill)), r_of(e), ALU.mult)
            else:
                op = nc.vector.scalar_tensor_tensor(pair(out), pair(bank_of(fill)), factor, r_of(e), ALU.mult, ALU.mult)
            op.then_inc(evac_done, 1)

        def ffn(f):
            st, e = stages[f"up{f}"], reads[f"up{f}"]

            def body(i):
                p = FPAIRS * f + i
                first, last = [isinstance(i, int) and i == n for n in (0, FPAIRS - 1)]
                if first or last:
                    split_low(*ahead_of(st, i, 0), (0,))
                dve.wait_ge(gate_copied, p + 1)
                nc.vector.tensor_tensor(pair(gate[:, :]), wide(UP_BANKS[0], 1), pair(gate[:, :]), ALU.add).then_inc(evac_done, 1)
                if first:
                    split_low(*ahead_of(st, i, 0), (1,))
                    stage_norm(f"up{f}")
                dve.wait_ge(evac_done, st["fill"] + 2 * i + 3)
                nc.vector.tensor_tensor(pair(gate[:, :]), pair(gate[:, :]), r_of(e), ALU.mult).then_inc(gate_made, 1)
                if first:
                    split_low(*ahead_of(st, i, 1), (0,))
                elif not last:
                    split_low(*ahead_of(st, i, 0), (0,))
                dve.wait_ge(gate_exp, p + 1)
                nc.vector.tensor_scalar(gate_e[:, :], gate_e[:, :], EXP_MAX, 1.0, ALU.min, ALU.add).then_inc(gate_den, 1)
                if not first:
                    split_low(*ahead_of(st, i, 0), (1,))
                dve.wait_ge(h_copied, p + 1)
                nc.vector.tensor_tensor(pair(h[:, :]), wide(UP_BANKS[1], 1), pair(h[:, :]), ALU.add).then_inc(evac_done, 1)
                if not first:
                    split_low(*ahead_of(st, i, 1), (0,))
                dve.wait_ge(gs_done, p + 1)
                dve.wait_ge(evac_done, st["fill"] + 2 * i + 4)
                nc.vector.tensor_tensor(h[:, :], h[:, :], gate_s[:, :], ALU.mult).then_inc(h_made, 1)
                split_low(*ahead_of(st, i, 1), (1,))

            first_to_last(dve, FPAIRS, body)
            st, e = stages[f"down{f}"], update_of[f"down{f}"]
            for m in range(NPAIR):
                split_low(*ahead_of(st, m, 0))
                dve.wait_ge(slot_done, at(st, m, 1)[0] + 3)
                nc.vector.scalar_tensor_tensor(pair(xpair(m)), wide(DOWN_BANKS[m % 2], 1), 0.5, pair(xpair(m)), ALU.mult, ALU.add).then_inc(half_added, 1)
                dve.wait_ge(half_added, NPAIR * f + m + 1)
                nc.vector.scalar_tensor_tensor(pair(xpair(m)), wide(DOWN_BANKS[m % 2], 0), 0.5, pair(xpair(m)), ALU.mult, ALU.add).then_inc(evac_done, 1)
                split_low(*ahead_of(st, m, 1), (0,) if f else ())
                low_x(e, m)
                split_low(*ahead_of(st, m, 1), (1,) if f else (0, 1))

        def out_slot(name, m):
            st, e = stages[name], update_of[name]
            for pair_of in range(NPAIR) if m == NPAIR - 1 else ():
                if pair_of < NPAIR - 1:
                    dve.wait_ge(out_ready, out_before(name) + pair_of + 1)
                else:
                    dve.wait_ge(slot_done, st["base"] + m + 3)
                update_x(e, pair_of, ps[:, OUT_BANKS[name][pair_of], :], 1.0)
                if pair_of > 1:
                    low_x(e, pair_of - 2)
            if m == NPAIR - 1:
                low_x(e, m - 1)
                low_x(e, m)
            split_low(*ahead_of(st, m // 2, m % 2))

        def hgrn():
            st, e = stages["hgrn"], reads["hgrn"]

            def sigmoid_one(n, tile):
                dve.wait_ge(hg_e, n)
                nc.vector.tensor_scalar(tile, tile, EXP_MAX, 1.0, ALU.min, ALU.add).then_inc(hg_d, 1)

            def queries(t):
                for hd in hg_heads(t, 2):
                    q = hg_q[:, hd // 2 % 2, hg_cols(hd)]
                    dve.wait_ge(hg_dec, hd + 1)
                    dve.wait_ge(hg_qs, hd // 2 + 1)
                    for level in range(LEVELS):
                        op = nc.vector.tensor_tensor(hg_half(hg_E[:, hd % 2, level, :], level, 1), hg_half(hg_E[:, hd % 2, level, :], level, 1),
                                                     hg_half(q, level, 1), ALU.mult)
                    op.then_inc(hg_qd, 1)

            def split_outputs(t):
                for u in hg_split(t):
                    dve.wait_ge(hg_ohi, u + 1)
                    nc.vector.tensor_tensor(hg_oT[1][:, 2 * u:2 * u + 2, :], hg_out[:, 2 * u:2 * u + 2, :],
                                            hg_oT[0][:, 2 * u:2 * u + 2, :].bitcast(F32), ALU.subtract).then_inc(o_ready, 2)

            def late(t):
                if t != HG_GATE[-1]:
                    split_outputs(t)
                for hd in hg_heads(t, 3):
                    if hd == 0:
                        dve.wait_ge(hg_mask_in, 16)
                        dve.wait_ge(hg_zero, 1)
                    dve.wait_ge(hg_S, hd + 1)
                    for level in range(LEVELS - 1):
                        b = 1 << level
                        nc.vector.tensor_tensor(hg_half(hg_M[:, level, :], level, 1), hg_all[:, P * level:P * (level + 1)].rearrange("p (n b) -> p n b", b=b),
                                                hg_mask[:, level, :].rearrange("p (n b) -> p n b", b=b), ALU.mult).then_inc(hg_sm, 1)
                    nc.vector.tensor_tensor(hg_M[:, LEVELS - 1, :].rearrange("p (a t) -> p a t", a=2),
                                            hg_all[:, HG_OWN:HG_OWN + T].rearrange("p (a t) -> p a t", a=2),
                                            ident.unsqueeze(1).broadcast_to([P, 2, P]), ALU.mult).then_inc(hg_sm, 1)
                    if hd:
                        dve.wait_ge(hg_o, hd)
                    nc.vector.tensor_copy(hg_Pc[:, :], hg_all[:, HG_CROSS:HG_CROSS + P]).then_inc(hg_Pcr, 1)
                    dve.wait_ge(hg_sm, LEVELS * (hd + 1))
                    nc.vector.tensor_reduce(hg_P[:, :], hg_M[:, :, :].rearrange("p l t -> p t l"), AX.X, ALU.add).then_inc(hg_Pr, 1)
                if t != HG_START[0] + 2:
                    queries(t)
                for hd in hg_heads(t, 5):
                    dve.wait_ge(hg_or, hd + 1)
                    nc.vector.scalar_tensor_tensor(hg_out[:, hd, :], hg_out[:, hd, :], aux[:, HG_NORM:HG_NORM + 1], hg_rms[:, :],
                                                   ALU.mult, ALU.mult).then_inc(hg_on, 1)
                if t == HG_GATE[-1]:
                    split_outputs(t)

            nc.vector.memset(rbx[BUCKETS:BUCKETS + 1, :], NEG).then_inc(bias_masked, 1)
            dve.wait_ge(bias_in, 32)
            dve.wait_ge(bias_masked, 1)
            nc.vector.tensor_copy(rbx8[:, :].rearrange("p (n k) -> p n k", k=REPEAT), rbx[:, :].unsqueeze(2).broadcast_to([BUCKETS + 1, GROUPS * HEADS, REPEAT])).then_inc(bias_masked, 1)
            stage_norm("hgrn", lambda: split_low(*ahead_of(st, 0, 0), (0,)))
            for t in range(HG_TICKS):
                if t < HG_SLOTS:
                    u, j = hg_slot(t)
                    n = st["base"] + t
                    if t == 1:
                        dve.wait_ge(lb_exp, 1)
                        nc.vector.tensor_tensor(lbt[:, 2, :], lbt[:, 0, :], lbt[:, 1, :], ALU.add).then_inc(lb_ready, 1)
                        dve.wait_ge(lb_ready, 2)
                        nc.vector.reciprocal(lbt[:, 3, :], lbt[:, 2, :]).then_inc(lb_ready, 1)
                        dve.wait_ge(lb_ready, 3)
                        nc.vector.tensor_tensor(lbt[:, 2, :], lbt[:, 0, :], lbt[:, 3, :], ALU.mult).then_inc(lb_ready, 1)
                        nc.vector.tensor_tensor(oml[:, :], lbt[:, 1, :], lbt[:, 3, :], ALU.mult).then_inc(lb_ready, 1)
                        dve.wait_ge(lb_ready, 5)
                        nc.vector.tensor_scalar(lb[:, :], lbt[:, 2, :], GATE_MIN, None, ALU.max).then_inc(lb_ready, 1)
                        nc.vector.tensor_scalar(lbt[:, 3, :], oml[:, :], GATE_MIN, None, ALU.max).then_inc(lb_ready, 1)
                        dve.wait_ge(lb_ready, 7)
                    if j == 2:
                        dve.wait_ge(hg_s, 3 * u + 2)
                        for a in range(2):
                            hd, cols = 2 * u + a, slice(T * a, T * (a + 1))
                            nc.vector.tensor_scalar(hg_exp[1][:, cols], hg_exp[1][:, cols], oml[:, hd:hd + 1], lb[:, hd:hd + 1],
                                                    ALU.mult, ALU.add).then_inc(hg_f, 1)
                    if t % 3 == 0 and 0 < t <= HG_QFI:
                        v = t // 3 - 1
                        dve.wait_ge(hg_lf, v + 1)
                        if v:
                            dve.wait_ge(hg_dif, 2 * v)
                        for a in range(2):
                            cols = slice(T * a, T * (a + 1))
                            nc.vector.tensor_tensor_scan(hg_c[:, cols], ones[:, 0:1].broadcast_to([P, T]),
                                                         hg_exp[1][:, cols], 0.0, ALU.mult, ALU.add).then_inc(hg_cum, 1)
                        for a in range(2):
                            hd, cols = 2 * v + a, slice(T * a, T * (a + 1))
                            dve.wait_ge(hg_l, 3 * v + 3)
                            dve.wait_ge(hg_cum, hd + 1)
                            nc.vector.scalar_tensor_tensor(hg_ck[:, cols], hg_exp[2][:, cols], ln_oml[:, hd:hd + 1], hg_c[:, cols],
                                                           ALU.subtract, ALU.add).then_inc(hg_ckd, 1)
                    dve.wait_ge(slot_done, n + 3)
                    if j == 0 and u:
                        dve.wait_ge(hg_qs, u)
                    if j == 1 and u:
                        dve.wait_ge(hg_vtr, u)
                    if j == 2:
                        dve.wait_ge(hg_e, 3 * u + 3)
                    if j == 3:
                        dve.wait_ge(hg_qs if u == 0 else hg_vtr if u == 1 else hg_gs, HG_UNITS if u < 2 else u - 1)
                    scaled(hg_raw[(0, 1, 1, u % 2)[j]][:, :], st["fill"] + t, e)
                    if t == HG_START[0] + 2:
                        queries(t)
                    split_low(n + 2, (n + 2) // 2, n % 2, kinds[n + 2], (0, 1) if t else (1,))
                    if j == 0:
                        sigmoid_one(3 * u + 1, hg_exp[0][:, :])
                    if j == 1:
                        sigmoid_one(3 * u + 2, hg_exp[1][:, :])
                        sigmoid_one(3 * u + 3, hg_exp[2][:, :])
                    if j == 3:
                        sigmoid_one(HG_QFI + u + 1, hg_exp[0][:, :])
                    if t == 0:
                        dve.wait_ge(late_turned, 1)
                        nc.vector.tensor_copy(gains[:, FIRST_ROWS:GAIN_ROWS], ps[:, HG_VBANK, 0:GAIN_ROWS - FIRST_ROWS])
                        nc.vector.tensor_copy(aux[:, :], ps[:, HG_VBANK, P:P + AUX]).then_inc(aux_ready, 1)
                        dve.wait_ge(aux_ready, 1)
                        l0, l1 = aux[:, 0:A_HEADS], aux[:, A_HEADS:2 * A_HEADS]
                        nc.vector.tensor_tensor(lbt[:, 2, :], l0, l1, ALU.max).then_inc(lb_ready, 1)
                        dve.wait_ge(lb_ready, 1)
                        nc.vector.tensor_tensor(lbt[:, 0, :], l0, lbt[:, 2, :], ALU.subtract).then_inc(lb_steps, 1)
                        nc.vector.tensor_tensor(lbt[:, 1, :], l1, lbt[:, 2, :], ALU.subtract).then_inc(lb_steps, 1)
                        dve.wait_ge(bias_made, 1)
                        nc.vector.tensor_copy(bias_rows[:, :, :], ps[:, HG_SCORES:HG_SCORES + GROUPS, 0:ROW]).then_inc(bias_copied, 1)
                    late(t)
                else:
                    late(t)
                    out_slot("hgrn_out", t - HG_SLOTS)


        def dil():
            st, e, ek = stages["dil"], reads["dil"], reads["dil"] - 1

            def steps(point):
                slot = dl_projected(point)
                if slot is not None and not dl_slot(slot)[2]:
                    n, (u, j, _) = dl_qk_number(slot), dl_slot(slot)
                    g = j // 2
                    dve.wait_ge(dl_rrd, n + 1)
                    if j % 2 == 0:
                        if u:
                            dve.wait_ge(dl_scored, 4 * u)
                        for odd in range(2):
                            rows = slice(HD * odd, HD * (odd + 1))
                            op = nc.vector.scalar_tensor_tensor(dl_q[rows, g, odd, :], dl_t[rows, slot % 2, :], q_gain[rows, g:g + 1],
                                                                dl_rr[rows, :], ALU.mult, ALU.mult)
                    else:
                        if u > 1:
                            dve.wait_ge(dl_scored, 4 * (u - 1))
                        op = nc.vector.scalar_tensor_tensor(dl_k[:, u % 2, g, :], dl_t[:, slot % 2, :], aux[:, HG_NORM + 1 + g:HG_NORM + 2 + g],
                                                            dl_rr[:, :], ALU.mult, ALU.mult)
                    op.then_inc(dl_qkd, 1)
                for two in dl_due(point, DL_PV):
                    u, c = divmod(two, 2)
                    if c == 1:
                        dve.wait_ge(dl_ohi, u + 1)
                        nc.vector.tensor_tensor(flat(dl_oT[1][:, 2 * u:2 * u + 2, :]), ps[:, DL_OUT, :],
                                                flat(dl_oT[0][:, 2 * u:2 * u + 2, :]).bitcast(F32), ALU.subtract).then_inc(o_ready, 2)
                for hd in dl_due(point, DL_SCALE):
                    dve.wait_ge(dl_exp, hd + 1)
                    nc.vector.reciprocal(dl_rcp[:, hd % 2, :], dl_sum[:, hd % 2, :]).then_inc(dl_rd, 1)
                    dve.wait_ge(dl_rd, hd + 1)
                    own = dl_S[:, hd % 2, 0:GROUPS * T]
                    nc.vector.tensor_scalar(own, own, dl_rcp[:, hd % 2, 1:2], None, ALU.mult).then_inc(dl_sc1, 1)
                for hd in dl_due(point, DL_SCORES):
                    dve.wait_ge(dl_scored, hd + 1)
                    dve.wait_ge((dl_bias_in0, dl_bias_in1)[hd % 2], 16 * (hd // 2 + 1))
                    if hd > 1:
                        dve.wait_ge(dl_turned, hd - 1)
                    S = dl_S[:, hd % 2, :]
                    for tile, keys in ((1, T), (0, P)):
                        nc.vector.tensor_tensor_reduce(dl_blocks(S, keys), dl_blocks(dl_ps, keys), dl_bias[:, hd % 2, :, T - keys:T],
                                                       1.0, -3.0e38, ALU.add, ALU.max, dl_max[:, hd % 2, tile:tile + 1]).then_inc(dl_biased, 1)
                    dve.wait_ge(dl_biased, 2 * hd + 2)
                    nc.vector.tensor_scalar(dl_nmax[:, hd % 2, :], dl_max[:, hd % 2, :], -1.0, None, ALU.mult).then_inc(dl_neg, 1)

            nc.vector.tensor_scalar(q_gain[:, :], aux[:, HG_NORM + 1 + GROUPS:HG_NORM + 1 + 2 * GROUPS], HD ** -0.5, None, ALU.mult).then_inc(q_gain_ready, 1)
            dve.wait_ge(q_gain_ready, 1)
            dve.wait_ge(dl_zero, 1)
            stage_norm("dil", lambda: split_low(*ahead_of(st, 0, 0), (0,)))
            for t in range(DL_TICKS):
                steps(2 * t)
                if t < DL_SLOTS:
                    n = st["base"] + t
                    u, j, values = dl_slot(t)
                    dve.wait_ge(slot_done, n + 3)
                    if t > 1:
                        if dl_slot(t - 2)[2]:
                            dve.wait_ge(dl_vtr, dl_v_number(t - 2) + 1)
                        else:
                            dve.wait_ge(dl_sqd, dl_qk_number(t - 2) + 1)
                    scaled(dl_t[:, t % 2, :], st["fill"] + t, ek if values or j % 2 else e)
                    split_low(n + 2, (n + 2) // 2, n % 2, kinds[n + 2], (0, 1) if t else (1,))
                else:
                    out_slot("dil_out", t - DL_SLOTS)
                steps(2 * t + 1)


        def stick():
            st, e = stages["stick"], reads["stick"]

            def late(t):
                for u in sk_scores_at(t):
                    dve.wait_ge(sk_ln, u + 1)
                    if u:
                        dve.wait_ge(sk_sum, u)
                    nc.vector.scalar_tensor_tensor(sk_sp[:, :], sk_all, 0.0, sk_e[:, :], ALU.max, ALU.add).then_inc(sk_spd, 1)
                for u in sk_values_at(t):
                    dve.wait_ge(sk_ohi, u + 1)
                    nc.vector.tensor_tensor(flat(sk_oT[1][:, 2 * u:2 * u + 2, :]), ps[:, SK_OUT, :],
                                            flat(sk_oT[0][:, 2 * u:2 * u + 2, :]).bitcast(F32), ALU.subtract).then_inc(o_ready, 2)

            stage_norm("stick", lambda: split_low(*ahead_of(st, 0, 0), (0,)))
            dve.wait_ge(sk_zero, 1)
            for t in range(SK_TICKS):
                n = st["base"] + t
                if t >= SK_SLOTS:
                    out_slot("stick_out", t - SK_SLOTS)
                    late(t)
                    continue
                dve.wait_ge(slot_done, n + 3)
                if t < SK_QK:
                    u = t // 2
                    if u > 1:
                        dve.wait_ge(sk_z, u - 1)
                    if t % 2 == 0:
                        for odd in range(2):
                            rows = slice(HD * odd, HD * (odd + 1))
                            op = nc.vector.scalar_tensor_tensor(pair(sk_q[rows, u % 2, odd, :]), pair(bank_of(st["fill"] + t)[rows, :]), HD ** -0.5,
                                                                r_of(e)[rows, :, :], ALU.mult, ALU.mult)
                        op.then_inc(evac_done, 1)
                    else:
                        scaled(sk_k[:, u % 2, :], st["fill"] + t, e)
                else:
                    u = t - SK_QK
                    if u > 1:
                        dve.wait_ge(sk_vtr, u - 1)
                    scaled(sk_t[:, u % 2, :], st["fill"] + t, e)
                split_low(n + 2, (n + 2) // 2, n % 2, kinds[n + 2], (0, 1) if t else (1,))
                late(t)


        def swa_kv():
            st, e = stages["swa_kv"], reads["swa_kv"]
            stage_norm("swa_kv", lambda: split_low(*ahead_of(st, 0, 0), (0,)))
            for j, tile in enumerate((kv_t, kv_v)):
                dve.wait_ge(slot_done, st["base"] + j + 3)
                scaled(tile[:, :], st["fill"] + j, e)
                if j == 0:
                    split_low(*ahead_of(st, 0, 0), (1,))
            dve.wait_ge(kv_rope_in, 32)
            dve.wait_ge(kv_rot, 1)
            nc.vector.tensor_tensor(pair(kv_s[:, :]), pair(ps[:, KV_ROT, :]), rope_of(1), ALU.mult).then_inc(kv_sin, 1)
            dve.wait_ge(kv_cos, 1)
            dve.wait_ge(kv_sin, 1)
            nc.vector.tensor_tensor(kv_c[:, :], kv_c[:, :], kv_s[:, :], ALU.add).then_inc(kv_sum, 1)
            split_low(*ahead_of(st, 0, 1))


        def swa():
            st, e = stages["swa"], reads["swa"]

            def early(t):
                for u in sw_at(t, 1):
                    dve.wait_ge(sw_rot, u + 1)
                    if u:
                        dve.wait_ge(sw_qr, u)
                    nc.vector.tensor_tensor(pair(sw_s[:, :]), pair(ps[:, SW_OUT, :]), rope_of(1), ALU.mult).then_inc(sw_sin, 1)
                    dve.wait_ge(sw_cos, u + 1)
                    dve.wait_ge(sw_sin, u + 1)
                    if u > 1:
                        dve.wait_ge(sw_scored, u - 1)
                    for odd in range(2):
                        rows = slice(HD * odd, HD * (odd + 1))
                        op = nc.vector.tensor_tensor(sw_q[rows, u % 2, odd, :], sw_c[rows, u % 2, :], sw_s[rows, :], ALU.add)
                    op.then_inc(sw_qr, 1)

            def late(t):
                for u in sw_at(t, 3):
                    dve.wait_ge(sw_ohi, u + 1)
                    nc.vector.tensor_tensor(flat(sw_oT[1][:, 2 * u:2 * u + 2, :]), ps[:, SW_OUT, :],
                                            flat(sw_oT[0][:, 2 * u:2 * u + 2, :]).bitcast(F32), ALU.subtract).then_inc(o_ready, 2)
                for u in sw_at(t, 1):
                    dve.wait_ge(sw_scored, u + 1)
                    if u > 1:
                        dve.wait_ge(sw_turned, u - 1)
                    for a in range(4):
                        for tile in range(2):
                            keys = T if tile else P
                            nc.vector.tensor_tensor_reduce(sw_biased(u, a, tile), sw_scores(a, tile), swa_mask[:, T - keys:T], 1.0,
                                                           sinks[:, 4 * u + a:4 * u + a + 1], ALU.add, ALU.max,
                                                           sw_max[:, u % 2, tile, a:a + 1]).then_inc(sw_masked, 1)
                    dve.wait_ge(sw_masked, 8 * u + 8)
                    nc.vector.tensor_scalar(sw_nmax[:, u % 2, :, :], sw_max[:, u % 2, :, :], -1.0, None, ALU.mult).then_inc(sw_neg, 1)
                    dve.wait_ge(sw_neg, u + 1)
                    nc.vector.tensor_tensor(sw_sink[:, u % 2, :, :], sw_nmax[:, u % 2, :, :],
                                            sinks[:, 4 * u:4 * u + 4].unsqueeze(1).broadcast_to([P, 2, 4]), ALU.add).then_inc(sw_dm, 1)

            def last(t):
                for u in sw_at(t, 2):
                    dve.wait_ge(sw_snk, u + 1)
                    dve.wait_ge(sw_exp, 8 * u + 8)
                    nc.vector.tensor_tensor(sw_den[:, u % 2, :, :], sw_sum[:, u % 2, :, :], sw_sink[:, u % 2, :, :], ALU.add).then_inc(sw_dn, 1)
                    dve.wait_ge(sw_dn, u + 1)
                    nc.vector.reciprocal(sw_rcp[:, u % 2, :, :], sw_den[:, u % 2, :, :]).then_inc(sw_rd, 1)
                    dve.wait_ge(sw_rd, u + 1)
                    own = sw_S[:, u % 2, 0:4 * T].rearrange("p (a k) -> p a k", a=4)
                    nc.vector.tensor_tensor(own, own, sw_rcp[:, u % 2, 1, :].unsqueeze(2).broadcast_to([P, 4, T]), ALU.mult).then_inc(sw_sc1, 1)

            stage_norm("swa", lambda: split_low(*ahead_of(st, 0, 0), (0,)))
            dve.wait_ge(sw_zero, 1)
            for t in range(SW_TICKS):
                early(t)
                last(t)
                if t < SW_UNITS:
                    dve.wait_ge(slot_done, st["base"] + t + 3)
                    if t > 1:
                        dve.wait_ge(sw_rot, t - 1)
                        dve.wait_ge(sw_cos, t - 1)
                    scaled(sw_t[:, t % 2, :], st["fill"] + t, e, HD ** -0.5)
                    split_low(*ahead_of(st, t // 2, t % 2), (0, 1) if t else (1,))
                elif t < SW_UNITS + 2:
                    out_slot("swa_out", t - SW_UNITS)
                late(t)
                if t >= SW_UNITS + 2:
                    out_slot("swa_out", t - SW_UNITS)

        nc.vector.memset(eps[:, :], EPS).then_inc(eps_ready, 1)
        dve.wait_ge(rows_turned, 1)
        nc.vector.tensor_copy(gains[:, 0:FIRST_ROWS], ps[:, BANK_SUM, 0:FIRST_ROWS]).then_inc(gains_ready, 1)
        def turned_x(m):
            dve.wait_ge(x_turned, m + 1)
            update_x(0, m, ps[:, X_BANKS[m], :], 1.0)

        turned_x(0)
        turned_x(1)
        for half in range(2):
            low_x(0, 2 * half)
            if half == 0:
                turned_x(2)
            split_low(*slot0(0), (half,))
            low_x(0, 2 * half + 1)
            if half == 0:
                turned_x(3)
        split_low(*slot0(1))
        for layer in layers:
            if layer.startswith("ffn"):
                ffn(int(layer[3:]))
            if layer == "hgrn":
                hgrn()
            if layer == "dil":
                dil()
            if layer == "stick":
                stick()
            if layer == "swa_kv":
                swa_kv()
            if layer == "swa":
                swa()
        norm(LAST, cols=T // P, bank=BANK_LAST)
        dve.wait_ge(final_turned, 1)
        for half in range(2):
            nc.vector.tensor_scalar(out_sb[:, 1, D // 2 * half:D // 2 * (half + 1)], ps[:, OUT_TURNED[2 + half], :], r[:, LAST % 2, 1:2], None,
                                    ALU.mult).then_inc(final_copied[1], 1)

    @block.gpsimd
    def _(pool):
        pool.sem_inc(gr_done, 1)
        pool.sem_inc(hT_ready, 1)

        def squares(e, m, fill):
            pool.wait_ge(evac_done, fill + 3)
            if m == 0:
                if e:
                    pool.wait_ge(ss_ready, e)
                nc.gpsimd.tensor_tensor(acc[:, :], xpair(m), xpair(m), ALU.mult).then_inc(acc_done, 1)
            elif m == NPAIR - 1:
                pool.wait_ge(acc_done, NPAIR * e + m)
                pool.wait_ge(sq_last_done, e + 1)
                nc.gpsimd.tensor_tensor(acc[:, :], acc[:, :], sq_last[:, :], ALU.add).then_inc(acc_done, 1)
            else:
                pool.wait_ge(acc_done, NPAIR * e + m)
                nc.gpsimd.tensor_tensor(sq[:, :], xpair(m), xpair(m), ALU.mult).then_inc(sq_done, 1)
                pool.wait_ge(sq_done, (NPAIR - 2) * e + m)
                nc.gpsimd.tensor_tensor(acc[:, :], acc[:, :], sq[:, :], ALU.add).then_inc(acc_done, 1)

        def ffn(f):
            st, e = stages[f"up{f}"], reads[f"up{f}"]
            pool.wait_ge(r_ready, e + 1)
            with pool.Fori(0, FPAIRS) as i:
                p = FPAIRS * f + i
                pool.wait_ge(gate_made, p + 1)
                nc.gpsimd.tensor_tensor(pair(gate_r[:, :]), pair(gate[:, :]), r_of(e), ALU.mult).then_inc(gr_done, 1)
                pool.wait_ge(gr_done, p + 2)
                pool.wait_ge(sig_ready, p + 1)
                nc.gpsimd.tensor_tensor(gate_s[:, :], gate_r[:, :], gate_s[:, :], ALU.mult).then_inc(gs_done, 1)
                pool.wait_ge(hhi_done, p + 1)
                nc.gpsimd.tensor_tensor(hidden(i, 1), pair(h[:, :]), hidden(i, 0).bitcast(F32), ALU.subtract).then_inc(hT_ready, 1)
            for m in range(NPAIR):
                squares(update_of[f"down{f}"], m, stages[f"down{f}"]["fill"] + m)

        def out_stage(name):
            for m in range(NPAIR):
                squares(update_of[name], m, stages[name]["fill"] + m)

        def hgrn():
            nc.gpsimd.memset(hg_M[:, :, :], 0.0).then_inc(hg_zero, 1)
            for t in range(HG_TICKS):
                for u in range(HG_UNITS):
                    if t == HG_QFI + u + 1:
                        pool.wait_ge(hg_s, HG_QFI + u + 1)
                        if u:
                            pool.wait_ge(hg_og, u)
                        nc.gpsimd.tensor_tensor(hg_g[:, :], hg_raw[u % 2][:, :], hg_exp[0][:, :], ALU.mult).then_inc(hg_gs, 1)
                if t % 3 == 2 and t < HG_QFI:
                    u = t // 3
                    pool.wait_ge(hg_s, 3 * u + 1)
                    if u > 1:
                        pool.wait_ge(hg_S, 2 * u - 2)
                    nc.gpsimd.tensor_tensor(hg_q[:, u % 2, :], hg_raw[0][:, :], hg_exp[0][:, :], ALU.mult).then_inc(hg_qs, 1)
                for hd in hg_heads(t, 4):
                    pool.wait_ge(hg_oc, hd + 1)
                    if hd:
                        pool.wait_ge(hg_oss, hd)
                    nc.gpsimd.tensor_tensor(hg_osq[:, :], hg_out[:, hd, :], hg_out[:, hd, :], ALU.mult).then_inc(hg_os2, 1)
                for hd in hg_heads(t, 0):
                    c, ck = hg_c[:, hg_cols(hd)], hg_ck[:, hg_cols(hd)]
                    pool.wait_ge(hg_ckd, hd + 1)
                    if hd > 1:
                        pool.wait_ge(hg_S, hd - 1)
                    for level in range(LEVELS):
                        b = 1 << level
                        first, second = hg_half(c, level, 0), hg_half(c, level, 1)
                        middle = first[:, :, b - 1:b].broadcast_to([P, T // (2 * b), b])
                        nc.gpsimd.tensor_tensor(hg_half(hg_E[:, hd % 2, level, :], level, 0), middle, hg_half(ck, level, 0), ALU.subtract)
                        op = nc.gpsimd.tensor_tensor(hg_half(hg_E[:, hd % 2, level, :], level, 1), second, middle, ALU.subtract)
                    op.then_inc(hg_dif, 1)
                for u in hg_units(t, 0):
                    pool.wait_ge(hg_on, 2 * u + 2)
                    pool.wait_ge(hg_gs, u + 1)
                    out = flat(hg_out[:, 2 * u:2 * u + 2, :])
                    nc.gpsimd.tensor_tensor(out, out, hg_g[:, :], ALU.mult).then_inc(hg_og, 1)
            out_stage("hgrn_out")


        def dil():
            st = stages["dil"]
            nc.gpsimd.memset(dl_q[:, :, :, :], 0.0).then_inc(dl_zero, 1)
            for point in range(2 * DL_TICKS):
                t, half = divmod(point, 2)
                for hd in dl_due(point, DL_SCALE):
                    pool.wait_ge(dl_rd, hd + 1)
                    own = dl_S[:, hd % 2, GROUPS * T:]
                    nc.gpsimd.tensor_tensor(own, own, dl_rcp[:, hd % 2, 0:1].broadcast_to([P, GROUPS * P]), ALU.mult).then_inc(dl_sc0, 1)
                if half and t < DL_SLOTS and not dl_slot(t)[2]:
                    n = dl_qk_number(t)
                    pool.wait_ge(evac_done, st["fill"] + t + 3)
                    if n:
                        pool.wait_ge(dl_ss, n)
                    nc.gpsimd.tensor_tensor(dl_sq[:, :], dl_t[:, t % 2, :], dl_t[:, t % 2, :], ALU.mult).then_inc(dl_sqd, 1)
            out_stage("dil_out")


        def stick():
            nc.gpsimd.memset(sk_q[:, :, :, :], 0.0).then_inc(sk_zero, 1)
            out_stage("stick_out")


        def swa_kv():
            st = stages["swa_kv"]
            pool.wait_ge(evac_done, st["fill"] + 3)
            pool.wait_ge(kv_rope_in, 32)
            nc.gpsimd.tensor_tensor(pair(kv_c[:, :]), pair(kv_t[:, :]), rope_of(0), ALU.mult).then_inc(kv_cos, 1)


        def swa():
            st = stages["swa"]
            nc.gpsimd.memset(sw_q[:, :, :, :], 0.0).then_inc(sw_zero, 1)
            for u in range(SW_UNITS + 1):
                if u < SW_UNITS:
                    pool.wait_ge(evac_done, st["fill"] + u + 3)
                    if u > 1:
                        pool.wait_ge(sw_qr, u - 1)
                    nc.gpsimd.tensor_tensor(pair(sw_c[:, u % 2, :]), pair(sw_t[:, u % 2, :]), rope_of(0), ALU.mult).then_inc(sw_cos, 1)
                if u:
                    pool.wait_ge(sw_rd, u)
                    own = sw_S[:, (u - 1) % 2, 4 * T:6 * T].rearrange("p (a k) -> p a k", a=4)
                    nc.gpsimd.tensor_tensor(own, own, sw_rcp[:, (u - 1) % 2, 0, :].unsqueeze(2).broadcast_to([P, 4, P]), ALU.mult).then_inc(sw_sc0, 1)
            out_stage("swa_out")

        for m in range(NPAIR):
            squares(0, m, m)
        for layer in layers:
            if layer.startswith("ffn"):
                ffn(int(layer[3:]))
            if layer == "hgrn":
                hgrn()
            if layer == "dil":
                dil()
            if layer == "stick":
                stick()
            if layer == "swa_kv":
                swa_kv()
            if layer == "swa":
                swa()
    ctx.close()


INPUTS = [
    "x", "norm_gain", "ffn_w_in", "ffn_w_out", "a_w_in", "a_lb_logits", "a_out_gain", "a_w_out", "kv_norm", "w_kv",
    "k_gain", "b_w_q", "b_q_gain", "b_w_o", "rel_bias", "ffn1_norm_2", "ffn1_w_in_2", "ffn1_w_out_2",
    "mix_norm_2", "ffn2_norm_2", "ffn2_w_in_2", "ffn2_w_out_2", "sb_w_qkv_2", "sb_w_o_2", "kv_norm_2", "kv_w_2",
    "swa_w_q_2", "swa_sinks_2", "swa_w_o_2", "final_norm_2",
]


def kernel(**inputs):
    import concourse.bacc as bacc
    from concourse.bass_utils import run_bass_kernel_spmd

    nc = bacc.Bacc("TRN2", target_bir_lowering=False, num_devices=1)
    arrays = {name: np.ascontiguousarray(inputs[name]) for name in INPUTS}
    arrays["consts"] = constants()
    io = {name: nc.dram_tensor(f"in_{name}", a.shape, F32, kind="ExternalInput").ap() for name, a in arrays.items()}
    io["out"] = nc.dram_tensor("out", (1, T, D), F32, kind="ExternalOutput").ap()
    build_program(nc, io)
    result = run_bass_kernel_spmd(nc, [{f"in_{name}": a for name, a in arrays.items()}], core_ids=[0])
    return result.results[0]["out"]
```
